# Optimizing a Trainium2 kernel written in Bass

```python
import jax
import jax.numpy as jnp
from jax import lax
import numpy as np

D_MODEL = 1024
BATCH = 1
SEQ = 1024
DEPTH = 1

GRID_W = 64
CTX_LEN = 256
EPS = 1e-6
NEG_INF = -1e30
ROPE_THETA = 10000.0

N_BRANCH = 3
BRANCH_WIDTH = 512

GDN_HEADS = 4
GDN_DK = 128
GDN_DV = 128
GDN_CHUNK = 64
GDN_CONV = 4

SWA_Q_HEADS = 8
SWA_KV_HEADS = 2
SWA_GROUP = SWA_Q_HEADS // SWA_KV_HEADS
SWA_HEAD_DIM = 64
SWA_WINDOW = 128
SWA_BLOCK = 128

LRU_WIDTH = 512
LRU_BLOCKS = 8
LRU_CONV = 4
LRU_C = 8.0

N_EXPERTS = 16
EXPERT_HIDDEN = 2048
EC_CAPACITY = 2

IN_SIZES = (GDN_HEADS * GDN_DK, GDN_HEADS * GDN_DK, GDN_HEADS * GDN_DV, GDN_HEADS * GDN_DV,
            2 * GDN_HEADS, 2 * GDN_HEADS,
            SWA_Q_HEADS * SWA_HEAD_DIM, SWA_KV_HEADS * SWA_HEAD_DIM, SWA_KV_HEADS * SWA_HEAD_DIM,
            LRU_WIDTH, LRU_WIDTH,
            N_BRANCH * D_MODEL)
IN_SPLITS = tuple(sum(IN_SIZES[:i + 1]) for i in range(len(IN_SIZES) - 1))
D_IN = sum(IN_SIZES)

kernel_name = 'hybrid_gdn_swa_rglru_ecmoe_prefix_dit'

F32 = jnp.float32

def rmsnorm(t, g):
    tf = t.astype(F32)
    tf = tf * lax.rsqrt(jnp.mean(tf * tf, axis=-1, keepdims=True) + EPS)
    return (tf * g.astype(F32)).astype(t.dtype)

def l2norm(t):
    tf = t.astype(F32)
    return tf * lax.rsqrt(jnp.sum(tf * tf, axis=-1, keepdims=True) + EPS)

def split_heads(t, n):
    return t.reshape(t.shape[:-1] + (n, t.shape[-1] // n))

def maybe_flip(t, rev):
    return jnp.flip(t, axis=1) if rev else t

def centred_depthwise_conv(t, w):
    k = w.shape[0]
    return lax.conv_general_dilated(
        t, w[:, None, :].astype(t.dtype), window_strides=(1,),
        padding=[(k // 2, k - 1 - k // 2)], dimension_numbers=('NWC', 'WIO', 'NWC'),
        feature_group_count=t.shape[-1])

def adaln(cond, w, b):
    return jnp.split(jax.nn.silu(cond) @ w + b, 6, axis=-1)

def modulate(t, shift, scale):
    return t * (1 + scale) + shift

def unit_lower_inverse(a):
    c = a.shape[-1]
    eye = jnp.eye(c, dtype=a.dtype)
    inv = eye - a
    p = a
    for _ in range(int(np.log2(c)) - 1):
        p = p @ p
        inv = inv @ (eye + p)
    return inv

def gdn_chunked(q, k, v, g, beta, s0):
    b, l, h, _ = q.shape
    c = GDN_CHUNK
    n = l // c

    def blocks(t):
        return jnp.moveaxis(t.reshape((b, n, c, h) + t.shape[3:]), (1, 2), (0, 3))

    qb, kb, vb, betab = blocks(q), blocks(k), blocks(v), blocks(beta)
    gb = jnp.cumsum(blocks(g), axis=-1)
    incl = jnp.tril(jnp.ones((c, c), bool))
    strict = jnp.tril(jnp.ones((c, c), bool), -1)
    diff = gb[..., :, None] - gb[..., None, :]
    decay = jnp.where(incl, jnp.exp(jnp.where(incl, diff, 0.0)), 0.0)
    k_beta = kb * betab[..., None]
    a_mat = jnp.where(strict, jnp.einsum('nbhid,nbhjd->nbhij', k_beta, kb) * decay, 0.0)
    t_mat = unit_lower_inverse(a_mat)
    u = t_mat @ (vb * betab[..., None])
    w = t_mat @ (k_beta * jnp.exp(gb)[..., None])
    qk = jnp.einsum('nbhid,nbhjd->nbhij', qb, kb) * decay

    def step(s, inp):
        q_c, k_c, u_c, w_c, qk_c, g_c = inp
        v_new = u_c - w_c @ s
        o = (q_c * jnp.exp(g_c)[..., None]) @ s + qk_c @ v_new
        g_last = g_c[..., -1:]
        s = s * jnp.exp(g_last)[..., None] + jnp.einsum(
            'bhcd,bhce->bhde', k_c * jnp.exp(g_last - g_c)[..., None], v_new)
        return s, o

    s_fin, o = lax.scan(step, s0, (qb, kb, u, w, qk, gb))
    o = jnp.moveaxis(o, (0, 3), (1, 2)).reshape(b, l, h, v.shape[-1])
    return o, s_fin

def gdn_prepare(q, k, v, conv_w):
    qkv = jax.nn.silu(centred_depthwise_conv(jnp.concatenate([q, k, v], axis=-1), conv_w))
    q, k, v = jnp.split(qkv, [GDN_HEADS * GDN_DK, 2 * GDN_HEADS * GDN_DK], axis=-1)
    q = l2norm(split_heads(q, GDN_HEADS)) * (GDN_DK ** -0.5)
    k = l2norm(split_heads(k, GDN_HEADS))
    v = split_heads(v, GDN_HEADS).astype(F32)
    return q, k, v

def gdn_gates(a, b, a_log, dt_bias, d):
    sl = slice(d * GDN_HEADS, (d + 1) * GDN_HEADS)
    g = -jnp.exp(a_log[d].astype(F32)) * jax.nn.softplus(a[..., sl].astype(F32) + dt_bias[d].astype(F32))
    beta = jax.nn.sigmoid(b[..., sl].astype(F32))
    return g, beta

def gdn_mixer(parts_x, parts_c, conv_w, a_log, dt_bias, onorm_g, need_ctx):
    qx, kx, vx, zx, ax, bx = parts_x
    qc, kc, vc, zc, ac, bc = parts_c
    seq_x = gdn_prepare(qx, kx, vx, conv_w)
    seq_c = gdn_prepare(qc, kc, vc, conv_w)
    batch = qx.shape[0]
    o_x = jnp.zeros(seq_x[2].shape, F32)
    o_c = jnp.zeros(seq_c[2].shape, F32)
    for d in range(2):
        rev = d == 1
        gx, betax = gdn_gates(ax, bx, a_log, dt_bias, d)
        gc, betac = gdn_gates(ac, bc, a_log, dt_bias, d)
        s0 = jnp.zeros((batch, GDN_HEADS, GDN_DK, GDN_DV), F32)
        oc_d, s_ctx = gdn_chunked(*(maybe_flip(t, rev) for t in (*seq_c, gc, betac)), s0)
        ox_d, _ = gdn_chunked(*(maybe_flip(t, rev) for t in (*seq_x, gx, betax)), s_ctx)
        o_x = o_x + maybe_flip(ox_d, rev)
        o_c = o_c + maybe_flip(oc_d, rev)

    def finish(o, z):
        y = rmsnorm(o, onorm_g) * jax.nn.silu(split_heads(z, GDN_HEADS).astype(F32))
        return y.reshape(z.shape).astype(z.dtype)

    return finish(o_x, zx), (finish(o_c, zc) if need_ctx else None)

def axial_rope(length, dh):
    rows = length // GRID_W
    row = jnp.repeat(jnp.arange(rows, dtype=F32), GRID_W)
    col = jnp.tile(jnp.arange(GRID_W, dtype=F32), rows)
    axis_dim = dh // 2
    inv_freq = ROPE_THETA ** (-jnp.arange(0, axis_dim, 2, dtype=F32) / axis_dim)
    ang = jnp.concatenate([row[:, None] * inv_freq, col[:, None] * inv_freq], axis=-1)
    return jnp.cos(ang), jnp.sin(ang)

def apply_rope(t, cos, sin):
    tf = t.astype(F32)
    t1, t2 = tf[..., 0::2], tf[..., 1::2]
    cs, sn = cos[None, :, None, :], sin[None, :, None, :]
    out = jnp.stack([t1 * cs - t2 * sn, t1 * sn + t2 * cs], axis=-1).reshape(t.shape)
    return out.astype(t.dtype)

def band_mask(nb, length):
    a = jnp.arange(SWA_BLOCK)[:, None]
    s = jnp.arange(3 * SWA_BLOCK)[None, :]
    kpos = jnp.arange(nb)[:, None, None] * SWA_BLOCK - SWA_BLOCK + s
    in_window = jnp.abs(s - SWA_BLOCK - a) <= SWA_WINDOW
    return in_window[None] & (kpos >= 0) & (kpos < length)

def swa_mixer(qx, kx, vx, qc, kc, vc, qn_g, kn_g, sink, need_ctx):
    b, l, _ = qx.shape
    lc = qc.shape[1]
    scale = SWA_HEAD_DIM ** -0.5
    cos, sin = axial_rope(l, SWA_HEAD_DIM)
    qx = apply_rope(rmsnorm(split_heads(qx, SWA_Q_HEADS), qn_g), cos, sin)
    kx = apply_rope(rmsnorm(split_heads(kx, SWA_KV_HEADS), kn_g), cos, sin)
    vx = split_heads(vx, SWA_KV_HEADS)
    qc = rmsnorm(split_heads(qc, SWA_Q_HEADS), qn_g)
    kc = rmsnorm(split_heads(kc, SWA_KV_HEADS), kn_g)
    vc = split_heads(vc, SWA_KV_HEADS)
    sink_l = sink.astype(F32).reshape(SWA_KV_HEADS, SWA_GROUP)

    nb = l // SWA_BLOCK
    qb = qx.reshape(b, nb, SWA_BLOCK, SWA_KV_HEADS, SWA_GROUP, SWA_HEAD_DIM)

    def windows(t):
        tp = jnp.pad(t, ((0, 0), (SWA_BLOCK, SWA_BLOCK), (0, 0), (0, 0)))
        tp = tp.reshape(b, nb + 2, SWA_BLOCK, SWA_KV_HEADS, SWA_HEAD_DIM)
        return jnp.concatenate([tp[:, :-2], tp[:, 1:-1], tp[:, 2:]], axis=2)

    kw, vw = windows(kx), windows(vx)
    s_loc = jnp.einsum('bnqkgd,bnskd->bnkgqs', qb, kw).astype(F32) * scale
    s_loc = jnp.where(band_mask(nb, l)[None, :, None, None], s_loc, NEG_INF)
    s_ctx = jnp.einsum('bnqkgd,bskd->bnkgqs', qb, kc).astype(F32) * scale
    sink_col = jnp.broadcast_to(sink_l[None, None, :, :, None, None], s_loc.shape[:-1] + (1,))
    p = jax.nn.softmax(jnp.concatenate([s_loc, s_ctx, sink_col], axis=-1), axis=-1).astype(vx.dtype)
    w3 = 3 * SWA_BLOCK
    o = (jnp.einsum('bnkgqs,bnskd->bnqkgd', p[..., :w3], vw)
         + jnp.einsum('bnkgqs,bskd->bnqkgd', p[..., w3:w3 + lc], vc))
    out_x = o.reshape(b, l, SWA_Q_HEADS * SWA_HEAD_DIM)
    if not need_ctx:
        return out_x, None

    qcg = qc.reshape(b, lc, SWA_KV_HEADS, SWA_GROUP, SWA_HEAD_DIM)
    s = jnp.einsum('bqkgd,bskd->bkgqs', qcg, kc).astype(F32) * scale
    sink_c = jnp.broadcast_to(sink_l[None, :, :, None, None], s.shape[:-1] + (1,))
    pc = jax.nn.softmax(jnp.concatenate([s, sink_c], axis=-1), axis=-1)[..., :lc].astype(vc.dtype)
    out_c = jnp.einsum('bkgqs,bskd->bqkgd', pc, vc).reshape(b, lc, SWA_Q_HEADS * SWA_HEAD_DIM)
    return out_x, out_c

def linear_scan(a, bterm, h0):
    bterm = bterm.at[:, 0].add(a[:, 0] * h0)

    def combine(lft, rgt):
        return lft[0] * rgt[0], rgt[0] * lft[1] + rgt[1]

    _, h = lax.associative_scan(combine, (a, bterm), axis=1)
    return h

def lru_coeffs(u, gate_w, gate_b, lam):
    b, l, _ = u.shape
    ub = u.reshape(b, l, LRU_BLOCKS, LRU_WIDTH // LRU_BLOCKS)
    pre = jnp.einsum('blki,gkij->gblkj', ub, gate_w.astype(F32)).reshape(2, b, l, LRU_WIDTH)
    pre = pre + gate_b.astype(F32)[:, None, None, :]
    r, i = jax.nn.sigmoid(pre[0]), jax.nn.sigmoid(pre[1])
    log_a = -LRU_C * r * jax.nn.softplus(-lam.astype(F32))
    return jnp.exp(log_a), jnp.sqrt(-jnp.expm1(2.0 * log_a)) * (i * u)

def lru_mixer(xr_x, y_x, xr_c, y_c, conv_w, conv_b, gate_w, gate_b, lam, need_ctx):
    ux = (centred_depthwise_conv(xr_x, conv_w) + conv_b).astype(F32)
    uc = (centred_depthwise_conv(xr_c, conv_w) + conv_b).astype(F32)
    batch = ux.shape[0]
    h_x = jnp.zeros(ux.shape, F32)
    h_c = jnp.zeros(uc.shape, F32)
    for d in range(2):
        rev = d == 1
        ac, bc = lru_coeffs(maybe_flip(uc, rev), gate_w[d], gate_b[d], lam[d])
        ax, bx = lru_coeffs(maybe_flip(ux, rev), gate_w[d], gate_b[d], lam[d])
        hc_d = linear_scan(ac, bc, jnp.zeros((batch, LRU_WIDTH), F32))
        hx_d = linear_scan(ax, bx, hc_d[:, -1])
        h_x = h_x + maybe_flip(hx_d, rev)
        h_c = h_c + maybe_flip(hc_d, rev)
    out_x = (h_x * jax.nn.gelu(y_x.astype(F32))).astype(y_x.dtype)
    out_c = (h_c * jax.nn.gelu(y_c.astype(F32))).astype(y_c.dtype) if need_ctx else None
    return out_x, out_c

def merge(branches, gate_logits, w_branch, w_out):
    gates = jnp.split(jax.nn.sigmoid(gate_logits.astype(F32)).astype(gate_logits.dtype), N_BRANCH, axis=-1)
    mixed = gates[0] * (branches[0] @ w_branch[0])
    for i in range(1, N_BRANCH):
        mixed = mixed + gates[i] * (branches[i] @ w_branch[i])
    return mixed @ w_out

def mixer_sublayer(hx, hc, w_in, gdn_conv_w, gdn_a_log, gdn_dt_bias, gdn_onorm_g,
                   swa_qnorm_g, swa_knorm_g, swa_sink, lru_conv_w, lru_conv_b,
                   lru_gate_w, lru_gate_b, lru_lambda, w_branch, w_out, need_ctx):
    px = jnp.split(hx @ w_in, IN_SPLITS, axis=-1)
    pc = jnp.split(hc @ w_in, IN_SPLITS, axis=-1)
    a_x, a_c = gdn_mixer(px[0:6], pc[0:6], gdn_conv_w, gdn_a_log, gdn_dt_bias, gdn_onorm_g, need_ctx)
    b_x, b_c = swa_mixer(*px[6:9], *pc[6:9], swa_qnorm_g, swa_knorm_g, swa_sink, need_ctx)
    c_x, c_c = lru_mixer(px[9], px[10], pc[9], pc[10], lru_conv_w, lru_conv_b,
                         lru_gate_w, lru_gate_b, lru_lambda, need_ctx)
    out_x = merge((a_x, b_x, c_x), px[11], w_branch, w_out)
    out_c = merge((a_c, b_c, c_c), pc[11], w_branch, w_out) if need_ctx else None
    return out_x, out_c

def expert_choice_ffn(h, w_router, w_gate, w_up, w_down):
    b, t, _ = h.shape
    cap = EC_CAPACITY * t // N_EXPERTS
    aff = jax.nn.softmax((h @ w_router).astype(F32), axis=-1)
    gates, idx = lax.top_k(jnp.swapaxes(aff, 1, 2), cap)
    bidx = jnp.arange(b)[:, None, None]
    xs = h[bidx, idx]
    hid = jax.nn.silu(jnp.einsum('becd,edf->becf', xs, w_gate)) * jnp.einsum('becd,edf->becf', xs, w_up)
    ys = jnp.einsum('becf,efd->becd', hid, w_down) * gates[..., None].astype(h.dtype)
    return jnp.zeros_like(h).at[bidx, idx].add(ys.astype(h.dtype))

def setup_inputs(seed: int = 0) -> dict:
    key = jax.random.key(seed)
    ks = jax.random.split(key, 32)

    def nrm(i, shape, scale):
        return jax.random.normal(ks[i], shape, F32) * scale

    dt = jnp.exp(jax.random.uniform(ks[9], (DEPTH, 2, GDN_HEADS), F32, np.log(1e-3), np.log(1e-1)))
    u = jax.random.uniform(ks[18], (DEPTH, 2, LRU_WIDTH), F32, 0.9, 0.999)
    a0 = u ** (1.0 / LRU_C)
    bw = LRU_WIDTH // LRU_BLOCKS
    return {
        'x': nrm(0, (BATCH, SEQ, D_MODEL), 1.0),
        'c': nrm(1, (BATCH, D_MODEL), 1.0),
        'ctx': nrm(2, (BATCH, CTX_LEN, D_MODEL), 1.0),
        'c_ctx': nrm(3, (D_MODEL,), 1.0),
        'w_ada': nrm(4, (DEPTH, D_MODEL, 6 * D_MODEL), 0.5 * D_MODEL ** -0.5),
        'b_ada': nrm(5, (DEPTH, 6 * D_MODEL), 0.01),
        'norm1_g': 1.0 + nrm(6, (DEPTH, D_MODEL), 0.01),
        'norm2_g': 1.0 + nrm(7, (DEPTH, D_MODEL), 0.01),
        'w_in': nrm(8, (DEPTH, D_MODEL, D_IN), D_MODEL ** -0.5),
        'gdn_conv_w': nrm(10, (DEPTH, GDN_CONV, 2 * GDN_HEADS * GDN_DK + GDN_HEADS * GDN_DV), GDN_CONV ** -0.5),
        'gdn_a_log': jnp.log(jax.random.uniform(ks[11], (DEPTH, 2, GDN_HEADS), F32, 1.0, 16.0)),
        'gdn_dt_bias': dt + jnp.log(-jnp.expm1(-dt)),
        'gdn_onorm_g': 1.0 + nrm(12, (DEPTH, GDN_DV), 0.01),
        'swa_qnorm_g': 1.0 + nrm(13, (DEPTH, SWA_HEAD_DIM), 0.01),
        'swa_knorm_g': 1.0 + nrm(14, (DEPTH, SWA_HEAD_DIM), 0.01),
        'swa_sink': nrm(15, (DEPTH, SWA_Q_HEADS), 0.5),
        'lru_conv_w': nrm(16, (DEPTH, LRU_CONV, LRU_WIDTH), LRU_CONV ** -0.5),
        'lru_conv_b': nrm(17, (DEPTH, LRU_WIDTH), 0.01),
        'lru_gate_w': nrm(19, (DEPTH, 2, 2, LRU_BLOCKS, bw, bw), bw ** -0.5),
        'lru_gate_b': nrm(20, (DEPTH, 2, 2, LRU_WIDTH), 0.01),
        'lru_lambda': jnp.log(a0) - jnp.log1p(-a0),
        'w_branch': nrm(21, (DEPTH, N_BRANCH, BRANCH_WIDTH, D_MODEL), BRANCH_WIDTH ** -0.5),
        'w_out': nrm(22, (DEPTH, D_MODEL, D_MODEL), D_MODEL ** -0.5),
        'w_router': nrm(23, (DEPTH, D_MODEL, N_EXPERTS), D_MODEL ** -0.5),
        'w_exp_gate': nrm(24, (DEPTH, N_EXPERTS, D_MODEL, EXPERT_HIDDEN), D_MODEL ** -0.5),
        'w_exp_up': nrm(25, (DEPTH, N_EXPERTS, D_MODEL, EXPERT_HIDDEN), D_MODEL ** -0.5),
        'w_exp_down': nrm(26, (DEPTH, N_EXPERTS, EXPERT_HIDDEN, D_MODEL), EXPERT_HIDDEN ** -0.5),
    }

def reference(x, c, ctx, c_ctx, w_ada, b_ada, norm1_g, norm2_g, w_in, gdn_conv_w, gdn_a_log,
              gdn_dt_bias, gdn_onorm_g, swa_qnorm_g, swa_knorm_g, swa_sink, lru_conv_w,
              lru_conv_b, lru_gate_w, lru_gate_b, lru_lambda, w_branch, w_out, w_router,
              w_exp_gate, w_exp_up, w_exp_down):
    cond_x = c[:, None, :]
    cond_c = c_ctx[None, None, :]
    cx = ctx
    for layer in range(DEPTH):
        need_ctx = layer < DEPTH - 1
        mx = adaln(cond_x, w_ada[layer], b_ada[layer])
        mc = adaln(cond_c, w_ada[layer], b_ada[layer])
        hx = modulate(rmsnorm(x, norm1_g[layer]), mx[0], mx[1])
        hc = modulate(rmsnorm(cx, norm1_g[layer]), mc[0], mc[1])
        ox, oc = mixer_sublayer(hx, hc, w_in[layer], gdn_conv_w[layer], gdn_a_log[layer],
                                gdn_dt_bias[layer], gdn_onorm_g[layer], swa_qnorm_g[layer],
                                swa_knorm_g[layer], swa_sink[layer], lru_conv_w[layer],
                                lru_conv_b[layer], lru_gate_w[layer], lru_gate_b[layer],
                                lru_lambda[layer], w_branch[layer], w_out[layer], need_ctx)
        x = x + mx[2] * ox
        hx = modulate(rmsnorm(x, norm2_g[layer]), mx[3], mx[4])
        x = x + mx[5] * expert_choice_ffn(hx, w_router[layer], w_exp_gate[layer],
                                          w_exp_up[layer], w_exp_down[layer])
        if need_ctx:
            cx = cx + mc[2] * oc
            hc = modulate(rmsnorm(cx, norm2_g[layer]), mc[3], mc[4])
            cx = cx + mc[5] * expert_choice_ffn(hc, w_router[layer], w_exp_gate[layer],
                                                w_exp_up[layer], w_exp_down[layer])
    return x


_drawn_inputs = setup_inputs


def setup_inputs(seed=0):
    import zlib

    import numpy as np

    out = dict(_drawn_inputs(seed))
    spreads = {}
    factors = {'ctx': 2.719,
     'b_ada': 2.918,
     'norm1_g': 8.0,
     'norm2_g': 8.0,
     'gdn_a_log': 2.814,
     'gdn_onorm_g': 8.0,
     'swa_qnorm_g': 8.0,
     'swa_knorm_g': 8.0,
     'swa_sink': 8.0,
     'lru_conv_b': 4.625,
     'lru_gate_b': 8.0}
    for name, (base, spread) in spreads.items():
        noise = np.random.default_rng([zlib.crc32(name.encode()), seed]).standard_normal(out[name].shape)
        drawn = base * np.exp(spread * noise) if base else spread * noise
        out[name] = jnp.asarray(drawn.astype(out[name].dtype))
    for name, factor in factors.items():
        out[name] = (out[name] * factor).astype(out[name].dtype)
    return out
```

```python
from contextlib import ExitStack

import concourse.bass as bass
from concourse import mybir
from concourse.alu_op_type import AluOpType as ALU

ACT = mybir.ActivationFunctionType
F32 = mybir.dt.float32
U32 = mybir.dt.uint32
AX = mybir.AxisListType.X

P = 128
D = 1024
KD = D // P
SEQ, CTX = 1024, 256
CT, XT = CTX // P, SEQ // P
NT = CT + XT
TOK = CTX + SEQ
EPS = 1e-6
BIG = 1e30

GH, GC = 4, 64
W5 = 512
C5 = W5 // P
SH, SKV, HD = 8, 2, 64
NQK = SH + SKV
KEYS = 3 * P + CTX
NE, EH = 16, 2048
CAP = 2 * SEQ // NE

Q0, Z0, AB0, S0, XR0, Y0, G0 = 0, 1536, 2048, 2064, 2832, 3344, 3856

PCOL = dict(cc=KD * 2, b_ada=2 * KD, n1=KD, gconv=48, lconv=16, lconvb=4, lgb=16, lam=8, onorm=1)
PROW = dict(alog=8, dtb=8, qkg=NQK * HD, sink=SH)
PCON = dict(ident=P, ones=P, ident64=GC, blk=P, tri128=2 * P, tri=2 * GC, md=2 * GC, mdt=2 * GC, strict=2 * GC)
PSWA = dict(smask=3 * KEYS, cos=XT * 32, sin=XT * 32)


def offsets(widths):
    at, out = 0, {}
    for name, w in widths.items():
        out[name] = (at, at + w)
        at += w
    return out, at


PCOL_AT, PCOL_N = offsets(PCOL)
PROW_AT, PROW_N = offsets(PROW)
PCON_AT, PCON_N = offsets(PCON)
PSWA_AT, PSWA_N = offsets(PSWA)


class Core:

    def __init__(self, nc, io, ctx):
        self.nc, self.io, self.ctx = nc, io, ctx
        self.ps = ctx.enter_context(nc.psum_tensor("ps", [P, 8, 512], F32))
        self.col = self.keep("col_params", [P, PCOL_N])
        self.row = self.keep("row_params", [P, PROW_N])
        self.con = self.keep("tables", [P, PCON_N])
        self.mods = self.keep("mods", [P, 2 * KD, 2])
        self.silu_c = self.keep("silu_c", [P, KD, 2])
        self.scale1 = self.keep("scale1", [P, KD, 2])
        self.hT = None

    def keep(self, name, shape, dt=F32):
        return self.ctx.enter_context(self.nc.sbuf_tensor(name, shape, dt))

    def sem(self, name):
        self.sems.append(self.nc.alloc_semaphore(name=name))
        return self.sems[-1]

    def phase(self, build, *args):
        self.sems = []
        build(self, *args)
        self.nc.clear_and_free_semaphores(self.sems)
        self.nc.all_engine_barrier()

    def c(self, name):
        a, b = PCOL_AT[name]
        return self.col[:, a:b]

    def r(self, name):
        a, b = PROW_AT[name]
        return self.row[:, a:b]

    def k(self, name):
        a, b = PCON_AT[name]
        return self.con[:, a:b]

    def a(self, name):
        a, b = PSWA_AT[name]
        return self.swa_con[:, a:b]


def adaln(core):
    nc, io, ps = core.nc, core.io, core.ps
    NG, GW = 2 * D // 512, 512
    s_par, s_ld = core.sem("ada_params"), [core.sem(f"ada_w{i}") for i in range(NG)]
    s_silu, s_mm, s_row, s_col, s_ev, s_sc = (core.sem("ada_" + n) for n in (
        "silu", "multiplied", "rows_kept", "columns", "biased", "scale"))
    w_view = io["w_ada"].rearrange("(k p) n -> p k n", p=P)
    with ExitStack() as ctx:
        w = ctx.enter_context(nc.sbuf_tensor("w_ada_sb", [P, NG, KD, GW], F32))
        rows = ctx.enter_context(nc.sbuf_tensor("ada_rows", [2, NG, GW], F32))
        cc = core.c("cc").rearrange("p (k s) -> p k s", s=2)
        block = ctx.enter_context(nc.Block())

        @block.sync
        def _(sp):
            sp.dma_start(core.col[:], io["col"]).then_inc(s_par, 16)
            for g in range(NG):
                sp.dma_start(w[:, g], w_view[:, :, g * GW:(g + 1) * GW]).then_inc(s_ld[g], 16)
            sp.dma_start(core.con[:], io["con"]).then_inc(s_par, 16)
            sp.dma_start(core.row[:], io["row"]).then_inc(s_par, 16)

        @block.scalar
        def _(act):
            act.wait_ge(s_par, 48)
            nc.scalar.activation(core.silu_c[:], cc, ACT.Silu).then_inc(s_silu, 1)
            for g in range(NG):
                act.wait_ge(s_mm, g + 1)
                nc.scalar.copy(rows[:, g, :], ps[0:2, g, :]).then_inc(s_row, 1)

        @block.tensor
        def _(pe):
            def columns(g):
                pe.wait_ge(s_row, g + 1)
                for n in range(GW // P):
                    at = 2 * (g * GW // P + n)
                    tr = nc.tensor.transpose(ps[:, NG, at:at + 2], rows[:, g, n * P:(n + 1) * P], core.k("ident")[0:2, 0:2])
                return tr
            pe.wait_ge(s_silu, 1)
            for g in range(NG):
                pe.wait_ge(s_ld[g], 16)
                for k in range(KD):
                    mm = nc.tensor.matmul(ps[0:2, g, :], core.silu_c[:, k, :], w[:, g, k, :],
                                          start=(k == 0), stop=(k == KD - 1))
                mm.then_inc(s_mm, 1)
                if g:
                    columns(g - 1)
            columns(NG - 1).then_inc(s_col, 1)

        @block.vector
        def _(dve):
            dve.wait_ge(s_col, 1)
            nc.vector.tensor_tensor(
                core.mods[:], ps[:, NG, 0:4 * KD].rearrange("p (n s) -> p n s", s=2),
                core.c("b_ada").unsqueeze(2).broadcast_to([P, 2 * KD, 2]), ALU.add).then_inc(s_ev, 1)
            dve.wait_ge(s_ev, 1)
            nc.vector.scalar_tensor_tensor(
                core.scale1[:], core.mods[:, KD:2 * KD, :], 1.0,
                core.c("n1").unsqueeze(2).broadcast_to([P, KD, 2]), ALU.add, ALU.mult).then_inc(s_sc, 1)
            dve.wait_ge(s_sc, 1)


def norm1(core):
    nc, io, ps = core.nc, core.io, core.ps
    hT = core.hT
    s_ld = [core.sem(f"n1_x{i}") for i in range(2)]
    s_sq, s_v, s_rt, s_r, s_xn, s_tr = (core.sem("n1_" + n) for n in ("square", "mean", "root", "recip", "scaled", "transposed"))
    s_ea, s_ed = core.sem("n1_evac_act"), core.sem("n1_evac_dve")
    x_view = io["tokens"].rearrange("(t p) d -> t p d", p=P)
    H = KD // 2
    with ExitStack() as ctx:
        x = ctx.enter_context(nc.sbuf_tensor("x_tile", [P, 2, D], F32))
        xn = ctx.enter_context(nc.sbuf_tensor("x_scaled", [P, 2, D], F32))
        junk = ctx.enter_context(nc.sbuf_tensor("squares", [P, D], F32))
        st = ctx.enter_context(nc.sbuf_tensor("stats", [P, 2, 4], F32))
        ident = core.k("ident")
        block = ctx.enter_context(nc.Block())
        shift1 = core.mods

        def rounds(eng, body):
            body(0, 0, True)
            with eng.Fori(1, NT // 2) as i:
                body(i, 1, False)

        @block.sync
        def _(sp):
            def body(i, _, peeled):
                for j in range(2):
                    if not peeled:
                        sp.wait_ge(s_xn, 2 * (i - 1) + j + 1)
                    sp.dma_start(x[:, j, :], x_view[2 * i + j]).then_inc(s_ld[j], 16)
            rounds(sp, body)

        @block.scalar
        def _(act):
            def body(i, x_tiles, peeled):
                for j in range(2):
                    t = 2 * i + j
                    act.wait_ge(s_ld[j], 16 * i + 16)
                    if not (peeled and j == 0):
                        act.wait_ge(s_rt, t)
                    nc.scalar.activation(junk[:], x[:, j, :], ACT.Square, accum_out=st[:, j, 0:1]).then_inc(s_sq, 1)
                    act.wait_ge(s_v, t + 1)
                    nc.scalar.activation(st[:, j, 2:3], st[:, j, 1:2], ACT.Sqrt).then_inc(s_rt, 1)
                for j in range(2):
                    t = 2 * i + j
                    act.wait_ge(s_tr, t + 1)
                    for k in range(H):
                        ev = nc.scalar.activation(
                            hT[:, k, bass.ts(t, P)], ps[:, 2 * j, k * P:(k + 1) * P], ACT.Identity,
                            scale=core.scale1[:, k, 1 - x_tiles:2 - x_tiles],
                            bias=shift1[:, k, 1 - x_tiles:2 - x_tiles])
                    ev.then_inc(s_ea, 1)
            rounds(act, body)

        @block.vector
        def _(dve):
            def body(i, x_tiles, peeled):
                for j in range(2):
                    t = 2 * i + j
                    dve.wait_ge(s_sq, t + 1)
                    nc.vector.tensor_scalar(st[:, j, 1:2], st[:, j, 0:1], 1.0 / D, EPS, ALU.mult, ALU.add).then_inc(s_v, 1)
                    dve.wait_ge(s_rt, t + 1)
                    nc.vector.reciprocal(st[:, j, 3:4], st[:, j, 2:3]).then_inc(s_r, 1)
                    dve.wait_ge(s_r, t + 1)
                    if not peeled:
                        dve.wait_ge(s_tr, 2 * (i - 1) + j + 1)
                    nc.vector.tensor_scalar(xn[:, j, :], x[:, j, :], st[:, j, 3:4], None, ALU.mult).then_inc(s_xn, 1)
                for j in range(2):
                    t = 2 * i + j
                    dve.wait_ge(s_tr, t + 1)
                    for k in range(H, KD):
                        ev = nc.vector.tensor_scalar(
                            hT[:, k, bass.ts(t, P)], ps[:, 2 * j + 1, (k - H) * P:(k - H + 1) * P],
                            core.scale1[:, k, 1 - x_tiles:2 - x_tiles], shift1[:, k, 1 - x_tiles:2 - x_tiles],
                            ALU.mult, ALU.add)
                    ev.then_inc(s_ed, 1)
            rounds(dve, body)

        @block.tensor
        def _(pe):
            def body(i, _, peeled):
                for j in range(2):
                    t = 2 * i + j
                    pe.wait_ge(s_xn, t + 1)
                    if not peeled:
                        pe.wait_ge(s_ea, 2 * (i - 1) + j + 1)
                        pe.wait_ge(s_ed, 2 * (i - 1) + j + 1)
                    for k in range(KD):
                        tr = nc.tensor.transpose(ps[:, 2 * j + k // H, (k % H) * P:(k % H + 1) * P],
                                                 xn[:, j, k * P:(k + 1) * P], ident)
                    tr.then_inc(s_tr, 1)
            rounds(pe, body)


class Serial:

    def __init__(self, eng, sem, base=0):
        self.eng, self.sem, self.base, self.n = eng, sem, base, 0

    def __call__(self, ins):
        ins.then_inc(self.sem, 1)
        self.n += 1
        self.eng.wait_ge(self.sem, self.base + self.n)


LOG_TERMS = 9


def softplus_tail(nc, step, z, s, q, acc):
    v = nc.vector
    step(v.tensor_scalar(q, z, 2.0, None, ALU.add))
    step(v.reciprocal(s, q))
    step(v.tensor_tensor(s, s, z, ALU.mult))
    step(v.tensor_tensor(q, s, s, ALU.mult))
    step(v.tensor_scalar(acc, q, 1.0 / (2 * LOG_TERMS + 1), 1.0 / (2 * LOG_TERMS - 1), ALU.mult, ALU.add))
    for n in range(LOG_TERMS - 2, -1, -1):
        step(v.tensor_tensor(acc, acc, q, ALU.mult))
        step(v.tensor_scalar(acc, acc, 1.0 / (2 * n + 1), None, ALU.add))
    step(v.scalar_tensor_tensor(acc, acc, 2.0, s, ALU.mult, ALU.mult))


def load_w_in(core, sp, dst, col, width, sem):
    sp.dma_start(dst, core.io["w_in"].rearrange("(k p) n -> p k n", p=P)[:, :, col:col + width]).then_inc(sem, 16)


PIECES = ((0, CTX, 2 * CTX - CTX), (CTX, 512, 512), (CTX + 512, 512, 1024))
PADDED = 2 + CTX + 1 + 2 + SEQ + 1
PAD_AT = (2, 2 + CTX + 1 + 2)
CONV = PADDED - 3


def lru(core):
    nc, io, ps, hT = core.nc, core.io, core.ps, core.hT
    gy = core.branch[2]
    s_w = [core.sem(f"lru_w{i}") for i in range(2)]
    s_bias, s_lw, s_lm, s_lb = core.sem("late_biases"), core.sem("late_w"), core.sem("late_multiplied"), core.sem("late_biased")
    s_lgw, s_pad = core.sem("lru_gate_weights"), core.sem("lru_padding")
    s_mm, s_xr, s_gy = core.sem("lru_projected"), core.sem("lru_xr_kept"), core.sem("lru_gelu_kept")
    s_pre, s_dve, s_u = core.sem("lru_gates_multiplied"), core.sem("lru_dve_steps"), core.sem("lru_conv_done")
    s_ez, s_par = core.sem("lru_exp_lambda"), core.sem("lru_decay_rate")
    s_ri, s_et, s_sq, s_iu, s_unit = (core.sem("lru_" + n) for n in
                                      ("sigmoids", "exp_tanh", "roots", "input_gated", "unit_done"))
    flat = ps[:].rearrange("p b n -> p (b n)")
    with ExitStack() as ctx:
        def sb(name, shape):
            return ctx.enter_context(nc.sbuf_tensor(name, shape, F32))
        w = sb("lru_w_in", [P, 2, KD, W5])
        wl = w[:, 0]
        lgw = sb("lru_gw", [P, 2, 2, C5, P])
        xr = sb("lru_xr", [P, C5, PADDED])
        u = sb("lru_u", [P, PADDED])
        par = sb("lru_par", [P, 6, 8])
        R, I, T, S = (sb("lru_" + n, [P, 2, TOK]) for n in "RITS")
        iu = sb("lru_iu", [P, TOK])
        block = ctx.enter_context(nc.Block())
        UNITS = [(c, d) for c in range(C5) for d in range(2)]
        lgb = core.c("lgb").rearrange("p (d g c) -> p d g c", d=2, g=2)
        conv_w = core.c("lconv").rearrange("p (c j) -> p c j", j=4)
        NP8 = 2 * C5

        def u_of(c):
            return (u[:, 0:CTX], u[:, CTX + 3:CTX + 3 + SEQ])

        @block.sync
        def _(sp):
            load_w_in(core, sp, w[:, 0], XR0, W5, s_w[0])
            load_w_in(core, sp, w[:, 1], Y0, W5, s_w[1])
            sp.dma_start(lgw[:].rearrange("p d g c n -> p (d g c n)"), io["lgw"]).then_inc(s_lgw, 16)
            for r in range(4):
                sp.dma_start(core.late_mods[32 * r:32 * r + 1, :], io["b_late"][r:r + 1, :]).then_inc(s_bias, 16)
            sp.dma_start(core.late[64:65, 0, :], io["n2_row"]).then_inc(s_bias, 16)
            for g in range(4 * D // 512):
                if g:
                    sp.wait_ge(s_lm, g)
                else:
                    sp.wait_ge(s_mm, C5)
                sp.dma_start(wl, io["w_ada"].rearrange("(k p) n -> p k n", p=P)
                             [:, :, 2 * D + 512 * g:2 * D + 512 * g + 512]).then_inc(s_lw, 16)

        @block.gpsimd
        def _(pool):
            nc.gpsimd.memset(xr[:, :, 0:2], 0.0)
            nc.gpsimd.memset(xr[:, :, 2 + CTX:5 + CTX], 0.0)
            nc.gpsimd.memset(xr[:, :, PADDED - 1:PADDED], 0.0).then_inc(s_pad, 1)
            for n, (c, d) in enumerate(UNITS):
                pool.wait_ge(s_ri, n + 1)
                pool.wait_ge(s_u, c + 1)
                if n:
                    pool.wait_ge(s_unit, n)
                for a, (at, num, _) in zip(u_of(c), ((0, CTX, 0), (CTX, SEQ, 0))):
                    op = nc.gpsimd.tensor_tensor(iu[:, at:at + num], I[:, d, at:at + num], a, ALU.mult)
                op.then_inc(s_iu, 1)

        @block.tensor
        def _(pe):
            for c in range(C5):
                if c == 0:
                    pe.wait_ge(s_w[0], 16)
                if c >= 2:
                    pe.wait_ge(s_xr, c - 1)
                for t0, n, at in PIECES:
                    for k in range(KD):
                        mm = nc.tensor.matmul(flat[:, (c % 2) * 1536 + at:(c % 2) * 1536 + at + n],
                                              w[:, 0, k, c * P:(c + 1) * P], hT[:, k, t0:t0 + n],
                                              start=(k == 0), stop=(k == KD - 1))
                mm.then_inc(s_mm, 1)
            def project_y(c):
                if c == 0:
                    pe.wait_ge(s_w[1], 16)
                else:
                    pe.wait_ge(s_gy, c)
                for t0, n, at in PIECES[1:]:
                    for k in range(KD):
                        mm = nc.tensor.matmul(flat[:, 2560 + at:2560 + at + n], w[:, 1, k, c * P:(c + 1) * P],
                                              hT[:, k, t0:t0 + n], start=(k == 0), stop=(k == KD - 1))
                mm.then_inc(s_mm, 1)

            def late_mods(g):
                r, q = divmod(g, 2)
                pe.wait_ge(s_lw, 16 * g + 16)
                if q == 0:
                    pe.wait_ge(s_gy, r + 1)
                for k in range(KD):
                    mm = nc.tensor.matmul(ps[32 * r:32 * r + 1, 6 + q, :], core.silu_c[:, k, 0:1], wl[:, k, :],
                                          start=(k == 0), stop=(k == KD - 1))
                mm.then_inc(s_lm, 1)

            project_y(0)
            pe.wait_ge(s_lgw, 16)
            pe.wait_ge(s_xr, C5)
            for n, (c, d) in enumerate(UNITS):
                pe.wait_ge(s_u, c + 1)
                if n:
                    pe.wait_ge(s_ri, n)
                for g in range(2):
                    for a, (t0, num, at) in ((u_of(c)[0], PIECES[0]), (u_of(c)[1][:, 0:512], PIECES[1]),
                                             (u_of(c)[1][:, 512:SEQ], PIECES[2])):
                        mm = nc.tensor.matmul(flat[:, g * 1536 + at:g * 1536 + at + num], lgw[:, d, g, c, :], a,
                                              start=True, stop=True)
                mm.then_inc(s_pre, 1)
                if d:
                    late_mods(2 * c)
                    late_mods(2 * c + 1)
                if d and c + 1 < C5:
                    pe.wait_ge(s_lb, 2 * c + 2)
                    project_y(c + 1)

        @block.scalar
        def _(act):
            def gelu(c):
                act.wait_ge(s_mm, C5 + c + 1)
                nc.scalar.activation(gy[:, c, :], flat[:, 3072:4096], ACT.Gelu_apprx_tanh).then_inc(s_gy, 1)

            nc.scalar.activation(par[:, 0, :], core.c("lam"), ACT.Abs).then_inc(s_ez, 1)
            act.wait_ge(s_ez, 1)
            nc.scalar.activation(par[:, 1, :], par[:, 0, :], ACT.Exp, scale=-1.0).then_inc(s_ez, 1)
            for c in range(C5):
                if c == 0:
                    gelu(0)
                for d in range(2):
                    n = 2 * c + d
                    act.wait_ge(s_pre, n + 1)
                    if c:
                        act.wait_ge(s_unit, n - 1)
                    for g, dst in ((0, R), (1, I)):
                        a = nc.scalar.activation(dst[:, d, :], flat[:, g * 1536 + 256:g * 1536 + 1536], ACT.Sigmoid,
                                                 bias=lgb[:, d, g, c:c + 1])
                    a.then_inc(s_ri, 1)
                act.wait_ge(s_ri, 2 * c + 2)
                act.wait_ge(s_par, 1)
                for d in range(2):
                    j = d * C5 + c
                    nc.scalar.activation(T[:, d, :], R[:, d, :], ACT.Tanh, scale=par[:, 4, j:j + 1])
                for d in range(2):
                    j = d * C5 + c
                    nc.scalar.activation(R[:, d, :], R[:, d, :], ACT.Exp, scale=par[:, 5, j:j + 1]).then_inc(s_et, 1)
                act.wait_ge(s_et, 2 * c + 2)
                for d in range(2):
                    nc.scalar.activation(S[:, d, :], T[:, d, :], ACT.Sqrt).then_inc(s_sq, 1)
                if c + 1 < C5:
                    gelu(c + 1)

        @block.vector
        def _(dve):
            step = Serial(dve, s_dve)
            v = nc.vector
            dve.wait_ge(s_ez, 2)
            softplus_tail(nc, step, par[:, 1, :], par[:, 2, :], par[:, 3, :], par[:, 0, :])
            step(v.tensor_scalar(par[:, 1, :], core.c("lam"), -1.0, 0.0, ALU.mult, ALU.max))
            step(v.tensor_tensor(par[:, 0, :], par[:, 0, :], par[:, 1, :], ALU.add))
            v.tensor_scalar(par[:, 4, :], par[:, 0, :], 4.0, None, ALU.mult)
            v.tensor_scalar(par[:, 5, :], par[:, 0, :], -8.0, None, ALU.mult).then_inc(s_par, 1)
            dve.wait_ge(s_pad, 1)
            for c in range(C5):
                dve.wait_ge(s_mm, c + 1)
                o = (c % 2) * 1536
                v.tensor_copy(xr[:, c, 2:2 + CTX], flat[:, o + 256:o + 512])
                v.tensor_copy(xr[:, c, PAD_AT[1]:PAD_AT[1] + SEQ], flat[:, o + 512:o + 1536]).then_inc(s_xr, 1)
            dve.wait_ge(s_xr, C5)
            for c in range(C5):
                if c:
                    dve.wait_ge(s_pre, 2 * c)
                    dve.wait_ge(s_iu, 2 * c)
                step(v.tensor_scalar(u[:, 0:CONV], xr[:, c, 0:CONV], conv_w[:, c, 0:1], core.c("lconvb")[:, c:c + 1],
                                     ALU.mult, ALU.add))
                for j in range(1, 4):
                    op = v.scalar_tensor_tensor(u[:, 0:CONV], xr[:, c, j:j + CONV], conv_w[:, c, j:j + 1],
                                                u[:, 0:CONV], ALU.mult, ALU.add)
                    step(op) if j < 3 else op.then_inc(s_u, 1)
                for d in range(2):
                    n = 2 * c + d
                    if d:
                        dve.wait_ge(s_bias, 80)
                        row = slice(32 * c, 32 * c + 1)
                        for q in range(2):
                            cols = slice(512 * q, 512 * q + 512)
                            dve.wait_ge(s_lm, n + q)
                            v.tensor_tensor(core.late_mods[row, cols], core.late_mods[row, cols], ps[row, 6 + q, :],
                                            ALU.add).then_inc(s_lb, 1)
                    r, t, s = R[:, d, :], T[:, d, :], S[:, d, :]
                    dve.wait_ge(s_sq, n + 1)
                    step(v.scalar_tensor_tensor(t, r, 1.0, t, ALU.add, ALU.mult))
                    step(v.tensor_scalar(t, t, -1.0, 1.0, ALU.mult, ALU.add))
                    step(v.scalar_tensor_tensor(s, t, 1.0, s, ALU.add, ALU.mult))
                    dve.wait_ge(s_iu, n + 1)
                    step(v.tensor_tensor(s, s, iu[:], ALU.mult))
                    if d == 0:
                        v.tensor_tensor_scan(r, t, s, 0.0, ALU.mult, ALU.add).then_inc(s_unit, 1)
                    else:
                        rc, tc, sc = r[:, 0:CTX], t[:, 0:CTX], s[:, 0:CTX]
                        rx, tx, sx = r[:, CTX:], t[:, CTX:], s[:, CTX:]
                        step(v.tensor_tensor_scan(rc[:, ::-1], tc[:, ::-1], sc[:, ::-1], 0.0, ALU.mult, ALU.add))
                        step(v.tensor_tensor_scan(rx[:, ::-1], tx[:, ::-1], sx[:, ::-1], r[:, 0:1], ALU.mult, ALU.add))
                        step(v.tensor_tensor(S[:, 0, CTX:], R[:, 0, CTX:], R[:, 1, CTX:], ALU.add))
                        dve.wait_ge(s_gy, c + 1)
                        v.tensor_tensor(gy[:, c, :], gy[:, c, :], S[:, 0, CTX:], ALU.mult).then_inc(s_unit, 1)


PADK = P + SEQ + P
KEYCOLS = PADK + CTX


def swa_project(core, qT, kT, V):
    nc, io, ps, hT = core.nc, core.io, core.ps, core.hT
    flat = ps[:].rearrange("p b n -> p (b n)")
    s_w, s_zero, s_con = core.sem("swa_w"), core.sem("swa_zeroed"), core.sem("swa_tables")
    s_mm, s_v, s_sq, s_ss, s_rt, s_dve, s_rd = (core.sem("swap_" + n) for n in
                                          ("projected", "v_kept", "squares", "means", "roots", "dve_steps", "banks_read"))
    s_g, s_pp, s_rope, s_tr, s_ev = (core.sem("swap_" + n) for n in ("gained", "pool_products", "rotated", "transposed", "evacuated"))
    with ExitStack() as ctx:
        def sb(name, shape):
            return ctx.enter_context(nc.sbuf_tensor(name, shape, F32))
        w = sb("swa_w_in", [P, KD, 768])
        sq = sb("swa_squares", [P, NQK, HD])
        st = sb("swa_stats", [P, 2, 4, NQK])
        t = sb("swa_normed", [P, 2, NQK, HD])
        m = sb("swa_products", [P, 4, NQK, HD // 2])
        dst = sb("swa_rotated", [P, 2, NQK, HD])
        block = ctx.enter_context(nc.Block())
        KV0, NQ = SH * HD, SH
        cos = core.a("cos").rearrange("p (t d) -> p t d", t=XT)
        sin = core.a("sin").rearrange("p (t d) -> p t d", t=XT)
        gain = core.r("qkg").rearrange("p (h d) -> p h d", d=HD)

        def heads(tile):
            return slice(NQ, NQK) if tile < CT else slice(0, NQK)

        def bank(tile):
            o = 1024 * (tile % 2)
            return flat[:, o:o + 768]

        @block.sync
        def _(sp):
            sp.dma_start(core.swa_con[:], io["swa_con"]).then_inc(s_con, 16)
            load_w_in(core, sp, w[:], S0, 768, s_w)
            sp.wait_ge(s_con, 16)

        @block.gpsimd
        def _(pool):
            g = nc.gpsimd
            pool.wait_ge(s_con, 16)
            g.memset(kT[:, 0:P], 0.0)
            g.memset(kT[:, P + SEQ:PADK], 0.0)
            g.memset(V[:, 0, :], 0.0)
            g.memset(V[:, 1 + XT, :], 0.0).then_inc(s_zero, 1)
            for n in range(NT):
                if n < CT:
                    continue
                pool.wait_ge(s_g, n + 1)
                if n > CT:
                    pool.wait_ge(s_rope, n)
                tt = t[:, n % 2].rearrange("p h (d e) -> p h d e", e=2)
                cs = cos[:, n - CT, :].unsqueeze(1).broadcast_to([P, NQK, 32])
                sn = sin[:, n - CT, :].unsqueeze(1).broadcast_to([P, NQK, 32])
                g.tensor_tensor(m[:, 1], tt[:, :, :, 1], sn, ALU.mult)
                g.tensor_tensor(m[:, 3], tt[:, :, :, 1], cs, ALU.mult).then_inc(s_pp, 1)

        @block.tensor
        def _(pe):
            def transposes(n):
                pe.wait_ge(s_rope, n + 1)
                if n >= CT + 2:
                    pe.wait_ge(s_ev, n - 1)
                o = 2048 + 1024 * (n % 2)
                pairs = range(4, 5) if n < CT else range(5)
                for i in pairs:
                    tr = nc.tensor.transpose(flat[:, o + i * P:o + (i + 1) * P],
                                             dst[:, n % 2, 2 * i:2 * i + 2, :].rearrange("p h d -> p (h d)"),
                                             core.k("ident"))
                tr.then_inc(s_tr, 1)

            pe.wait_ge(s_w, 16)
            for n in range(NT):
                if n >= 2:
                    pe.wait_ge(s_rd, n - 1)
                    pe.wait_ge(s_v, n - 1)
                    pe.wait_ge(s_sq, n - 1)
                out = bank(n)
                for a, b in ((0, KV0), (KV0, 768)) if n >= CT else ((KV0, 768),):
                    for k in range(KD):
                        mm = nc.tensor.matmul(out[:, a:b], hT[:, k, n * P:(n + 1) * P], w[:, k, a:b],
                                              start=(k == 0), stop=(k == KD - 1))
                mm.then_inc(s_mm, 1)
                if n:
                    transposes(n - 1)
            transposes(NT - 1)

        @block.scalar
        def _(act):
            def keep(n):
                act.wait_ge(s_tr, n + 1)
                o = 2048 + 1024 * (n % 2)
                if n >= CT:
                    nc.scalar.copy(qT[:, :, (n - CT) * P:(n - CT + 1) * P],
                                   flat[:, o:o + 512].rearrange("p (g q) -> p g q", g=4))
                at = PADK + n * P if n < CT else P + (n - CT) * P
                nc.scalar.copy(kT[:, at:at + P], flat[:, o + 512:o + 640]).then_inc(s_ev, 1)

            for n in range(NT):
                act.wait_ge(s_mm, n + 1)
                h = heads(n)
                out = bank(n)[:, 0:NQK * HD].rearrange("p (h d) -> p h d", d=HD)
                if n:
                    act.wait_ge(s_ss, n)
                nc.scalar.activation(sq[:, h, :], out[:, h, :], ACT.Square).then_inc(s_sq, 1)
                nc.scalar.copy(V[:, (1 + XT + 1 + n) if n < CT else 1 + n - CT, :], bank(n)[:, 640:768]).then_inc(s_v, 1)
                act.wait_ge(s_ss, n + 1)
                nc.scalar.activation(st[:, n % 2, 1, h], st[:, n % 2, 0, h], ACT.Sqrt).then_inc(s_rt, 1)
                if n:
                    keep(n - 1)
            keep(NT - 1)

        @block.vector
        def _(dve):
            step = Serial(dve, s_dve)
            v = nc.vector
            dve.wait_ge(s_con, 16)
            for n in range(NT):
                h, b = heads(n), n % 2
                N = NQK if n >= CT else SKV
                out = bank(n)[:, 0:NQK * HD].rearrange("p (h d) -> p h d", d=HD)
                dve.wait_ge(s_sq, n + 1)
                step(v.tensor_reduce(st[:, b, 2, h], sq[:, h, :], AX, ALU.add))
                v.tensor_scalar(st[:, b, 0, h], st[:, b, 2, h], 1.0 / HD, EPS, ALU.mult, ALU.add).then_inc(s_ss, 1)
                dve.wait_ge(s_rt, n + 1)
                step(v.reciprocal(st[:, b, 3, h], st[:, b, 1, h]))
                v.tensor_tensor(t[:, b, h, :], out[:, h, :], st[:, b, 3, h].unsqueeze(2).broadcast_to([P, N, HD]),
                                ALU.mult).then_inc(s_rd, 1)
                dve.wait_ge(s_rd, n + 1)
                v.tensor_tensor(t[:, b, h, :], t[:, b, h, :], gain[:, h, :], ALU.mult).then_inc(s_g, 1)
                dve.wait_ge(s_g, n + 1)
                if n >= 2:
                    dve.wait_ge(s_tr, n - 1)
                tt = t[:, b].rearrange("p h (d e) -> p h d e", e=2)
                if n < CT:
                    v.tensor_copy(dst[:, b, NQ:, 0:32], tt[:, NQ:, :, 0])
                    v.tensor_copy(dst[:, b, NQ:, 32:64], tt[:, NQ:, :, 1]).then_inc(s_rope, 1)
                    continue
                cs = cos[:, n - CT, :].unsqueeze(1).broadcast_to([P, NQK, 32])
                sn = sin[:, n - CT, :].unsqueeze(1).broadcast_to([P, NQK, 32])
                v.tensor_tensor(m[:, 0], tt[:, :, :, 0], cs, ALU.mult)
                step(v.tensor_tensor(m[:, 2], tt[:, :, :, 0], sn, ALU.mult))
                dve.wait_ge(s_pp, n - CT + 1)
                q_dst = dst[:, b, 0:NQ, :].rearrange("p (g v) d -> p v g d", v=2)
                for lo, x, y, op in ((0, 0, 1, ALU.subtract), (32, 2, 3, ALU.add)):
                    v.tensor_tensor(q_dst[:, :, :, lo:lo + 32], m[:, x, 0:NQ].rearrange("p (v g) d -> p v g d", v=2),
                                    m[:, y, 0:NQ].rearrange("p (v g) d -> p v g d", v=2), op)
                    last = v.tensor_tensor(dst[:, b, NQ:, lo:lo + 32], m[:, x, NQ:], m[:, y, NQ:], op)
                last.then_inc(s_rope, 1)
            dve.wait_ge(s_zero, 1)


def swa_attend(core, qT, kT, V):
    nc, io, ps = core.nc, core.io, core.ps
    out_b = core.branch[1]
    flat = ps[:].rearrange("p b n -> p (b n)")
    s_s, s_mx, s_nm, s_e, s_es, s_den, s_dve, s_p, s_tr, s_pt, s_pv, s_o = (core.sem("swa_" + n) for n in (
        "scores", "masked_max", "minus_max", "exps", "sink_exp", "den", "dve_steps", "probs", "probs_turned", "turned_kept",
        "values_summed", "output_kept"))
    with ExitStack() as ctx:
        def sb(name, shape):
            return ctx.enter_context(nc.sbuf_tensor(name, shape, F32))
        S = sb("swa_S", [P, 2, KEYS])
        pr = sb("swa_P", [P, 3, KEYS])
        PT = sb("swa_PT", [P, 2, 5, 4, P])
        sc = sb("swa_cols", [P, 2, 8])
        block = ctx.enter_context(nc.Block())
        mask = core.a("smask").rearrange("p (m s) -> p m s", m=3)
        sink = core.r("sink")
        JOBS = [(n, kv, g) for n in range(XT) for kv in range(SKV) for g in range(4)]

        @block.tensor
        def _(pe):
            def turned(m):
                n, kv, g = JOBS[m]
                pe.wait_ge(s_p, m + 1)
                if m >= 2:
                    pe.wait_ge(s_pt, m - 1)
                big, small = (4, 5) if m % 2 == 0 else (6, 5)
                lo = 256 * (m % 2)
                for i in range(5):
                    if i == 4 and m:
                        pe.wait_ge(s_pt, m)
                    o = ps[:, big, i * P:(i + 1) * P] if i < 4 else ps[:, small, lo:lo + P]
                    tr = nc.tensor.transpose(o, pr[:, m % 3, i * P:(i + 1) * P], core.k("ident"))
                tr.then_inc(s_tr, 1)

            def values(m):
                n, kv, _ = JOBS[m]
                pe.wait_ge(s_pt, m + 1)
                if kv == 0 and n:
                    pe.wait_ge(s_o, n)
                for i in range(5):
                    tile = n + i if i < 3 else XT + 2 + i - 3
                    mm = nc.tensor.matmul(ps[64 * kv:64 * kv + 64, 7, :], V[:, tile, 64 * kv:64 * kv + 64],
                                          PT[:, kv, i].rearrange("p g q -> p (g q)"), start=(i == 0), stop=(i == 4))
                mm.then_inc(s_pv, 1)

            for m, (n, kv, g) in enumerate(JOBS):
                if m >= 2:
                    pe.wait_ge(s_mx, m - 1)
                o = 1024 * (m % 2)
                q = qT[64 * kv:64 * kv + 64, g, n * P:(n + 1) * P]
                nc.tensor.matmul(flat[:, o + P:o + 4 * P], q, kT[64 * kv:64 * kv + 64, n * P:(n + 3) * P],
                                 start=True, stop=True)
                nc.tensor.matmul(flat[:, o + 4 * P:o + 6 * P], q, kT[64 * kv:64 * kv + 64, PADK:KEYCOLS],
                                 start=True, stop=True).then_inc(s_s, 1)
                if m >= 2:
                    turned(m - 2)
                    if m % 4 == 2 and m > 4:
                        values(m - 3)
            turned(len(JOBS) - 2)
            turned(len(JOBS) - 1)
            values(len(JOBS) - 1)

        @block.vector
        def _(dve):
            v = nc.vector
            step = Serial(dve, s_dve)

            def evacuate(n):
                dve.wait_ge(s_pv, 2 * n + 2)
                v.tensor_copy(out_b[:, :, n * P:(n + 1) * P], ps[:, 7, :].rearrange("p (g q) -> p g q", g=4)).then_inc(s_o, 1)

            def norm(m):
                b = m % 2
                dve.wait_ge(s_es, m + 1)
                step(v.tensor_tensor(sc[:, b, 4:5], sc[:, b, 2:3], sc[:, b, 3:4], ALU.add))
                step(v.reciprocal(sc[:, b, 5:6], sc[:, b, 4:5]))
                v.tensor_scalar(pr[:, m % 3], pr[:, m % 3], sc[:, b, 5:6], None, ALU.mult).then_inc(s_p, 1)

            for m, (n, kv, g) in enumerate(JOBS):
                b, o = m % 2, 1024 * (m % 2)
                kind = 0 if n == 0 else 2 if n == XT - 1 else 1
                slot = 2 * g + kv
                dve.wait_ge(s_s, m + 1)
                v.tensor_tensor_reduce(S[:, b], flat[:, o + P:o + 6 * P], mask[:, kind], HD ** -0.5,
                                       sink[:, slot:slot + 1], ALU.add, ALU.max, sc[:, b, 0:1]).then_inc(s_mx, 1)
                dve.wait_ge(s_mx, m + 1)
                v.tensor_scalar(sc[:, b, 1:2], sc[:, b, 0:1], -1.0, None, ALU.mult).then_inc(s_nm, 1)
                if m:
                    norm(m - 1)
                if m % 8 == 3 and m > 8:
                    evacuate((m - 11) // 8)
            norm(len(JOBS) - 1)
            evacuate(XT - 1)

        @block.scalar
        def _(act):
            def kept(m):
                n, kv, g = JOBS[m]
                act.wait_ge(s_tr, m + 1)
                if n and g == 0:
                    act.wait_ge(s_pv, 2 * (n - 1) + kv + 1)
                big, lo = (4, 0) if m % 2 == 0 else (6, 256)
                nc.scalar.copy(PT[:, kv, 0:4, g, :], ps[:, big, :].rearrange("p (i q) -> p i q", i=4))
                nc.scalar.copy(PT[:, kv, 4, g, :], ps[:, 5, lo:lo + P]).then_inc(s_pt, 1)

            for m, (n, kv, g) in enumerate(JOBS):
                b, slot = m % 2, 2 * g + kv
                act.wait_ge(s_nm, m + 1)
                if m >= 3:
                    act.wait_ge(s_tr, m - 2)
                nc.scalar.activation(pr[:, m % 3], S[:, b], ACT.Exp, bias=sc[:, b, 1:2], accum_out=sc[:, b, 2:3]).then_inc(s_e, 1)
                nc.scalar.activation(sc[:, b, 3:4], sink[:, slot:slot + 1], ACT.Exp, bias=sc[:, b, 1:2]).then_inc(s_es, 1)
                if m >= 2:
                    kept(m - 2)
            kept(len(JOBS) - 2)
            kept(len(JOBS) - 1)


def swa(core):
    core.branch[1] = core.keep("branch_swa", [P, C5, SEQ])
    with ExitStack() as ctx:
        def sb(name, shape):
            return ctx.enter_context(core.nc.sbuf_tensor(name, shape, F32))
        core.swa_con = sb("swa_tables_sb", [P, PSWA_N])
        qT, kT, V = sb("qT", [P, 4, SEQ]), sb("kT", [P, KEYCOLS]), sb("V", [P, XT + 2 + CT, P])
        core.phase(swa_project, qT, kT, V)
        core.phase(swa_attend, qT, kT, V)


class Gdn:

    def __init__(self, core, ctx):
        def sb(name, shape):
            return ctx.enter_context(core.nc.sbuf_tensor(name, shape, F32))
        self.ktok, self.vtok = sb("gdn_ktok", [P, NT, GH, P]), sb("gdn_vtok", [P, NT, GH, P])
        self.kT, self.qT = sb("gdn_kT", [P, GH, TOK]), sb("gdn_qT", [P, GH, SEQ])
        self.g, self.gb, self.beta, self.bg, self.el = (sb("gdn_" + n, [P, NT, 2 * GH]) for n in ("g", "gb", "beta", "bg", "el"))


def gdn_project(core, G):
    nc, io, ps, hT = core.nc, core.io, core.ps, core.hT
    flat = ps[:].rearrange("p b n -> p (b n)")
    GW = 256
    CH = 3 * C5
    s_w = [core.sem(f"gdn_w{i}") for i in range(2)]
    names = ("padded", "projected", "raw_kept", "conv", "silu", "by_tokens", "squares", "means", "roots", "dve_steps",
             "tok_kept", "turned_back", "turned_kept")
    s_pad, s_mm, s_raw, s_cv, s_si, s_tt, s_sq, s_ss, s_rt, s_dve, s_tk, s_tb, s_tbk = (core.sem("gdnp_" + n) for n in names)
    with ExitStack() as ctx:
        def sb(name, shape):
            return ctx.enter_context(nc.sbuf_tensor(name, shape, F32))
        w = sb("gdn_w_in", [P, 2, KD, GW])
        raw = sb("gdn_raw", [P, 2, PADDED])
        cv = sb("gdn_conv", [P, PADDED])
        si = sb("gdn_silu", [P, PADDED])
        sq = sb("gdn_squares", [P, NT, P])
        qtok = sb("gdn_qtok", [P, NT, P])
        st = sb("gdn_stats", [P, 4, NT])
        block = ctx.enter_context(nc.Block())
        conv_w = core.c("gconv").rearrange("p (c j) -> p c j", j=4)
        TOKB = 1536 * 1 + 256
        TURN = 3072
        tok_ps = flat[:, TOKB:TOKB + TOK].rearrange("p (t c) -> p t c", c=P)

        def turns(c):
            return 2 * min(c, C5) + 3 * max(0, c - C5)

        def si_tile(t):
            o = t * P if t < CT else CTX + 3 + (t - CT) * P
            return si[:, o:o + P]

        @block.sync
        def _(sp):
            for n in range(CH * P // GW):
                if n >= 2:
                    sp.wait_ge(s_mm, 2 * (n - 1))
                load_w_in(core, sp, w[:, n % 2], Q0 + n * GW, GW, s_w[n % 2])

        @block.gpsimd
        def _(pool):
            for b in range(2):
                nc.gpsimd.memset(raw[:, b, 0:2], 0.0)
                nc.gpsimd.memset(raw[:, b, 2 + CTX:5 + CTX], 0.0)
                nc.gpsimd.memset(raw[:, b, PADDED - 1:PADDED], 0.0).then_inc(s_pad, 1)

        @block.tensor
        def _(pe):
            def by_tokens(c):
                pe.wait_ge(s_si, c + 1)
                if c:
                    pe.wait_ge(s_tk, c)
                for t in range(NT):
                    tr = nc.tensor.transpose(tok_ps[:, t, :], si_tile(t), core.k("ident"))
                tr.then_inc(s_tt, 1)

            def turn_back(c):
                pe.wait_ge(s_tk, c + 1)
                tiles = list(range(CT if c < C5 else 0, NT))
                for i in range(0, len(tiles), 4):
                    group = tiles[i:i + 4]
                    n = turns(c) + i // 4
                    if n >= 2:
                        pe.wait_ge(s_tbk, n - 1)
                    for j, t in enumerate(group):
                        src = qtok[:, t, :] if c < C5 else G.ktok[:, t, c - C5, :]
                        tr = nc.tensor.transpose(flat[:, TURN + 512 * (n % 2) + j * P:TURN + 512 * (n % 2) + (j + 1) * P],
                                                 src, core.k("ident"))
                    tr.then_inc(s_tb, 1)

            for c in range(CH):
                pe.wait_ge(s_w[(c // 2) % 2], 16 * (c // 4 + 1))
                if c:
                    pe.wait_ge(s_raw, c)
                for t0, n, at in PIECES:
                    for k in range(KD):
                        mm = nc.tensor.matmul(flat[:, at:at + n], w[:, (c // 2) % 2, k, (c % 2) * P:(c % 2 + 1) * P],
                                              hT[:, k, t0:t0 + n], start=(k == 0), stop=(k == KD - 1))
                mm.then_inc(s_mm, 1)
                if c:
                    by_tokens(c - 1)
                if 2 <= c <= 2 * C5 + 1:
                    turn_back(c - 2)
            by_tokens(CH - 1)

        @block.scalar
        def _(act):
            def turned_kept(c):
                tiles = list(range(CT if c < C5 else 0, NT))
                for i in range(0, len(tiles), 4):
                    n, count = turns(c) + i // 4, len(tiles[i:i + 4])
                    act.wait_ge(s_tb, n + 1)
                    dst = (G.qT[:, c, (tiles[i] - CT) * P:] if c < C5 else G.kT[:, c - C5, tiles[i] * P:])[:, 0:count * P]
                    nc.scalar.copy(dst, flat[:, TURN + 512 * (n % 2):TURN + 512 * (n % 2) + count * P]).then_inc(s_tbk, 1)

            for c in range(CH + 1):
                if c < CH:
                    act.wait_ge(s_mm, c + 1)
                    if c >= 2:
                        act.wait_ge(s_cv, c - 1)
                    nc.scalar.copy(raw[:, c % 2, 2:2 + CTX], flat[:, 256:512])
                    nc.scalar.copy(raw[:, c % 2, PAD_AT[1]:PAD_AT[1] + SEQ], flat[:, 512:1536]).then_inc(s_raw, 1)
                    act.wait_ge(s_cv, c + 1)
                    if c:
                        act.wait_ge(s_tt, c)
                    nc.scalar.activation(si[:, 0:CONV], cv[:, 0:CONV], ACT.Silu).then_inc(s_si, 1)
                if 1 <= c:
                    b = c - 1
                    act.wait_ge(s_tt, b + 1)
                    if b < 2 * C5:
                        if b:
                            act.wait_ge(s_ss, b)
                        nc.scalar.activation(sq[:], tok_ps, ACT.Square).then_inc(s_sq, 1)
                        act.wait_ge(s_ss, b + 1)
                        nc.scalar.activation(st[:, 2, :], st[:, 1, :], ACT.Sqrt).then_inc(s_rt, 1)
                    else:
                        nc.scalar.copy(G.vtok[:, :, b - 2 * C5, :], tok_ps).then_inc(s_tk, 1)
                if 2 <= c <= 2 * C5 + 1:
                    turned_kept(c - 2)

        @block.vector
        def _(dve):
            v = nc.vector
            step = Serial(dve, s_dve)
            dve.wait_ge(s_pad, 2)
            for c in range(CH + 1):
                if c < CH:
                    dve.wait_ge(s_raw, c + 1)
                    if c:
                        dve.wait_ge(s_si, c)
                    r = raw[:, c % 2]
                    step(v.tensor_scalar(cv[:, 0:CONV], r[:, 0:CONV], conv_w[:, c, 0:1], None, ALU.mult))
                    for j in range(1, 4):
                        op = v.scalar_tensor_tensor(cv[:, 0:CONV], r[:, j:j + CONV], conv_w[:, c, j:j + 1],
                                                    cv[:, 0:CONV], ALU.mult, ALU.add)
                        step(op) if j < 3 else op.then_inc(s_cv, 1)
                if 1 <= c <= 2 * C5:
                    b = c - 1
                    dve.wait_ge(s_sq, b + 1)
                    step(v.tensor_reduce(st[:, 0, :], sq[:], AX, ALU.add))
                    v.tensor_scalar(st[:, 1, :], st[:, 0, :], EPS, None, ALU.add).then_inc(s_ss, 1)
                    dve.wait_ge(s_rt, b + 1)
                    step(v.reciprocal(st[:, 3, :], st[:, 2, :]))
                    if b < C5:
                        step(v.tensor_scalar(st[:, 3, :], st[:, 3, :], P ** -0.5, None, ALU.mult))
                    if b == C5:
                        dve.wait_ge(s_tb, turns(C5))
                    if 1 <= b < C5:
                        dve.wait_ge(s_tb, turns(b))
                    dst = qtok[:] if b < C5 else G.ktok[:, :, b - C5, :]
                    v.tensor_tensor(dst, tok_ps, st[:, 3, :].unsqueeze(2).broadcast_to([P, NT, P]), ALU.mult).then_inc(s_tk, 1)


def gdn_gates(core, G):
    nc, io, ps, hT = core.nc, core.io, core.ps, core.hT
    s_w, s_ab, s_dve, s_x, s_z, s_be, s_g, s_sum, s_gb, s_e = (core.sem("gdng_" + n) for n in (
        "w", "projected", "dve_steps", "shifted", "exp", "beta", "decay", "summed", "sums_kept", "exps"))
    with ExitStack() as ctx:
        def sb(name, shape):
            return ctx.enter_context(nc.sbuf_tensor(name, shape, F32))
        w = sb("gdn_w_ab", [P, KD, 16])
        x, z, t1, t2, acc, ea = (sb("gdn_sp_" + n, [P, NT, 8]) for n in ("x", "z", "s", "q", "acc", "ea"))
        block = ctx.enter_context(nc.Block())
        ab = ps[:, 0, 0:NT * 16].rearrange("p (t c) -> p t c", c=16)
        sums = ps[:, 1, 0:NT * 8].rearrange("p (t c) -> p t c", c=8)
        total = ps[:, 2, 0:NT * 8].rearrange("p (t c) -> p t c", c=8)

        @block.sync
        def _(sp):
            load_w_in(core, sp, w[:], AB0, 16, s_w)

        @block.tensor
        def _(pe):
            pe.wait_ge(s_w, 16)
            for t in range(NT):
                for k in range(KD):
                    mm = nc.tensor.matmul(ab[:, t, :], hT[:, k, t * P:(t + 1) * P], w[:, k, :],
                                          start=(k == 0), stop=(k == KD - 1))
            mm.then_inc(s_ab, 1)
            pe.wait_ge(s_g, 1)
            for d in range(2):
                nc.tensor.matmul(sums[:, :, 4 * d:4 * d + 4], core.k("tri128")[:, d * P:(d + 1) * P],
                                 G.g[:, :, 4 * d:4 * d + 4], start=True, stop=True)
            nc.tensor.matmul(total, core.k("blk"), G.g[:], start=True, stop=True).then_inc(s_sum, 1)

        @block.scalar
        def _(act):
            act.wait_ge(s_ab, 1)
            nc.scalar.activation(G.beta[:], ab[:, :, 8:16], ACT.Sigmoid).then_inc(s_be, 1)
            act.wait_ge(s_x, 1)
            nc.scalar.activation(z[:], x[:], ACT.Abs).then_inc(s_z, 1)
            act.wait_ge(s_z, 1)
            nc.scalar.activation(z[:], z[:], ACT.Exp, scale=-1.0).then_inc(s_z, 1)
            nc.scalar.activation(ea[:, 0, :], core.r("alog"), ACT.Exp).then_inc(s_z, 1)
            act.wait_ge(s_gb, 2)
            nc.scalar.activation(t1[:], G.gb[:], ACT.Exp).then_inc(s_e, 1)
            nc.scalar.activation(G.el[:], t2[:], ACT.Exp).then_inc(s_e, 1)

        @block.vector
        def _(dve):
            v = nc.vector
            step = Serial(dve, s_dve)
            wide = lambda a: a.unsqueeze(1).broadcast_to([P, NT, 8])
            dve.wait_ge(s_be, 1)
            v.tensor_tensor(x[:], ab[:, :, 0:8], wide(core.r("dtb")), ALU.add).then_inc(s_x, 1)
            dve.wait_ge(s_z, 3)
            softplus_tail(nc, step, z[:], t1[:], t2[:], acc[:])
            step(v.scalar_tensor_tensor(acc[:], x[:], 0.0, acc[:], ALU.max, ALU.add))
            v.scalar_tensor_tensor(G.g[:], acc[:], -1.0, wide(ea[:, 0, :]), ALU.mult, ALU.mult).then_inc(s_g, 1)
            dve.wait_ge(s_sum, 1)
            v.tensor_copy(G.gb[:], sums).then_inc(s_gb, 1)
            dve.wait_ge(s_gb, 1)
            v.tensor_tensor(t2[:], total, G.gb[:], ALU.subtract).then_inc(s_gb, 1)
            dve.wait_ge(s_e, 2)
            dve.wait_ge(s_be, 1)
            step(v.tensor_tensor(G.bg[:], G.beta[:], t1[:], ALU.mult))


def gdn_scan(core, G):
    nc, io, ps, hT = core.nc, core.io, core.ps, core.hT
    oT = core.branch[0]
    LEVELS = 6
    names = dict(rows=1, rows_full=1, grams=1, diffs=1, exp_D=1, exp_DT="latent", exp_rows=1, beta_mask=1, A=1, qkd="latent", A_turned=1,
                 PT=LEVELS - 1, Pk=LEVELS - 1, X=LEVELS, powers=LEVELS, scaled=1, qe="latent", uw=1, w_kept=1, u_kept=1,
                 ws=2, v_new=2, o="2 latent", state=2, state_kept="1 + 2", o_kept="2 latent", strict_beta=1)
    S = [{n: core.sem(f"gdns_{n}{d}") for n in names} for d in range(2)]
    s_dve = core.sem("gdns_dve_steps")
    GROUPS, FILL, STAGES = 3 * KD, 3, 13
    JOBS = 2 * GROUPS
    s_gw, s_gst = [core.sem(f"gate_w{i}") for i in range(2)], [core.sem(f"gate_stored{i}") for i in range(2)]
    s_gmm, s_gcp = core.sem("gate_multiplied"), core.sem("gate_copied")
    with ExitStack() as ctx:
        gw0 = ctx.enter_context(nc.sbuf_tensor("gate_w_sb", [P, KD, P], F32))
        gw = (gw0[:], core.late[:, 1, :].rearrange("p (k n) -> p k n", k=KD))
        gl = core.late[:, 0, :].rearrange("p (b t) -> p b t", b=2)

        def sb(name, shape):
            return [ctx.enter_context(nc.sbuf_tensor(f"gdns_{name}{d}", shape, F32)) for d in range(2)]
        rows, D, DT, bm = (sb(n, [P, GH, GC]) for n in ("rows", "D", "DT", "bm"))
        diff = rows
        QKD, Pw = sb("QKDT", [P, GH, GC]), sb("P", [P, GH, GC])
        XP = sb("XP", [P, GH, 2, GC])
        kbg, ke, vb, u, St, wT, qe = (sb(n, [P, GH, P]) for n in ("kbg", "ke", "vb", "u", "S", "wT", "qe"))
        vn = u
        rows_full = sb("rows_full", [P, 2, GH, GC])
        E = sb("E", [P, 2, GH, GC])
        block = ctx.enter_context(nc.Block())
        ident, ones = core.k("ident"), core.k("ones")
        tri, md, mdt, strict = (core.k(n).rearrange("p (d j) -> p d j", d=2) for n in ("tri", "md", "mdt", "strict"))
        HALF = [slice(0, GC), slice(GC, P)]

        def tile_of(s, d):
            return s if d == 0 else (CT - 1 - s if s < CT else NT + CT - 1 - s)

        def chunk(d, i):
            return i if d == 0 else 1 - i

        def wide(a):
            return a.unsqueeze(1).broadcast_to([P, GH, GC])

        def cols(a, t, d, n):
            return a[:, t, 4 * d:4 * d + 4].unsqueeze(2).broadcast_to([P, GH, n])

        def bank(d, b):
            return ps[:, 4 * d + b, :]

        def heads(a):
            return a.rearrange("p (h j) -> p h j", h=GH)

        def flat(a):
            return a.rearrange("p h e -> p (h e)")

        def right(hd):
            return slice(4 * GC + GC * hd, 5 * GC + GC * hd)

        BOTH = range(2)

        def last_place(job):
            return (KD * job + KD - 1) // FILL

        def jobs_between(a, b):
            return [j for j in range(JOBS) if a <= last_place(j) < b]

        @block.sync
        def _(sp):
            def load(g, slot):
                sp.dma_start(gw[slot], io["w_gates"][g].rearrange("p (k n) -> p k n", k=KD)).then_inc(s_gw[slot], 16)

            def store(i, j):
                sp.wait_ge(s_gcp, 12 * i + j + 1)
                sp.dma_start(core.gate_dram[2 * i + j // 6, j % 2, :, (j // 2) % 3, :], gl[:, j % 2, :])\
                    .then_inc(s_gst[j % 2], 16)
            load(0, 0)
            load(1, 1)
            for i in range(GROUPS // 6):
                for j in range(12):
                    store(i, j)
                    if j % 2 and 6 * i + j // 2 + 2 < GROUPS:
                        load(6 * i + j // 2 + 2, (j // 2) % 2)
            for b in BOTH:
                sp.wait_ge(s_gst[b], 16 * GROUPS)

        @block.tensor
        def _(pe):
            mmul = nc.tensor.matmul

            def fill(s, stage):
                place = STAGES * s + stage
                for n in range(FILL * place, min(FILL * place + FILL, JOBS * KD)):
                    job, k = divmod(n, KD)
                    g, half = divmod(job, 2)
                    if k == 0 and half == 0:
                        pe.wait_ge(s_gw[g % 2], 16 * (g // 2 + 1))
                    if k == 0 and job >= 2:
                        pe.wait_ge(s_gcp, job - 1)
                    mm = mmul(ps[:, 3 + 4 * half, :], gw[g % 2][:, k, :], hT[:, k, CTX + 512 * half:CTX + 512 * half + 512],
                              start=(k == 0), stop=(k == KD - 1))
                    if k == KD - 1:
                        mm.then_inc(s_gmm, 1)

            def grams(s, d):
                q, t = S[d], tile_of(s, d)
                pe.wait_ge(q["rows"], s + 1)
                if s:
                    pe.wait_ge(q["v_new"], 2 * s)
                    pe.wait_ge(q["state_kept"], 1 + 2 * s)
                    pe.wait_ge(q["w_kept"], s)
                if s > CT:
                    pe.wait_ge(q["o_kept"], 2 * (s - CT))
                mmul(bank(d, 0)[:, 0:256], core.k("blk"), flat(rows[d][:]), start=True, stop=True)
                pe.wait_ge(q["rows_full"], s + 1)
                mmul(bank(d, 1), ones, rows_full[d][:].rearrange("p c h j -> p (c h j)"), start=True, stop=True)
                for c in BOTH:
                    t0 = t * P + GC * c
                    for hd in range(GH):
                        k = G.kT[:, hd, t0:t0 + GC]
                        mm = mmul(bank(d, 0)[HALF[c], 256 + GC * hd:256 + GC * hd + GC], k, k, start=True, stop=True)
                        if s >= CT:
                            mm = mmul(bank(d, 2)[HALF[c], GC * hd:GC * hd + GC], k, G.qT[:, hd, t0 - CTX:t0 - CTX + GC],
                                      start=True, stop=True)
                mm.then_inc(q["grams"], 1)

            def turn_A(s, d):
                q = S[d]
                pe.wait_ge(q["A"], s + 1)
                if s >= CT:
                    pe.wait_ge(q["qkd"], s - CT + 1)
                for c in BOTH:
                    for hd in range(GH):
                        mm = mmul(bank(d, 2)[HALF[c], GC * hd:GC * hd + GC], Pw[d][HALF[c], hd, :],
                                  ident[HALF[c], HALF[c]], start=True, stop=True)
                mm.then_inc(q["A_turned"], 1)

            def power(s, d, lev):
                q = S[d]
                if lev:
                    pe.wait_ge(q["Pk"], (LEVELS - 1) * s + lev)
                if lev < LEVELS - 1:
                    pe.wait_ge(q["PT"], (LEVELS - 1) * s + lev + 1)
                if lev:
                    pe.wait_ge(q["X"], LEVELS * s + lev)
                for c in BOTH:
                    for hd in range(GH):
                        at, Pm = slice(GC * hd, GC * hd + GC), Pw[d][HALF[c], hd, :]
                        if lev < LEVELS - 1:
                            mm = mmul(bank(d, 0)[HALF[c], at], XP[d][HALF[c], hd, 1, :], Pm, start=True, stop=True)
                        if lev < LEVELS - 2:
                            mm = mmul(bank(d, 2)[HALF[c], at], Pm, XP[d][HALF[c], hd, 1, :], start=True, stop=True)
                        if lev:
                            mm = mmul(bank(d, 2)[HALF[c], right(hd)], Pm, XP[d][HALF[c], hd, 0, :], start=True, stop=True)
                mm.then_inc(q["powers"], 1)

            def uw(s, d):
                q = S[d]
                pe.wait_ge(q["X"], LEVELS * (s + 1))
                pe.wait_ge(q["scaled"], s + 1)
                pe.wait_ge(q["exp_rows"], s + 1)
                for c in BOTH:
                    for hd in range(GH):
                        X = XP[d][HALF[c], hd, 0, :]
                        mmul(bank(d, 1)[HALF[c], P * hd:P * hd + P], X, vb[d][HALF[c], hd, :], start=True, stop=True)
                        mm = mmul(bank(d, 2 - 2 * c)[:, GC * hd:GC * hd + GC], kbg[d][HALF[c], hd, :], X, start=True, stop=True)
                mm.then_inc(q["uw"], 1)

            def scan_ws(s, d, i):
                q, c = S[d], chunk(d, i)
                if i == 0:
                    pe.wait_ge(q["w_kept"], s + 1)
                pe.wait_ge(q["state_kept"], 1 + 2 * s + i)
                for hd in range(GH):
                    mm = mmul(bank(d, 0)[HALF[c], P * hd:P * hd + P], wT[d][:, hd, HALF[c]], St[d][:, hd, :],
                              start=True, stop=True)
                mm.then_inc(q["ws"], 1)

            def scan_out(s, d, i):
                q, c = S[d], chunk(d, i)
                pe.wait_ge(q["v_new"], 2 * s + i + 1)
                if i == 0:
                    pe.wait_ge(q["u_kept"], s + 1)
                for hd in range(GH):
                    mm = mmul(bank(d, 1)[:, P * hd:P * hd + P], ke[d][HALF[c], hd, :], vn[d][HALF[c], hd, :],
                              start=True, stop=True)
                mm.then_inc(q["state"], 1)
                if s >= CT:
                    if i == 0:
                        pe.wait_ge(q["qe"], s - CT + 1)
                    else:
                        pe.wait_ge(q["o_kept"], 2 * (s - CT) + 1)
                    for hd in range(GH):
                        o = bank(d, 2)[:, right(hd)]
                        mmul(o, St[d][:, hd, :], qe[d][:, hd, HALF[c]], start=True, stop=False)
                        mm = mmul(o, vn[d][HALF[c], hd, :], QKD[d][HALF[c], hd, :], start=False, stop=True)
                    mm.then_inc(q["o"], 1)

            for s in range(NT):
                for d in BOTH:
                    grams(s, d)
                fill(s, 0)
                for d in BOTH:
                    turn_A(s, d)
                fill(s, 1)
                for lev in range(LEVELS):
                    for d in BOTH:
                        power(s, d, lev)
                    fill(s, 2 + lev)
                for d in BOTH:
                    uw(s, d)
                fill(s, 8)
                for i in BOTH:
                    for d in BOTH:
                        scan_ws(s, d, i)
                    fill(s, 9 + 2 * i)
                    for d in BOTH:
                        scan_out(s, d, i)
                    fill(s, 10 + 2 * i)

        @block.vector
        def _(dve):
            v = nc.vector
            step = Serial(dve, s_dve)

            def make_rows(s, d):
                if s:
                    dve.wait_ge(S[d]["grams"], s)
                v.tensor_tensor(rows[d][:], wide(tri[:, d, :]), cols(G.g, tile_of(s, d), d, GC), ALU.mult)                    .then_inc(S[d]["rows"], 1)

            def make_diffs(s, d):
                q, t = S[d], tile_of(s, d)
                dve.wait_ge(q["grams"], s + 1)
                step(v.tensor_tensor(diff[d][:], heads(bank(d, 0)[:, 0:256]), cols(G.gb, t, d, GC), ALU.subtract))
                if s:
                    dve.wait_ge(q["beta_mask"], s)
                v.tensor_tensor(D[d][:], diff[d][:], wide(md[:, d, :]), ALU.max)
                v.tensor_tensor(DT[d][:], diff[d][:], wide(mdt[:, d, :]), ALU.min).then_inc(q["diffs"], 1)

            def make_A(s, d):
                q = S[d]
                dve.wait_ge(q["beta_mask"], s + 1)
                if s:
                    dve.wait_ge(q["powers"], LEVELS * s)
                v.tensor_tensor(Pw[d][:], heads(bank(d, 0)[:, 256:512]), bm[d][:], ALU.mult).then_inc(q["A"], 1)
                if s >= CT:
                    dve.wait_ge(q["exp_DT"], s - CT + 1)
                    v.tensor_tensor(QKD[d][:], heads(bank(d, 2)[:, 0:256]), DT[d][:], ALU.mult).then_inc(q["qkd"], 1)

            def first_X(s, d):
                q = S[d]
                dve.wait_ge(q["PT"], (LEVELS - 1) * s + 1)
                if s:
                    dve.wait_ge(q["uw"], s)
                v.scalar_tensor_tensor(XP[d][:, :, 0, :], XP[d][:, :, 1, :], -1.0, wide(core.k("ident64")),
                                       ALU.mult, ALU.add).then_inc(q["X"], 1)

            def next_X(s, d, lev):
                q = S[d]
                dve.wait_ge(q["powers"], LEVELS * s + lev + 1)
                dve.wait_ge(q["X"], LEVELS * s + lev)
                if lev < LEVELS - 2:
                    dve.wait_ge(q["PT"], (LEVELS - 1) * s + lev + 2)
                v.tensor_tensor(XP[d][:, :, 0, :], XP[d][:, :, 0, :],
                                heads(bank(d, 2)[:, 256:512]), ALU.add).then_inc(q["X"], 1)

            def keep_u(s, d):
                dve.wait_ge(S[d]["uw"], s + 1)
                v.tensor_copy(flat(u[d][:]), bank(d, 1)).then_inc(S[d]["u_kept"], 1)

            def new_v(s, d, i):
                q, h = S[d], HALF[chunk(d, i)]
                dve.wait_ge(q["ws"], 2 * s + i + 1)
                dve.wait_ge(q["u_kept"], s + 1)
                v.tensor_tensor(flat(vn[d][h]), flat(u[d][h]), bank(d, 0)[h, :], ALU.subtract).then_inc(q["v_new"], 1)

            def new_state(s, d, i):
                q, c, t = S[d], chunk(d, i), tile_of(s, d)
                last = GC - 1 if d == 0 else 0
                if s >= CT:
                    dve.wait_ge(q["o"], 2 * (s - CT) + i + 1)
                dve.wait_ge(q["state"], 2 * s + i + 1)
                dve.wait_ge(q["state_kept"], 1 + 2 * s + i)
                for hd in range(GH):
                    op = v.scalar_tensor_tensor(St[d][:, hd, :], St[d][:, hd, :], E[d][:, c, hd, last:last + 1],
                                                bank(d, 1)[:, P * hd:P * hd + P], ALU.mult, ALU.add)
                op.then_inc(q["state_kept"], 1)
                if s >= CT:
                    other = NT + CT - 1 - s
                    if other < s:
                        dve.wait_ge(S[1 - d]["o_kept"], 2 * (other - CT) + 2)
                    x = (t - CT) * P + GC * c
                    v.tensor_tensor(oT[:, :, x:x + GC], oT[:, :, x:x + GC], heads(bank(d, 2)[:, 256:512]),
                                    ALU.add).then_inc(q["o_kept"], 1)

            step(v.memset(oT[:], 0.0))
            for d in BOTH:
                v.memset(St[d][:], 0.0).then_inc(S[d]["state_kept"], 1)
            for s in range(NT):
                for d in BOTH:
                    make_rows(s, d)
                for d in BOTH:
                    make_diffs(s, d)
                for d in BOTH:
                    make_A(s, d)
                for d in BOTH:
                    first_X(s, d)
                for lev in range(1, LEVELS):
                    for d in BOTH:
                        next_X(s, d, lev)
                for d in BOTH:
                    keep_u(s, d)
                for i in BOTH:
                    for d in BOTH:
                        new_v(s, d, i)
                    for d in BOTH:
                        new_state(s, d, i)

        @block.scalar
        def _(act):
            def exps(s, d):
                q = S[d]
                act.wait_ge(q["diffs"], s + 1)
                nc.scalar.activation(D[d][:], D[d][:], ACT.Exp, scale=-1.0).then_inc(q["exp_D"], 1)
                if s >= CT:
                    nc.scalar.activation(DT[d][:], DT[d][:], ACT.Exp).then_inc(q["exp_DT"], 1)
                if s:
                    act.wait_ge(q["state_kept"], 1 + 2 * s)
                if s > CT:
                    act.wait_ge(q["qe"], s - CT)
                nc.scalar.activation(E[d][:].rearrange("p c h j -> p (c h j)"), bank(d, 1), ACT.Exp).then_inc(q["exp_rows"], 1)

            def keep_PT(s, d, lev):
                q = S[d]
                if lev == 0:
                    act.wait_ge(q["A_turned"], s + 1)
                else:
                    act.wait_ge(q["powers"], LEVELS * s + lev)
                    if lev == 1:
                        act.wait_ge(q["X"], LEVELS * s + 1)
                nc.scalar.copy(XP[d][:, :, 1, :], heads(bank(d, 2)[:, 0:256])).then_inc(q["PT"], 1)

            def keep_P(s, d, lev):
                q = S[d]
                act.wait_ge(q["powers"], LEVELS * s + lev)
                nc.scalar.copy(Pw[d][:], heads(bank(d, 0)[:, 0:256])).then_inc(q["Pk"], 1)

            def keep_w(s, d):
                act.wait_ge(S[d]["uw"], s + 1)
                nc.scalar.copy(wT[d][:, :, 0:GC], heads(bank(d, 2)[:, 0:256]))
                nc.scalar.copy(wT[d][:, :, GC:P], heads(bank(d, 0)[:, 0:256])).then_inc(S[d]["w_kept"], 1)

            def copy_gates(s, a, b):
                for j in jobs_between(STAGES * s + a, STAGES * s + b):
                    act.wait_ge(s_gmm, j + 1)
                    if j >= 2:
                        act.wait_ge(s_gst[j % 2], 16 * (j // 2))
                    nc.scalar.copy(gl[:, j % 2, :], ps[:, 3 + 4 * (j % 2), :]).then_inc(s_gcp, 1)

            for s in range(NT):
                for d in BOTH:
                    exps(s, d)
                for d in BOTH:
                    keep_PT(s, d, 0)
                copy_gates(s, 0, 1)
                for lev in range(1, LEVELS):
                    for d in BOTH:
                        keep_P(s, d, lev)
                        if lev < LEVELS - 1:
                            keep_PT(s, d, lev)
                    copy_gates(s, lev, lev + 1)
                for d in BOTH:
                    keep_w(s, d)
                copy_gates(s, LEVELS, STAGES)

        @block.gpsimd
        def _(pool):
            g = nc.gpsimd
            tri_full = core.k("tri128").rearrange("p (d c j) -> p d c j", d=2, c=2)
            for s in range(NT):
                for d in BOTH:
                    q, t = S[d], tile_of(s, d)
                    if s:
                        pool.wait_ge(q["grams"], s)
                    for c in BOTH:
                        op = g.tensor_tensor(rows_full[d][:, c], wide(tri_full[:, d, c]), cols(G.g, t, d, GC), ALU.mult)
                    op.then_inc(q["rows_full"], 1)
                    if s:
                        pool.wait_ge(q["A"], s)
                    g.tensor_tensor(bm[d][:], wide(strict[:, d, :]), cols(G.beta, t, d, GC), ALU.mult)                        .then_inc(q["strict_beta"], 1)
                for d in BOTH:
                    q = S[d]
                    pool.wait_ge(q["exp_D"], s + 1)
                    pool.wait_ge(q["strict_beta"], s + 1)
                    g.tensor_tensor(bm[d][:], bm[d][:], D[d][:], ALU.mult).then_inc(q["beta_mask"], 1)
                for d in BOTH:
                    q, t = S[d], tile_of(s, d)
                    if s:
                        pool.wait_ge(q["uw"], s)
                        pool.wait_ge(q["state"], 2 * s)
                    g.tensor_tensor(vb[d][:], G.vtok[:, t], cols(G.beta, t, d, P), ALU.mult)
                    g.tensor_tensor(kbg[d][:], G.ktok[:, t], cols(G.bg, t, d, P), ALU.mult)
                    g.tensor_tensor(ke[d][:], G.ktok[:, t], cols(G.el, t, d, P), ALU.mult).then_inc(q["scaled"], 1)
                if s < CT:
                    continue
                for d in BOTH:
                    q, t = S[d], tile_of(s, d)
                    pool.wait_ge(q["exp_rows"], s + 1)
                    if s > CT:
                        pool.wait_ge(q["o"], 2 * (s - CT))
                    x = (t - CT) * P
                    g.tensor_tensor(qe[d][:].rearrange("p h (c j) -> p h c j", c=2),
                                    G.qT[:, :, x:x + P].rearrange("p h (c j) -> p h c j", c=2),
                                    E[d][:].rearrange("p c h j -> p h c j"), ALU.mult).then_inc(q["qe"], 1)


def gdn_finish(core):
    nc, io, ps, hT = core.nc, core.io, core.ps, core.hT
    oT = core.branch[0]
    flat = ps[:].rearrange("p b n -> p (b n)")
    s_w, s_sq, s_ss, s_mean, s_rt, s_dve, s_dg, s_rows, s_mm, s_z, s_n, s_y = (core.sem("gdnf_" + n) for n in (
        "w", "squares", "sums", "means", "roots", "dve_steps", "diagonals", "rows", "projected", "silu", "normed", "done"))
    with ExitStack() as ctx:
        def sb(name, shape):
            return ctx.enter_context(nc.sbuf_tensor(name, shape, F32))
        w = sb("gdnf_w_z", [P, KD, W5])
        sq = sb("gdnf_sq", [P, GH, SEQ])
        zs = sb("gdnf_z", [P, GH, SEQ])
        st = sb("gdnf_stats", [P, 3, XT, GH])
        diag = sb("gdnf_diag", [P, 2, GH, P])
        block = ctx.enter_context(nc.Block())
        sums = ps[:, 7, 0:XT * GH].rearrange("p (t h) -> p t h", h=GH)

        @block.sync
        def _(sp):
            load_w_in(core, sp, w[:], Z0, W5, s_w)

        @block.tensor
        def _(pe):
            pe.wait_ge(s_sq, 1)
            for t in range(XT):
                for h in range(GH):
                    mm = nc.tensor.matmul(sums[:, t, h:h + 1], sq[:, h, t * P:(t + 1) * P], core.k("ones")[:, 0:1],
                                          start=True, stop=True)
            mm.then_inc(s_ss, 1)
            pe.wait_ge(s_w, 16)
            for n in range(2 * C5):
                c, half = divmod(n, 2)
                if n >= 3:
                    pe.wait_ge(s_z, n - 2)
                for k in range(KD):
                    mm = nc.tensor.matmul(ps[:, n % 3, :], w[:, k, c * P:(c + 1) * P],
                                          hT[:, k, CTX + 512 * half:CTX + 512 * half + 512], start=(k == 0), stop=(k == KD - 1))
                mm.then_inc(s_mm, 1)
                pe.wait_ge(s_dg, n + 1)
                if n >= 2:
                    pe.wait_ge(s_n, n - 1)
                nc.tensor.matmul(ps[:, 4 + n % 2, :], core.k("ones"), diag[:, n % 2].rearrange("p h t -> p (h t)"),
                                 start=True, stop=True).then_inc(s_rows, 1)

        @block.scalar
        def _(act):
            nc.scalar.activation(sq[:], oT[:], ACT.Square).then_inc(s_sq, 1)
            act.wait_ge(s_mean, 1)
            nc.scalar.activation(st[:, 1], st[:, 0], ACT.Sqrt).then_inc(s_rt, 1)
            for n in range(2 * C5):
                c, half = divmod(n, 2)
                act.wait_ge(s_mm, n + 1)
                nc.scalar.activation(zs[:, c, 512 * half:512 * half + 512], ps[:, n % 3, :], ACT.Silu).then_inc(s_z, 1)

        @block.vector
        def _(dve):
            v = nc.vector
            step = Serial(dve, s_dve)
            dve.wait_ge(s_ss, 1)
            v.tensor_scalar(st[:, 0], sums, 1.0 / P, EPS, ALU.mult, ALU.add).then_inc(s_mean, 1)
            dve.wait_ge(s_rt, 1)
            step(v.reciprocal(st[:, 2], st[:, 1]))
            for t in range(XT):
                if t >= 2:
                    dve.wait_ge(s_rows, t - 1)
                v.tensor_tensor(diag[:, t % 2], core.k("ident").unsqueeze(1).broadcast_to([P, GH, P]),
                                st[:, 2, t, :].unsqueeze(2).broadcast_to([P, GH, P]), ALU.mult).then_inc(s_dg, 1)
                dve.wait_ge(s_rows, t + 1)
                o = oT[:, :, t * P:(t + 1) * P]
                v.scalar_tensor_tensor(o, o, core.c("onorm"), ps[:, 4 + t % 2, :].rearrange("p (h t) -> p h t", h=GH),
                                       ALU.mult, ALU.mult).then_inc(s_n, 1)
            dve.wait_ge(s_n, XT)
            dve.wait_ge(s_z, 2 * C5)
            v.tensor_tensor(oT[:], oT[:], zs[:], ALU.mult).then_inc(s_y, 1)
            dve.wait_ge(s_y, 1)


def gdn(core, dump=None):
    with ExitStack() as ctx:
        G = Gdn(core, ctx)
        core.phase(gdn_project, G)
        core.phase(gdn_gates, G)
        if dump == "gdnp":
            n = NT * GH * P
            return dump_many(core, [(0, G.ktok[:]), (n, G.vtok[:]), (2 * n, G.kT[:]), (3 * n, G.qT[:]),
                                    (3 * n + 4096, G.g[:]), (3 * n + 4176, G.beta[:])])
        core.phase(gdn_scan, G)
    core.phase(gdn_finish)


def dump_many(core, parts):
    nc = core.nc
    s = nc.alloc_semaphore(name="dumped")
    with nc.Block() as block:
        @block.sync
        def _(sp):
            for at, ap in parts:
                n = 1
                for m in ap.shape[1:]:
                    n *= m
                names = "abcd"[:len(ap.shape) - 1]
                src = ap.rearrange(f"p {' '.join(names)} -> p ({' '.join(names)})") if len(names) > 1 else ap
                sp.dma_start(core.io["out"][:, at:at + n], src).then_inc(s, 16)
            sp.wait_ge(s, 16 * len(parts))

def merge(core, mixT):
    nc, io, ps = core.nc, core.io, core.ps
    s_w, s_gl = [core.sem(f"mix_w{i}") for i in range(2)], [core.sem(f"mix_logits{i}") for i in range(2)]
    s_mm, s_sg, s_dve, s_m, s_sum = (core.sem("mix_" + n) for n in ("multiplied", "sigmoids", "dve_steps", "banks_read", "summed"))
    with ExitStack() as ctx:
        def sb(name, shape):
            return ctx.enter_context(nc.sbuf_tensor(name, shape, F32))
        wb = sb("mix_w_branch", [P, 2, 3, C5, P])
        sg = sb("mix_sigmoids", [P, 2, 3, 512])
        block = ctx.enter_context(nc.Block())

        @block.sync
        def _(sp):
            def body(i, first):
                for b in range(2):
                    if not first:
                        sp.wait_ge(s_mm, 4 * (i - 1) + 2 * b + 2)
                    sp.dma_start(wb[:, b].rearrange("p i k n -> p (i k n)"), io["w_mix"][2 * i + b]).then_inc(s_w[b], 16)
                    for half in range(2):
                        if not (first and b == 0):
                            sp.wait_ge(s_sum, 4 * i + 2 * b + half - 1)
                        sp.dma_start(sg[:, half].rearrange("p g t -> p (g t)"),
                                     core.gate_dram[2 * i + b, half].rearrange("p g t -> p (g t)")).then_inc(s_gl[half], 16)
            body(0, True)
            with sp.Fori(1, KD // 2) as i:
                body(i, False)

        @block.tensor
        def _(pe):
            def body(i, first):
                for b in range(2):
                    pe.wait_ge(s_w[b], 16 * i + 16)
                    for half in range(2):
                        if not (first and b == 0):
                            pe.wait_ge(s_m, 4 * i + 2 * b + half - 1)
                        for g in range(3):
                            for k in range(C5):
                                mm = nc.tensor.matmul(ps[:, 3 * half + g, :], wb[:, b, g, k, :],
                                                      core.branch[g][:, k, 512 * half:512 * half + 512],
                                                      start=(k == 0), stop=(k == C5 - 1))
                        mm.then_inc(s_mm, 1)
            body(0, True)
            with pe.Fori(1, KD // 2) as i:
                body(i, False)

        @block.scalar
        def _(act):
            with act.Fori(0, KD // 2) as i:
                for j in range(4):
                    act.wait_ge(s_gl[j % 2], 32 * i + 16 * (j // 2) + 16)
                    nc.scalar.activation(sg[:, j % 2], sg[:, j % 2], ACT.Sigmoid).then_inc(s_sg, 1)

        @block.vector
        def _(dve):
            v = nc.vector
            with dve.Fori(0, KD // 2) as i:
                step = Serial(dve, s_dve, 4 * i)
                for b in range(2):
                    for half in range(2):
                        dve.wait_ge(s_sg, 4 * i + 2 * b + half + 1)
                        dve.wait_ge(s_mm, 4 * i + 2 * b + half + 1)
                        v.tensor_tensor(sg[:, half], sg[:, half], ps[:, 3 * half:3 * half + 3, :], ALU.mult).then_inc(s_m, 1)
                        dve.wait_ge(s_m, 4 * i + 2 * b + half + 1)
                        step(v.tensor_tensor(sg[:, half, 0, :], sg[:, half, 0, :], sg[:, half, 1, :], ALU.add))
                        v.tensor_tensor(mixT[:, bass.ds(2 * i + b, 1), 512 * half:512 * half + 512].rearrange("p a t -> p (a t)"),
                                        sg[:, half, 0, :], sg[:, half, 2, :], ALU.add).then_inc(s_sum, 1)


def mod_rows(core, rows):
    nc, ps = core.nc, core.ps
    s_sc, s_mm, s_cp = (core.sem("rows_" + n) for n in ("scaled", "spread", "kept"))
    with ExitStack() as ctx:
        block = ctx.enter_context(nc.Block())
        late = core.late_mods
        JOBS = [(r, q) for r in (0, 1, 2, 3) for q in range(2)]
        dest = (rows[:, 0, :], rows[:, 2, :], rows[:, 1, :], core.moe_gain)

        @block.vector
        def _(dve):
            nc.vector.scalar_tensor_tensor(late[64:65, :], late[64:65, :], 1.0, core.late[64:65, 0, :],
                                           ALU.add, ALU.mult).then_inc(s_sc, 1)

        @block.tensor
        def _(pe):
            for n, (r, q) in enumerate(JOBS):
                if r == 2 and q == 0:
                    pe.wait_ge(s_sc, 1)
                nc.tensor.matmul(ps[:, n, :], core.k("ones")[32 * r:32 * r + 1, :], late[32 * r:32 * r + 1, 512 * q:512 * q + 512],
                                 start=True, stop=True).then_inc(s_mm, 1)

        @block.scalar
        def _(act):
            for n, (r, q) in enumerate(JOBS):
                act.wait_ge(s_mm, n + 1)
                nc.scalar.copy(dest[r][:, 512 * q:512 * q + 512], ps[:, n, :]).then_inc(s_cp, 1)
            act.wait_ge(s_cp, len(JOBS))


def project_out(core, mixT, rows, affT, h2_dram):
    nc, io, ps = core.nc, core.io, core.ps
    s_w, s_x, s_o, s_h = core.sem("out_w"), [core.sem(f"out_x_in{i}") for i in range(2)], \
        [core.sem(f"out_stored{i}") for i in range(2)], [core.sem(f"h2_stored{i}") for i in range(2)]
    names = ("projected", "x1", "squares", "means", "roots", "dve_steps", "h2", "turned", "turned_kept", "logits", "max",
             "exps", "probs", "probs_turned", "aff_kept", "bank_read")
    s_mm, s_x1, s_sq, s_ss, s_rt, s_dve, s_h2, s_tr, s_tk, s_lg, s_mx, s_ex, s_pr, s_pt, s_ak, s_br = (core.sem("out_" + n) for n in names)
    with ExitStack() as ctx:
        def sb(name, shape):
            return ctx.enter_context(nc.sbuf_tensor(name, shape, F32))
        w = sb("out_w_sb", [P, KD, D])
        wr = sb("router_w", [P, KD, NE])
        x, x1, h2 = core.branch[0][:, 0:2, :], core.branch[0][:, 2:4, :], core.branch[1][:, 0:2, :]
        junk = core.branch[2][:, 0, :]
        h2T = sb("out_h2T", [P, 2, KD, P])
        st, pr = sb("out_stats", [P, 8]), sb("out_probs_sb", [P, 2, NE])
        block = ctx.enter_context(nc.Block())
        xv = io["tokens"].rearrange("(t p) d -> t p d", p=P)
        ov = io["out"].rearrange("(t p) d -> t p d", p=P)
        hv = h2_dram.rearrange("(t p) d -> t p d", p=P)

        @block.sync
        def _(sp):
            sp.dma_start(w[:], io["w_out"].rearrange("(k p) n -> p k n", p=P)).then_inc(s_w, 16)
            sp.dma_start(wr[:], io["w_router"].rearrange("(k p) n -> p k n", p=P)).then_inc(s_w, 16)
            for t in range(XT + 1):
                if t < XT:
                    if t >= 2:
                        sp.wait_ge(s_x1, t - 1)
                    sp.dma_start(x[:, t % 2, :], xv[CT + t]).then_inc(s_x[t % 2], 16)
                if t:
                    sp.wait_ge(s_x1, t)
                    sp.dma_start(ov[t - 1], x1[:, (t - 1) % 2, :]).then_inc(s_o[(t - 1) % 2], 16)
                    sp.wait_ge(s_h2, t)
                    sp.dma_start(hv[t - 1], h2[:, (t - 1) % 2, :]).then_inc(s_h[(t - 1) % 2], 16)
            for b in range(2):
                sp.wait_ge(s_o[b], 16 * XT // 2)
                sp.wait_ge(s_h[b], 16 * XT // 2)

        @block.tensor
        def _(pe):
            def route(t):
                pe.wait_ge(s_h2, t + 1)
                if t:
                    pe.wait_ge(s_tk, t)
                for k in range(KD):
                    tr = nc.tensor.transpose(ps[:, 4 + k // 4, (k % 4) * P:(k % 4 + 1) * P],
                                             h2[:, t % 2, k * P:(k + 1) * P], core.k("ident"))
                tr.then_inc(s_tr, 1)
                if t:
                    turn_probs(t - 1)
                pe.wait_ge(s_tk, t + 1)
                if t:
                    pe.wait_ge(s_ex, t)
                for k in range(KD):
                    mm = nc.tensor.matmul(ps[:, 6, 0:NE], h2T[:, t % 2, k, :], wr[:, k, :], start=(k == 0), stop=(k == KD - 1))
                mm.then_inc(s_lg, 1)

            def turn_probs(t):
                pe.wait_ge(s_pr, t + 1)
                if t:
                    pe.wait_ge(s_ak, t)
                nc.tensor.transpose(ps[0:NE, 7, 0:P], pr[:, t % 2, :], core.k("ident")).then_inc(s_pt, 1)

            pe.wait_ge(s_w, 32)
            for t in range(XT):
                if t >= 2:
                    pe.wait_ge(s_x1, t - 1)
                for n in range(2):
                    for k in range(KD):
                        mm = nc.tensor.matmul(ps[:, 2 * (t % 2) + n, :], mixT[:, k, t * P:(t + 1) * P],
                                              w[:, k, 512 * n:512 * n + 512], start=(k == 0), stop=(k == KD - 1))
                mm.then_inc(s_mm, 1)
                if t:
                    route(t - 1)
            route(XT - 1)
            turn_probs(XT - 1)

        @block.scalar
        def _(act):
            def keep_turned(t):
                act.wait_ge(s_tr, t + 1)
                if t >= 2:
                    act.wait_ge(s_lg, t - 1)
                nc.scalar.copy(h2T[:, t % 2].rearrange("p k t -> p (k t)"),
                               ps[:, 4:6, :].rearrange("p b n -> p (b n)")).then_inc(s_tk, 1)

            def route(t):
                act.wait_ge(s_mx, t + 1)
                if t >= 2:
                    act.wait_ge(s_pt, t - 1)
                nc.scalar.activation(pr[:, t % 2, :], ps[:, 6, 0:NE], ACT.Exp, bias=st[:, 5:6], accum_out=st[:, 6:7]).then_inc(s_ex, 1)

            for t in range(XT):
                if t:
                    keep_turned(t - 1)
                act.wait_ge(s_x1, t + 1)
                if t:
                    act.wait_ge(s_ss, t)
                nc.scalar.activation(junk, x1[:, t % 2, :], ACT.Square, accum_out=st[:, 0:1]).then_inc(s_sq, 1)
                act.wait_ge(s_ss, t + 1)
                nc.scalar.activation(st[:, 2:3], st[:, 1:2], ACT.Sqrt).then_inc(s_rt, 1)
                if t:
                    route(t - 1)
            keep_turned(XT - 1)
            route(XT - 1)

        @block.vector
        def _(dve):
            v = nc.vector
            step = Serial(dve, s_dve)

            def softmax(t):
                dve.wait_ge(s_lg, t + 1)
                v.tensor_reduce(st[:, 5:6], ps[:, 6, 0:NE], AX, ALU.max, negate=True).then_inc(s_mx, 1)
                dve.wait_ge(s_ex, t + 1)
                step(v.reciprocal(st[:, 7:8], st[:, 6:7]))
                v.tensor_scalar(pr[:, t % 2, :], pr[:, t % 2, :], st[:, 7:8], None, ALU.mult).then_inc(s_pr, 1)
                dve.wait_ge(s_pt, t + 1)
                v.tensor_copy(affT[:, t * P:(t + 1) * P], ps[0:NE, 7, 0:P]).then_inc(s_ak, 1)

            for t in range(XT):
                b = t % 2
                dve.wait_ge(s_mm, t + 1)
                dve.wait_ge(s_x[b], 16 * (t // 2 + 1))
                if t >= 2:
                    dve.wait_ge(s_o[b], 16 * (t // 2))
                    dve.wait_ge(s_sq, t - 1)
                step(v.tensor_tensor(x1[:, b, :], ps[:, 2 * b:2 * b + 2, :].rearrange("p b n -> p (b n)"), rows[:, 0, :], ALU.mult))
                v.tensor_tensor(x1[:, b, :], x1[:, b, :], x[:, b, :], ALU.add).then_inc(s_x1, 1)
                dve.wait_ge(s_sq, t + 1)
                v.tensor_scalar(st[:, 1:2], st[:, 0:1], 1.0 / D, EPS, ALU.mult, ALU.add).then_inc(s_ss, 1)
                dve.wait_ge(s_rt, t + 1)
                step(v.reciprocal(st[:, 3:4], st[:, 2:3]))
                if t >= 2:
                    dve.wait_ge(s_h[b], 16 * (t // 2))
                    dve.wait_ge(s_tr, t - 1)
                step(v.scalar_tensor_tensor(h2[:, b, :], x1[:, b, :], st[:, 3:4], rows[:, 1, :], ALU.mult, ALU.mult))
                v.tensor_tensor(h2[:, b, :], h2[:, b, :], rows[:, 2, :], ALU.add).then_inc(s_h2, 1)
                if t:
                    softmax(t - 1)
            softmax(XT - 1)
            dve.wait_ge(s_ak, XT)


def choose(core, affT, idx, gate):
    nc, ps = core.nc, core.ps
    ROUNDS = CAP // 8
    s_dve, s_sel, s_tr, s_end = (core.sem("topk_" + n) for n in ("steps", "chosen", "turned", "kept"))
    with ExitStack() as ctx:
        best = ctx.enter_context(nc.sbuf_tensor("topk_best", [NE, CAP], F32))
        at = ctx.enter_context(nc.sbuf_tensor("topk_at", [NE, CAP], U32))
        at_f = ctx.enter_context(nc.sbuf_tensor("topk_at_f", [NE, CAP], F32))
        block = ctx.enter_context(nc.Block())

        @block.vector
        def _(dve):
            v = nc.vector
            step = Serial(dve, s_dve)
            for i in range(ROUNDS):
                b8, a8 = best[:, 8 * i:8 * i + 8], at[:, 8 * i:8 * i + 8]
                step(v.max(b8, affT[:]))
                step(v.max_index(a8, b8, affT[:]))
                step(v.match_replace(affT[:], b8, affT[:], -1.0))
            v.tensor_copy(at_f[:], at[:]).then_inc(s_sel, 1)
            dve.wait_ge(s_tr, 1)
            v.tensor_copy(idx[:, 0:NE], ps[:, 0, 0:NE])
            v.tensor_copy(gate[:], ps[:, 0, 64:64 + NE]).then_inc(s_end, 1)
            dve.wait_ge(s_end, 1)

        @block.tensor
        def _(pe):
            pe.wait_ge(s_sel, 1)
            nc.tensor.transpose(ps[:, 0, 0:NE], at_f[:], core.k("ident")[0:NE, 0:NE])
            nc.tensor.transpose(ps[:, 0, 64:64 + NE], best[:], core.k("ident")[0:NE, 0:NE]).then_inc(s_tr, 1)


def experts(core, idx, gate, h2_dram):
    nc, io, ps = core.nc, core.io, core.ps
    PIECES_E, RING, FN = 12, 6, EH // 512
    s_w = [core.sem(f"moe_w{i}") for i in range(RING)]
    s_xs, s_xt, s_xk = [core.sem(f"moe_gathered{i}") for i in range(2)], core.sem("moe_x_turned"), core.sem("moe_x_kept")
    s_piece, s_gu, s_si, s_hid, s_ht, s_hk, s_dn, s_y, s_gc = (core.sem("moe_" + n) for n in (
        "piece_used", "gate_up", "silu", "hidden", "hidden_turned", "hidden_kept", "down", "y", "gate_copied"))
    s_add = core.sem("moe_added")
    with ExitStack() as ctx:
        def sb(name, shape, dt=F32):
            return ctx.enter_context(nc.sbuf_tensor(name, shape, dt))
        w = sb("moe_w", [P, RING, 4096])
        gcur = sb("moe_gate", [P, 2])
        xs, xT = sb("moe_x", [P, 2, D]), sb("moe_xT", [P, 2, KD, P])
        si, hid, hT = sb("moe_silu_sb", [P, 2, 512]), sb("moe_hidden_sb", [P, 2, 512]), sb("moe_hiddenT", [P, FN, 4, P])
        y = sb("moe_y_sb", [P, 2, D])
        block = ctx.enter_context(nc.Block())
        pieces = io["w_experts"]

        def piece(j, e):
            return w[:, j % RING, :]

        @block.sync
        def _(sp):
            def load(e, j):
                sp.dma_start(w[:, j % RING, :], pieces[e, j]).then_inc(s_w[j % RING], 16)
            for j in range(RING):
                load(0, j)
            for j in range(RING, PIECES_E):
                sp.wait_ge(s_piece, j - RING + 1)
                load(0, j)
            with sp.Fori(1, NE) as e:
                for j in range(PIECES_E):
                    sp.wait_ge(s_piece, PIECES_E * e + j - RING + 1)
                    load(e, j)

        @block.gpsimd
        def _(pool):
            g = nc.gpsimd

            def gather(e):
                g.indirect_dma_start(xs[:, e % 2, :], None, h2_dram,
                                     bass.IndirectOffsetOnAxis(ap=idx[:, e:e + 1], axis=0)).then_inc(s_xs[e % 2], 16)

            def add(e):
                pool.wait_ge(s_y, e + 1)
                if e:
                    pool.wait_ge(s_add, 16 * e)
                g.indirect_dma_start(io["out"], bass.IndirectOffsetOnAxis(ap=idx[:, e:e + 1], axis=0), y[:, e % 2, :], None,
                                     compute_op=ALU.add).then_inc(s_add, 16)

            gather(0)
            for e in range(NE):
                if e + 1 < NE:
                    if e:
                        pool.wait_ge(s_xt, e)
                    gather(e + 1)
                add(e)
            pool.wait_ge(s_add, 16 * NE)

        @block.tensor
        def _(pe):
            def multiply(out, lhsT, rhs, ks, first, last):
                for n, k in enumerate(ks):
                    mm = nc.tensor.matmul(out, lhsT(k), rhs(k), start=(first and n == 0), stop=(last and n == len(ks) - 1))
                return mm

            def body(i, peeled):
                for b in range(2):
                    e = 2 * i + b
                    pe.wait_ge(s_xs[b], 16 * i + 16)
                    if not (peeled and b == 0):
                        pe.wait_ge(s_hk, FN * e)
                    for k in range(KD):
                        tr = nc.tensor.transpose(ps[:, 4 + k // 4, (k % 4) * P:(k % 4 + 1) * P],
                                                 xs[:, b, k * P:(k + 1) * P], core.k("ident"))
                    tr.then_inc(s_xt, 1)
                    pe.wait_ge(s_xk, e + 1)

                    def turn(n):
                        pe.wait_ge(s_hid, FN * e + n + 1)
                        if n >= 2:
                            pe.wait_ge(s_hk, FN * e + n - 1)
                        for f in range(4):
                            tr = nc.tensor.transpose(ps[:, 4 + n % 2, f * P:(f + 1) * P],
                                                     hid[:, n % 2, f * P:(f + 1) * P], core.k("ident"))
                        tr.then_inc(s_ht, 1)

                    for n in range(FN):
                        if not (peeled and b == 0 and n < 2):
                            pe.wait_ge(s_hid, FN * e + n - 1)
                        for u in range(2):
                            j = 2 * n + u
                            pe.wait_ge(s_w[j % RING], 16 * (2 * e + j // RING + 1))
                            wj = piece(j, e).rearrange("p (k n) -> p k n", k=KD)
                            mm = multiply(ps[:, 2 * (n % 2) + u, :], lambda k: xT[:, b, k, :], lambda k: wj[:, k, :],
                                          range(KD), True, True)
                            mm.then_inc(s_piece, 1)
                        if n:
                            turn(n - 1)
                    for n in range(FN):
                        j = 2 * FN + n
                        pe.wait_ge(s_w[j % RING], 16 * (2 * e + j // RING + 1))
                        if n == FN - 1:
                            turn(n)
                        pe.wait_ge(s_hk, FN * e + n + 1)
                        if n == 0 and not (peeled and b == 0):
                            pe.wait_ge(s_y, e)
                        wj = piece(j, e).rearrange("p (f n) -> p f n", f=4)
                        for half in range(2):
                            mm = multiply(ps[:, 6 + half, :], lambda f: hT[:, n, f, :],
                                          lambda f: wj[:, f, 512 * half:512 * half + 512], range(4), n == 0, n == FN - 1)
                        mm.then_inc(s_piece, 1)
            body(0, True)
            with pe.Fori(1, NE // 2) as i:
                body(i, False)

        @block.scalar
        def _(act):
            def body(i, peeled):
                for b in range(2):
                    e = 2 * i + b
                    act.wait_ge(s_xt, e + 1)
                    nc.scalar.copy(xT[:, b].rearrange("p k t -> p (k t)"), ps[:, 4:6, :].rearrange("p b n -> p (b n)")).then_inc(s_xk, 1)
                    for n in range(FN + 1):
                        if n < FN:
                            act.wait_ge(s_piece, PIECES_E * e + 2 * n + 2)
                            if not (peeled and b == 0 and n < 2):
                                act.wait_ge(s_hid, FN * e + n - 1)
                            nc.scalar.activation(si[:, n % 2, :], ps[:, 2 * (n % 2), :], ACT.Silu).then_inc(s_si, 1)
                        if n:
                            act.wait_ge(s_ht, FN * e + n)
                            if n == 1 and not (peeled and b == 0):
                                act.wait_ge(s_y, e)
                            nc.scalar.copy(hT[:, n - 1].rearrange("p f t -> p (f t)"), ps[:, 4 + (n - 1) % 2, :]).then_inc(s_hk, 1)
            body(0, True)
            with act.Fori(1, NE // 2) as i:
                body(i, False)

        @block.vector
        def _(dve):
            v = nc.vector

            def body(i, peeled):
                for b in range(2):
                    e = 2 * i + b
                    for n in range(FN):
                        dve.wait_ge(s_si, FN * e + n + 1)
                        if not (peeled and b == 0 and n < 2):
                            dve.wait_ge(s_ht, FN * e + n - 1)
                        v.tensor_tensor(hid[:, n % 2, :], si[:, n % 2, :], ps[:, 2 * (n % 2) + 1, :], ALU.mult).then_inc(s_hid, 1)
                    v.tensor_copy(gcur[:, b:b + 1], gate[:, bass.ds(e, 1)]).then_inc(s_gc, 1)
                    dve.wait_ge(s_gc, e + 1)
                    dve.wait_ge(s_piece, PIECES_E * e + PIECES_E)
                    if not peeled:
                        dve.wait_ge(s_add, 16 * (e - 1))
                    v.scalar_tensor_tensor(y[:, b, :], ps[:, 6:8, :].rearrange("p b n -> p (b n)"), gcur[:, b:b + 1],
                                           core.moe_gain[:], ALU.mult, ALU.mult).then_inc(s_y, 1)
            body(0, True)
            with dve.Fori(1, NE // 2) as i:
                body(i, False)


def tail(core, dump):
    nc = core.nc
    h2_dram = nc.dram_tensor("h2_rows", [SEQ, D], F32, kind="Internal").ap()
    with ExitStack() as ctx:
        def sb(name, shape, dt=F32):
            return ctx.enter_context(nc.sbuf_tensor(name, shape, dt))
        mixT = sb("mixT", [P, KD, SEQ])
        core.phase(merge, mixT)
        rows = sb("mod_rows_sb", [P, 3, D])
        core.phase(mod_rows, rows)
        if dump == "mixT":
            return dump_sbuf(core, mixT[:].rearrange("p a b -> p (a b)"))
        core.phase(project_out, mixT, rows, core.affT, h2_dram)
    if dump == "x1":
        return
    return h2_dram


def program(nc, io, upto=99, dump=None):
    with ExitStack() as whole:
        core = Core(nc, io, whole)
        core.late = core.keep("gain_and_affinities", [P, 2, D])
        core.moe_gain, core.affT = core.late[:, 0, :], core.late[0:NE, 1, :]
        core.gate_dram = nc.dram_tensor("gate_logits", [KD, 2, P, 3, 512], F32, kind="Internal").ap()
        idx, gate = core.keep("expert_tokens", [P, NE], U32), core.keep("expert_gates", [P, NE])
        if dump != "moe_only":
            core.phase(adaln)
        with ExitStack() as mixers:
            core.ctx = mixers
            core.hT = core.keep("hT", [P, KD, TOK])
            core.phase(norm1)
            core.branch = [core.keep("branch_gdn", [P, C5, SEQ]), None, None]
            if dump in (None, "gdn", "gdnp", "x1"):
                gdn(core, dump)
            if dump == "gdnp":
                return
            if dump == "gdn":
                return dump_sbuf(core, core.branch[0][:].rearrange("p a b -> p (a b)"))
            core.late_mods = core.keep("late_mods", [P, D])
            core.branch[2] = core.keep("branch_lru", [P, C5, SEQ])
            if dump in (None, "lru", "x1"):
                core.phase(lru)
            if dump == "lru":
                return dump_sbuf(core, core.branch[2][:].rearrange("p a b -> p (a b)"))
            swa(core)
            if dump == "swa":
                return dump_sbuf(core, core.branch[1][:].rearrange("p a b -> p (a b)"))
            h2_dram = tail(core, dump)
            if dump:
                return
        core.phase(choose, core.affT, idx, gate)
        core.phase(experts, idx, gate, h2_dram)


def dump_sbuf(core, ap):
    nc = core.nc
    s = nc.alloc_semaphore(name="dumped")
    with nc.Block() as block:
        @block.sync
        def _(sp):
            sp.dma_start(core.io["out"], ap).then_inc(s, 16)
            sp.wait_ge(s, 16)


def host_arrays(i):
    import numpy as np
    f = np.float32

    def by_chunk(v):
        v = np.asarray(v)
        v = v.reshape(-1, v.shape[-1] // P, P)
        return v.transpose(2, 0, 1).reshape(P, -1)

    g = {k: np.asarray(v) for k, v in i.items()}
    cc = np.stack([by_chunk(g["c"][0]), by_chunk(g["c_ctx"])], axis=2).reshape(P, -1)
    gconv = by_chunk(g["gdn_conv_w"][0]).reshape(P, 4, 12).transpose(0, 2, 1).reshape(P, -1)
    lconv = by_chunk(g["lru_conv_w"][0]).reshape(P, 4, 4).transpose(0, 2, 1).reshape(P, -1)
    col = dict(cc=cc, b_ada=by_chunk(g["b_ada"][0][:2 * D]), n1=by_chunk(g["norm1_g"][0]),
               gconv=gconv, lconv=lconv, lconvb=by_chunk(g["lru_conv_b"][0]), lgb=by_chunk(g["lru_gate_b"][0].reshape(4, W5)),
               lam=by_chunk(g["lru_lambda"][0]), onorm=g["gdn_onorm_g"][0].reshape(P, 1))
    col = np.concatenate([col[n].reshape(P, w) for n, w in PCOL.items()], axis=1)

    slots = [h + 4 * kv for h in range(4) for kv in range(2)]
    qkg = np.concatenate([np.tile(g["swa_qnorm_g"][0], SH), np.tile(g["swa_knorm_g"][0], SKV)])
    row = dict(alog=g["gdn_a_log"][0].reshape(-1), dtb=g["gdn_dt_bias"][0].reshape(-1), qkg=qkg,
               sink=g["swa_sink"][0][slots])
    row = np.concatenate([row[n] for n in PROW])
    row = np.ascontiguousarray(np.broadcast_to(row[None], (P, PROW_N)))

    a = np.arange(P)
    same = (a[:, None] // GC) == (a[None] // GC)
    lo = a[:, None] % GC
    j = np.arange(GC)[None]
    tri128 = np.concatenate([same & (a[:, None] <= a[None]), same & (a[:, None] >= a[None])], 1)
    tri = np.concatenate([lo <= j, lo >= j], 1)
    md = np.concatenate([np.where(lo >= j, 0, BIG), np.where(lo <= j, 0, BIG)], 1)
    mdt = np.concatenate([np.where(lo <= j, 0, -BIG), np.where(lo >= j, 0, -BIG)], 1)
    strict = np.concatenate([lo > j, lo < j], 1)
    s = np.arange(3 * P)[None]
    band = np.abs(s - P - a[:, None]) <= P
    sm = []
    for kind in range(3):
        ok = band & ~((kind == 0) & (s < P)) & ~((kind == 2) & (s >= 2 * P))
        sm.append(np.concatenate([np.where(ok, 0, -BIG), np.zeros((P, CTX))], 1))
    t = np.arange(SEQ)
    inv = 10000.0 ** (-np.arange(0, 32, 2) / 32)
    ang = np.concatenate([(t // 64)[:, None] * inv, (t % 64)[:, None] * inv], 1)
    by_tile = lambda v: v.reshape(XT, P, 32).transpose(1, 0, 2).reshape(P, -1)
    con = dict(ident=np.eye(P), ones=np.ones((P, P)), ident64=lo == j, blk=same, tri128=tri128, tri=tri, md=md, mdt=mdt,
               strict=strict, smask=np.concatenate(sm, 1), cos=by_tile(np.cos(ang)), sin=by_tile(np.sin(ang)))
    swa_con = np.concatenate([np.asarray(con[n], f) for n in PSWA], axis=1)
    con = np.concatenate([np.asarray(con[n], f) for n in PCON], axis=1)

    gw = g["lru_gate_w"][0]
    lgw = np.zeros((P, 2, 2, C5, P), f)
    for b in range(8):
        o = 64 * (b % 2)
        lgw[o:o + 64, :, :, b // 2, o:o + 64] = gw[:, :, b].transpose(2, 0, 1, 3)
    w_in = g["w_in"][0]
    w_gates = w_in[:, G0:].reshape(KD, P, 3, KD, P).transpose(3, 2, 1, 0, 4).reshape(3 * KD, P, -1)
    wb = g["w_branch"][0].copy()
    wb[1] = wb[1].reshape(2, 4, HD, D).transpose(1, 0, 2, 3).reshape(W5, D)
    w_mix = wb.reshape(3, C5, P, KD, P).transpose(3, 2, 0, 1, 4).reshape(KD, P, -1)
    wg, wu, wd = g["w_exp_gate"][0], g["w_exp_up"][0], g["w_exp_down"][0]
    pieces = np.empty((NE, 12, P, 4096), f)
    for q in range(4):
        for u, a in enumerate((wg, wu)):
            pieces[:, 2 * q + u] = a[:, :, 512 * q:512 * q + 512].reshape(NE, KD, P, 512).transpose(0, 2, 1, 3).reshape(NE, P, -1)
        pieces[:, 8 + q] = wd[:, 512 * q:512 * q + 512].reshape(NE, 4, P, D).transpose(0, 2, 1, 3).reshape(NE, P, -1)
    return {
        "tokens": np.concatenate([g["ctx"][0], g["x"][0]], axis=0), "col": col, "row": row, "con": con, "swa_con": swa_con,
        "b_late": g["b_ada"][0][2 * D:].reshape(4, D), "n2_row": g["norm2_g"][0].reshape(1, D), "w_ada": g["w_ada"][0], "w_in": w_in, "lgw": lgw.reshape(P, -1), "w_gates": w_gates, "w_mix": w_mix,
        "w_out": g["w_out"][0], "w_router": g["w_router"][0], "w_experts": pieces,
    }


def kernel(**inputs):
    import numpy as np
    import concourse.bacc as bacc
    from concourse.bass_utils import run_bass_kernel_spmd as run

    nc = bacc.Bacc("TRN2", target_bir_lowering=False, num_devices=1)
    arrays = {n: np.ascontiguousarray(a) for n, a in host_arrays(inputs).items()}
    io = {n: nc.dram_tensor(n, a.shape, F32, kind="ExternalInput").ap() for n, a in arrays.items()}
    io["out"] = nc.dram_tensor("out", [SEQ, D], F32, kind="ExternalOutput").ap()
    program(nc, io)
    r = run(nc, [arrays], core_ids=[0])
    return np.asarray(r.results[0]["out"]).reshape(1, SEQ, D)
```

```python
from contextlib import ExitStack

import concourse.bass as bass
from concourse import mybir
from concourse.alu_op_type import AluOpType as ALU

ACT = mybir.ActivationFunctionType
F32 = mybir.dt.float32
U32 = mybir.dt.uint32
F32R = mybir.dt.float32r
AX = mybir.AxisListType.X

P = 128
D = 1024
KD = D // P
SEQ, CTX = 1024, 256
CT, XT = CTX // P, SEQ // P
NT = CT + XT
TOK = CTX + SEQ
EPS = 1e-6
BIG = 1e30

GH, GC = 4, 64
W5 = 512
C5 = W5 // P
SH, SKV, HD = 8, 2, 64
NQK = SH + SKV
KEYS = 3 * P + CTX
NE, EH = 16, 2048
CAP = 2 * SEQ // NE

Q0, Z0, AB0, S0, XR0, Y0, G0 = 0, 1536, 2048, 2064, 2832, 3344, 3856

PCOL = dict(cc=KD * 2, b_ada=2 * KD, n1=KD, gconv=48, lconv=16, lconvb=4, lgb=16, lam=8, onorm=1)
PROW = dict(alog=8, dtb=8, qkg=NQK * HD, sink=SH)
PCON = dict(ident=P, ones=P, ident64=GC, blk=P, tri128=2 * P, md=2 * GC, mdt=2 * GC, strict=2 * GC)
PSWA = dict(smask=3 * KEYS, cos=XT * 32, sin=XT * 32)


def offsets(widths):
    at, out = 0, {}
    for name, w in widths.items():
        out[name] = (at, at + w)
        at += w
    return out, at


PCOL_AT, PCOL_N = offsets(PCOL)
PROW_AT, PROW_N = offsets(PROW)
PCON_AT, PCON_N = offsets(PCON)
PSWA_AT, PSWA_N = offsets(PSWA)


class Core:

    def __init__(self, nc, io, ctx):
        self.nc, self.io, self.ctx = nc, io, ctx
        self.ps = ctx.enter_context(nc.psum_tensor("ps", [P, 8, 512], F32))
        self.col = self.keep("col_params", [P, PCOL_N])
        self.row = self.keep("row_params", [P, PROW_N])
        self.con = self.keep("tables", [P, PCON_N])
        self.mods = self.keep("mods", [P, 2 * KD, 2])
        self.silu_c = self.keep("silu_c", [P, KD, 2])
        self.scale1 = self.keep("scale1", [P, KD, 2])
        self.hT = None

    def keep(self, name, shape, dt=F32):
        return self.ctx.enter_context(self.nc.sbuf_tensor(name, shape, dt))

    def sem(self, name):
        self.sems.append(self.nc.alloc_semaphore(name=name))
        return self.sems[-1]

    def phase(self, build, *args):
        self.sems = []
        build(self, *args)
        self.nc.clear_and_free_semaphores(self.sems)
        self.nc.all_engine_barrier()

    def c(self, name):
        a, b = PCOL_AT[name]
        return self.col[:, a:b]

    def r(self, name):
        a, b = PROW_AT[name]
        return self.row[:, a:b]

    def k(self, name):
        a, b = PCON_AT[name]
        return self.con[:, a:b]

    def a(self, name):
        a, b = PSWA_AT[name]
        return self.swa_con[:, a:b]


def adaln(core):
    nc, io, ps = core.nc, core.io, core.ps
    NG, GW = 2 * D // 512, 512
    s_par, s_tab, s_ld = core.sem("ada_params"), core.sem("ada_tables"), [core.sem(f"ada_w{i}") for i in range(NG)]
    s_silu, s_mm, s_row, s_col, s_ev, s_sc = (core.sem("ada_" + n) for n in (
        "silu", "multiplied", "rows_kept", "columns", "biased", "scale"))
    w_view = io["w_ada"].rearrange("(k p) n -> p k n", p=P)
    with ExitStack() as ctx:
        w = ctx.enter_context(nc.sbuf_tensor("w_ada_sb", [P, NG, KD, GW], F32))
        rows = ctx.enter_context(nc.sbuf_tensor("ada_rows", [2, NG, GW], F32))
        cc = core.c("cc").rearrange("p (k s) -> p k s", s=2)
        block = ctx.enter_context(nc.Block())

        @block.sync
        def _(sp):
            sp.dma_start(core.col[:], io["col"]).then_inc(s_par, 16)
            for g in range(NG):
                sp.dma_start(w[:, g], w_view[:, :, g * GW:(g + 1) * GW]).then_inc(s_ld[g], 16)
            sp.dma_start(core.con[:], io["con"]).then_inc(s_tab, 16)
            sp.dma_start(core.row[:], io["row"]).then_inc(s_tab, 16)
            sp.wait_ge(s_tab, 32)

        @block.scalar
        def _(act):
            act.wait_ge(s_par, 16)
            nc.scalar.activation(core.silu_c[:], cc, ACT.Silu).then_inc(s_silu, 1)
            for g in range(NG):
                act.wait_ge(s_mm, g + 1)
                nc.scalar.copy(rows[:, g, :], ps[0:2, g, :]).then_inc(s_row, 1)

        @block.tensor
        def _(pe):
            def columns(g):
                pe.wait_ge(s_row, g + 1)
                for n in range(GW // P):
                    at = 2 * (g * GW // P + n)
                    tr = nc.tensor.transpose(ps[:, NG, at:at + 2], rows[:, g, n * P:(n + 1) * P], core.k("ident")[0:2, 0:2])
                return tr
            pe.wait_ge(s_silu, 1)
            for g in range(NG):
                if g == 1:
                    pe.wait_ge(s_tab, 32)
                pe.wait_ge(s_ld[g], 16)
                for k in range(KD):
                    mm = nc.tensor.matmul(ps[0:2, g, :], core.silu_c[:, k, :], w[:, g, k, :],
                                          start=(k == 0), stop=(k == KD - 1))
                mm.then_inc(s_mm, 1)
                if g:
                    columns(g - 1)
            columns(NG - 1).then_inc(s_col, 1)

        @block.vector
        def _(dve):
            dve.wait_ge(s_col, 1)
            nc.vector.tensor_tensor(
                core.mods[:], ps[:, NG, 0:4 * KD].rearrange("p (n s) -> p n s", s=2),
                core.c("b_ada").unsqueeze(2).broadcast_to([P, 2 * KD, 2]), ALU.add).then_inc(s_ev, 1)
            dve.wait_ge(s_ev, 1)
            nc.vector.scalar_tensor_tensor(
                core.scale1[:], core.mods[:, KD:2 * KD, :], 1.0,
                core.c("n1").unsqueeze(2).broadcast_to([P, KD, 2]), ALU.add, ALU.mult).then_inc(s_sc, 1)
            dve.wait_ge(s_sc, 1)


def norm1(core):
    nc, io, ps = core.nc, core.io, core.ps
    hT = core.hT
    s_ld = [core.sem(f"n1_x{i}") for i in range(2)]
    s_sq, s_v, s_rt, s_r, s_xn, s_tr = (core.sem("n1_" + n) for n in ("square", "mean", "root", "recip", "scaled", "transposed"))
    s_ea, s_ed = core.sem("n1_evac_act"), core.sem("n1_evac_dve")
    x_view = io["tokens"].rearrange("(t p) d -> t p d", p=P)
    H = KD // 2
    with ExitStack() as ctx:
        x = ctx.enter_context(nc.sbuf_tensor("x_tile", [P, 2, D], F32))
        xn = ctx.enter_context(nc.sbuf_tensor("x_scaled", [P, 2, D], F32))
        junk = ctx.enter_context(nc.sbuf_tensor("squares", [P, D], F32))
        st = ctx.enter_context(nc.sbuf_tensor("stats", [P, 2, 4], F32))
        ident = core.k("ident")
        block = ctx.enter_context(nc.Block())
        shift1 = core.mods

        def rounds(eng, body):
            body(0, 0, True)
            with eng.Fori(1, NT // 2) as i:
                body(i, 1, False)

        @block.sync
        def _(sp):
            def body(i, _, peeled):
                for j in range(2):
                    if not peeled:
                        sp.wait_ge(s_xn, 2 * (i - 1) + j + 1)
                    sp.dma_start(x[:, j, :], x_view[2 * i + j]).then_inc(s_ld[j], 16)
            rounds(sp, body)

        @block.scalar
        def _(act):
            def body(i, x_tiles, peeled):
                for j in range(2):
                    t = 2 * i + j
                    act.wait_ge(s_ld[j], 16 * i + 16)
                    if not (peeled and j == 0):
                        act.wait_ge(s_rt, t)
                    nc.scalar.activation(junk[:], x[:, j, :], ACT.Square, accum_out=st[:, j, 0:1]).then_inc(s_sq, 1)
                    act.wait_ge(s_v, t + 1)
                    nc.scalar.activation(st[:, j, 2:3], st[:, j, 1:2], ACT.Sqrt).then_inc(s_rt, 1)
                for j in range(2):
                    t = 2 * i + j
                    act.wait_ge(s_tr, t + 1)
                    for k in range(H):
                        ev = nc.scalar.activation(
                            hT[:, k, bass.ts(t, P)], ps[:, 2 * j, k * P:(k + 1) * P], ACT.Identity,
                            scale=core.scale1[:, k, 1 - x_tiles:2 - x_tiles],
                            bias=shift1[:, k, 1 - x_tiles:2 - x_tiles])
                    ev.then_inc(s_ea, 1)
            rounds(act, body)

        @block.vector
        def _(dve):
            def body(i, x_tiles, peeled):
                for j in range(2):
                    t = 2 * i + j
                    dve.wait_ge(s_sq, t + 1)
                    nc.vector.tensor_scalar(st[:, j, 1:2], st[:, j, 0:1], 1.0 / D, EPS, ALU.mult, ALU.add).then_inc(s_v, 1)
                    dve.wait_ge(s_rt, t + 1)
                    nc.vector.reciprocal(st[:, j, 3:4], st[:, j, 2:3]).then_inc(s_r, 1)
                    dve.wait_ge(s_r, t + 1)
                    if not peeled:
                        dve.wait_ge(s_tr, 2 * (i - 1) + j + 1)
                    nc.vector.tensor_scalar(xn[:, j, :], x[:, j, :], st[:, j, 3:4], None, ALU.mult).then_inc(s_xn, 1)
                for j in range(2):
                    t = 2 * i + j
                    dve.wait_ge(s_tr, t + 1)
                    for k in range(H, KD):
                        ev = nc.vector.tensor_scalar(
                            hT[:, k, bass.ts(t, P)], ps[:, 2 * j + 1, (k - H) * P:(k - H + 1) * P],
                            core.scale1[:, k, 1 - x_tiles:2 - x_tiles], shift1[:, k, 1 - x_tiles:2 - x_tiles],
                            ALU.mult, ALU.add)
                    ev.then_inc(s_ed, 1)
            rounds(dve, body)

        @block.tensor
        def _(pe):
            def body(i, _, peeled):
                for j in range(2):
                    t = 2 * i + j
                    pe.wait_ge(s_xn, t + 1)
                    if not peeled:
                        pe.wait_ge(s_ea, 2 * (i - 1) + j + 1)
                        pe.wait_ge(s_ed, 2 * (i - 1) + j + 1)
                    for k in range(KD):
                        tr = nc.tensor.transpose(ps[:, 2 * j + k // H, (k % H) * P:(k % H + 1) * P],
                                                 xn[:, j, k * P:(k + 1) * P], ident)
                    tr.then_inc(s_tr, 1)
            rounds(pe, body)


class Serial:

    def __init__(self, eng, sem, base=0):
        self.eng, self.sem, self.base, self.n = eng, sem, base, 0

    def __call__(self, ins):
        ins.then_inc(self.sem, 1)
        self.n += 1
        self.eng.wait_ge(self.sem, self.base + self.n)


LOG_TERMS = 9


def softplus_tail(nc, step, z, s, q, acc):
    v = nc.vector
    step(v.tensor_scalar(q, z, 2.0, None, ALU.add))
    step(v.reciprocal(s, q))
    step(v.tensor_tensor(s, s, z, ALU.mult))
    step(v.tensor_tensor(q, s, s, ALU.mult))
    step(v.tensor_scalar(acc, q, 1.0 / (2 * LOG_TERMS + 1), 1.0 / (2 * LOG_TERMS - 1), ALU.mult, ALU.add))
    for n in range(LOG_TERMS - 2, -1, -1):
        step(v.tensor_tensor(acc, acc, q, ALU.mult))
        step(v.tensor_scalar(acc, acc, 1.0 / (2 * n + 1), None, ALU.add))
    step(v.scalar_tensor_tensor(acc, acc, 2.0, s, ALU.mult, ALU.mult))


def load_w_in(core, sp, dst, col, width, sem):
    sp.dma_start(dst, core.io["w_in"].rearrange("(k p) n -> p k n", p=P)[:, :, col:col + width]).then_inc(sem, 16)


PIECES = ((0, CTX, 2 * CTX - CTX), (CTX, 512, 512), (CTX + 512, 512, 1024))
PADDED = 2 + CTX + 1 + 2 + SEQ + 1
PAD_AT = (2, 2 + CTX + 1 + 2)
CONV = PADDED - 3


def lru(core):
    nc, io, ps, hT = core.nc, core.io, core.ps, core.hT
    gy = core.branch[2]
    s_w = [core.sem(f"lru_w{i}") for i in range(2)]
    s_bias, s_lw, s_lm, s_lb = core.sem("late_biases"), [core.sem(f"late_w{i}") for i in range(2)], core.sem("late_multiplied"), core.sem("late_biased")
    s_lgw, s_pad = core.sem("lru_gate_weights"), core.sem("lru_padding")
    s_mm, s_xr, s_gy = core.sem("lru_projected"), core.sem("lru_xr_kept"), core.sem("lru_gelu_kept")
    s_pre, s_dve, s_u = core.sem("lru_gates_multiplied"), core.sem("lru_dve_steps"), core.sem("lru_conv_done")
    s_ez, s_par = core.sem("lru_exp_lambda"), core.sem("lru_decay_rate")
    s_ri, s_et, s_sq, s_iu, s_unit = (core.sem("lru_" + n) for n in
                                      ("sigmoids", "exp_tanh", "roots", "input_gated", "unit_done"))
    flat = ps[:].rearrange("p b n -> p (b n)")
    with ExitStack() as ctx:
        def sb(name, shape):
            return ctx.enter_context(nc.sbuf_tensor(name, shape, F32))
        w = sb("lru_w_in", [P, 2, KD, W5])
        wl = w[:, 0]
        lgw = sb("lru_gw", [P, 2, 2, C5, P])
        xr = sb("lru_xr", [P, C5, PADDED])
        u = sb("lru_u", [P, 2, CONV])
        par = sb("lru_par", [P, 6, 8])
        R, I, T, S = (sb("lru_" + n, [P, 2, TOK]) for n in "RITS")
        iu = sb("lru_iu", [P, TOK])
        block = ctx.enter_context(nc.Block())
        UNITS = [(c, d) for c in range(C5) for d in range(2)]
        lgb = core.c("lgb").rearrange("p (d g c) -> p d g c", d=2, g=2)
        conv_w = core.c("lconv").rearrange("p (c j) -> p c j", j=4)
        NP8 = 2 * C5

        def u_of(c):
            return (u[:, c % 2, 0:CTX], u[:, c % 2, CTX + 3:CTX + 3 + SEQ])

        @block.sync
        def _(sp):
            load_w_in(core, sp, w[:, 0], XR0, W5, s_w[0])
            load_w_in(core, sp, w[:, 1], Y0, W5, s_w[1])
            sp.dma_start(lgw[:].rearrange("p d g c n -> p (d g c n)"), io["lgw"]).then_inc(s_lgw, 16)
            for r in range(4):
                sp.dma_start(core.late_mods[32 * r:32 * r + 1, :], io["b_late"][r:r + 1, :]).then_inc(s_bias, 16)
            sp.dma_start(core.late[64:65, 0, :], io["n2_row"]).then_inc(s_bias, 16)
            sp.wait_ge(s_mm, C5)
            for n in range(2 * 4 * D // 512):
                g, half = divmod(n, 2)
                if n >= 2:
                    sp.wait_ge(s_lm, n - 1)
                sp.dma_start(wl[:, 4 * half:4 * half + 4], io["w_ada"].rearrange("(k p) n -> p k n", p=P)
                             [:, 4 * half:4 * half + 4, 2 * D + 512 * g:2 * D + 512 * g + 512]).then_inc(s_lw[half], 16)

        @block.gpsimd
        def _(pool):
            nc.gpsimd.memset(xr[:, :, 0:2], 0.0)
            nc.gpsimd.memset(xr[:, :, 2 + CTX:5 + CTX], 0.0)
            nc.gpsimd.memset(xr[:, :, PADDED - 1:PADDED], 0.0).then_inc(s_pad, 1)
            for n, (c, d) in enumerate(UNITS):
                pool.wait_ge(s_ri, n + 1)
                pool.wait_ge(s_u, c + 1)
                if n:
                    pool.wait_ge(s_unit, n)
                for a, (at, num, _) in zip(u_of(c), ((0, CTX, 0), (CTX, SEQ, 0))):
                    op = nc.gpsimd.tensor_tensor(iu[:, at:at + num], I[:, d, at:at + num], a, ALU.mult)
                op.then_inc(s_iu, 1)

        @block.tensor
        def _(pe):
            for c in range(C5):
                if c == 0:
                    pe.wait_ge(s_w[0], 16)
                if c >= 2:
                    pe.wait_ge(s_xr, c - 1)
                for t0, n, at in PIECES:
                    for k in range(KD):
                        mm = nc.tensor.matmul(flat[:, (c % 2) * 1536 + at:(c % 2) * 1536 + at + n],
                                              w[:, 0, k, c * P:(c + 1) * P], hT[:, k, t0:t0 + n],
                                              start=(k == 0), stop=(k == KD - 1))
                mm.then_inc(s_mm, 1)
            def project_y(c):
                if c == 0:
                    pe.wait_ge(s_w[1], 16)
                else:
                    pe.wait_ge(s_gy, c)
                for t0, n, at in PIECES[1:]:
                    for k in range(KD):
                        mm = nc.tensor.matmul(flat[:, 2560 + at:2560 + at + n], w[:, 1, k, c * P:(c + 1) * P],
                                              hT[:, k, t0:t0 + n], start=(k == 0), stop=(k == KD - 1))
                mm.then_inc(s_mm, 1)

            def late_mods(g):
                r, q = divmod(g, 2)
                if q == 0:
                    pe.wait_ge(s_gy, r + 1)
                for k in range(KD):
                    if k % 4 == 0:
                        pe.wait_ge(s_lw[k // 4], 16 * g + 16)
                    mm = nc.tensor.matmul(ps[32 * r:32 * r + 1, 6 + q, :], core.silu_c[:, k, 0:1], wl[:, k, :],
                                          start=(k == 0), stop=(k == KD - 1))
                    if k % 4 == 3:
                        mm.then_inc(s_lm, 1)

            project_y(0)
            pe.wait_ge(s_lgw, 16)
            pe.wait_ge(s_xr, C5)
            for n, (c, d) in enumerate(UNITS):
                pe.wait_ge(s_u, c + 1)
                if n:
                    pe.wait_ge(s_ri, n)
                for g in range(2):
                    for a, (t0, num, at) in ((u_of(c)[0], PIECES[0]), (u_of(c)[1][:, 0:512], PIECES[1]),
                                             (u_of(c)[1][:, 512:SEQ], PIECES[2])):
                        mm = nc.tensor.matmul(flat[:, g * 1536 + at:g * 1536 + at + num], lgw[:, d, g, c, :], a,
                                              start=True, stop=True)
                mm.then_inc(s_pre, 1)
                if d:
                    late_mods(2 * c)
                    late_mods(2 * c + 1)
                if d and c + 1 < C5:
                    pe.wait_ge(s_lb, 2 * c + 2)
                    project_y(c + 1)

        @block.scalar
        def _(act):
            def gelu(c):
                act.wait_ge(s_mm, C5 + c + 1)
                nc.scalar.activation(gy[:, c, :], flat[:, 3072:4096], ACT.Gelu_apprx_tanh).then_inc(s_gy, 1)

            nc.scalar.activation(par[:, 0, :], core.c("lam"), ACT.Abs).then_inc(s_ez, 1)
            act.wait_ge(s_ez, 1)
            nc.scalar.activation(par[:, 1, :], par[:, 0, :], ACT.Exp, scale=-1.0).then_inc(s_ez, 1)
            for c in range(C5):
                if c == 0:
                    gelu(0)
                for d in range(2):
                    n = 2 * c + d
                    act.wait_ge(s_pre, n + 1)
                    if c and d == 0:
                        act.wait_ge(s_unit, n)
                    for g, dst in ((0, R), (1, I)):
                        a = nc.scalar.activation(dst[:, d, :], flat[:, g * 1536 + 256:g * 1536 + 1536], ACT.Sigmoid,
                                                 bias=lgb[:, d, g, c:c + 1])
                    a.then_inc(s_ri, 1)
                act.wait_ge(s_ri, 2 * c + 2)
                act.wait_ge(s_par, 1)
                for d in range(2):
                    j = d * C5 + c
                    nc.scalar.activation(T[:, d, :], R[:, d, :], ACT.Tanh, scale=par[:, 4, j:j + 1])
                for d in range(2):
                    j = d * C5 + c
                    nc.scalar.activation(R[:, d, :], R[:, d, :], ACT.Exp, scale=par[:, 5, j:j + 1]).then_inc(s_et, 1)
                act.wait_ge(s_et, 2 * c + 2)
                for d in range(2):
                    nc.scalar.activation(S[:, d, :], T[:, d, :], ACT.Sqrt).then_inc(s_sq, 1)
                if c + 1 < C5:
                    gelu(c + 1)

        @block.vector
        def _(dve):
            step = Serial(dve, s_dve)
            v = nc.vector
            dve.wait_ge(s_ez, 2)
            softplus_tail(nc, step, par[:, 1, :], par[:, 2, :], par[:, 3, :], par[:, 0, :])
            step(v.tensor_scalar(par[:, 1, :], core.c("lam"), -1.0, 0.0, ALU.mult, ALU.max))
            step(v.tensor_tensor(par[:, 0, :], par[:, 0, :], par[:, 1, :], ALU.add))
            v.tensor_scalar(par[:, 4, :], par[:, 0, :], 4.0, None, ALU.mult)
            v.tensor_scalar(par[:, 5, :], par[:, 0, :], -8.0, None, ALU.mult).then_inc(s_par, 1)
            dve.wait_ge(s_pad, 1)
            for c in range(C5):
                dve.wait_ge(s_mm, c + 1)
                o = (c % 2) * 1536
                v.tensor_copy(xr[:, c, 2:2 + CTX], flat[:, o + 256:o + 512])
                v.tensor_copy(xr[:, c, PAD_AT[1]:PAD_AT[1] + SEQ], flat[:, o + 512:o + 1536]).then_inc(s_xr, 1)
            dve.wait_ge(s_xr, C5)

            def convolve(c):
                if c >= 2:
                    dve.wait_ge(s_pre, 2 * c - 2)
                    dve.wait_ge(s_iu, 2 * c - 2)
                uc = u[:, c % 2]
                step(v.tensor_scalar(uc, xr[:, c, 0:CONV], conv_w[:, c, 0:1], core.c("lconvb")[:, c:c + 1],
                                     ALU.mult, ALU.add))
                for j in range(1, 4):
                    op = v.scalar_tensor_tensor(uc, xr[:, c, j:j + CONV], conv_w[:, c, j:j + 1], uc, ALU.mult, ALU.add)
                    step(op) if j < 3 else op.then_inc(s_u, 1)

            convolve(0)
            for c in range(C5):
                if c + 1 < C5:
                    convolve(c + 1)
                dve.wait_ge(s_bias, 80)
                row = slice(32 * c, 32 * c + 1)
                for q in range(2):
                    cols = slice(512 * q, 512 * q + 512)
                    dve.wait_ge(s_lm, 2 * (2 * c + q) + 2)
                    v.tensor_tensor(core.late_mods[row, cols], core.late_mods[row, cols], ps[row, 6 + q, :],
                                    ALU.add).then_inc(s_lb, 1)
                for d in range(2):
                    n = 2 * c + d
                    r, t, s = R[:, d, :], T[:, d, :], S[:, d, :]
                    dve.wait_ge(s_sq, n + 1)
                    step(v.scalar_tensor_tensor(t, r, 1.0, t, ALU.add, ALU.mult))
                    step(v.tensor_scalar(t, t, -1.0, 1.0, ALU.mult, ALU.add))
                    step(v.scalar_tensor_tensor(s, t, 1.0, s, ALU.add, ALU.mult))
                    dve.wait_ge(s_iu, n + 1)
                    step(v.tensor_tensor(s, s, iu[:], ALU.mult))
                    if d == 0:
                        v.tensor_tensor_scan(r, t, s, 0.0, ALU.mult, ALU.add).then_inc(s_unit, 1)
                    else:
                        rc, tc, sc = r[:, 0:CTX], t[:, 0:CTX], s[:, 0:CTX]
                        rx, tx, sx = r[:, CTX:], t[:, CTX:], s[:, CTX:]
                        step(v.tensor_tensor_scan(rc[:, ::-1], tc[:, ::-1], sc[:, ::-1], 0.0, ALU.mult, ALU.add))
                        step(v.tensor_tensor_scan(rx[:, ::-1], tx[:, ::-1], sx[:, ::-1], r[:, 0:1], ALU.mult, ALU.add))
                        step(v.tensor_tensor(S[:, 0, CTX:], R[:, 0, CTX:], R[:, 1, CTX:], ALU.add))
                        dve.wait_ge(s_gy, c + 1)
                        v.tensor_tensor(gy[:, c, :], gy[:, c, :], S[:, 0, CTX:], ALU.mult).then_inc(s_unit, 1)


PADK = P + SEQ + P
KEYCOLS = PADK + CTX


def swa_project(core, qT, kT, V):
    nc, io, ps, hT = core.nc, core.io, core.ps, core.hT
    flat = ps[:].rearrange("p b n -> p (b n)")
    s_w, s_zero, s_con = core.sem("swa_w"), core.sem("swa_zeroed"), core.sem("swa_tables")
    s_mm, s_v, s_sq, s_ss, s_rt, s_dve, s_rd = (core.sem("swap_" + n) for n in
                                          ("projected", "v_kept", "squares", "means", "roots", "dve_steps", "banks_read"))
    s_g, s_pp, s_rope, s_tr, s_ev = (core.sem("swap_" + n) for n in ("gained", "pool_products", "rotated", "transposed", "evacuated"))
    with ExitStack() as ctx:
        def sb(name, shape):
            return ctx.enter_context(nc.sbuf_tensor(name, shape, F32))
        w = sb("swa_w_in", [P, KD, 768])
        sq = sb("swa_squares", [P, NQK, HD])
        st = sb("swa_stats", [P, 2, 4, NQK])
        t = sb("swa_normed", [P, 2, NQK, HD])
        m = sb("swa_products", [P, 4, NQK, HD // 2])
        dst = sb("swa_rotated", [P, 2, NQK, HD])
        block = ctx.enter_context(nc.Block())
        KV0, NQ = SH * HD, SH
        cos = core.a("cos").rearrange("p (t d) -> p t d", t=XT)
        sin = core.a("sin").rearrange("p (t d) -> p t d", t=XT)
        gain = core.r("qkg").rearrange("p (h d) -> p h d", d=HD)

        def heads(tile):
            return slice(NQ, NQK) if tile < CT else slice(0, NQK)

        def bank(tile):
            o = 1024 * (tile % 2)
            return flat[:, o:o + 768]

        @block.sync
        def _(sp):
            load_w_in(core, sp, w[:], S0, 768, s_w)
            sp.dma_start(core.swa_con[:], io["swa_con"]).then_inc(s_con, 16)
            sp.wait_ge(s_con, 16)

        @block.gpsimd
        def _(pool):
            g = nc.gpsimd
            pool.wait_ge(s_con, 16)
            g.memset(kT[:, 0:P], 0.0)
            g.memset(kT[:, P + SEQ:PADK], 0.0)
            g.memset(V[:, 0, :], 0.0)
            g.memset(V[:, 1 + XT, :], 0.0).then_inc(s_zero, 1)
            for n in range(NT):
                if n < CT:
                    continue
                pool.wait_ge(s_g, n + 1)
                if n > CT:
                    pool.wait_ge(s_rope, n)
                tt = t[:, n % 2].rearrange("p h (d e) -> p h d e", e=2)
                cs = cos[:, n - CT, :].unsqueeze(1).broadcast_to([P, NQK, 32])
                sn = sin[:, n - CT, :].unsqueeze(1).broadcast_to([P, NQK, 32])
                g.tensor_tensor(m[:, 1], tt[:, :, :, 1], sn, ALU.mult)
                g.tensor_tensor(m[:, 3], tt[:, :, :, 1], cs, ALU.mult).then_inc(s_pp, 1)

        @block.tensor
        def _(pe):
            def transposes(n):
                pe.wait_ge(s_rope, n + 1)
                if n >= CT + 2:
                    pe.wait_ge(s_ev, n - 1)
                o = 2048 + 1024 * (n % 2)
                pairs = range(4, 5) if n < CT else range(5)
                for i in pairs:
                    tr = nc.tensor.transpose(flat[:, o + i * P:o + (i + 1) * P],
                                             dst[:, n % 2, 2 * i:2 * i + 2, :].rearrange("p h d -> p (h d)"),
                                             core.k("ident"))
                tr.then_inc(s_tr, 1)

            pe.wait_ge(s_w, 16)
            for n in range(NT):
                if n >= 2:
                    pe.wait_ge(s_rd, n - 1)
                    pe.wait_ge(s_v, n - 1)
                    pe.wait_ge(s_sq, n - 1)
                out = bank(n)
                for a, b in ((0, KV0), (KV0, 768)) if n >= CT else ((KV0, 768),):
                    for k in range(KD):
                        mm = nc.tensor.matmul(out[:, a:b], hT[:, k, n * P:(n + 1) * P], w[:, k, a:b],
                                              start=(k == 0), stop=(k == KD - 1))
                mm.then_inc(s_mm, 1)
                if n:
                    transposes(n - 1)
            transposes(NT - 1)

        @block.scalar
        def _(act):
            def keep(n):
                act.wait_ge(s_tr, n + 1)
                o = 2048 + 1024 * (n % 2)
                if n >= CT:
                    nc.scalar.copy(qT[:, :, (n - CT) * P:(n - CT + 1) * P],
                                   flat[:, o:o + 512].rearrange("p (g q) -> p g q", g=4))
                at = PADK + n * P if n < CT else P + (n - CT) * P
                nc.scalar.copy(kT[:, at:at + P], flat[:, o + 512:o + 640]).then_inc(s_ev, 1)

            for n in range(NT):
                act.wait_ge(s_mm, n + 1)
                h = heads(n)
                out = bank(n)[:, 0:NQK * HD].rearrange("p (h d) -> p h d", d=HD)
                if n:
                    act.wait_ge(s_ss, n)
                nc.scalar.activation(sq[:, h, :], out[:, h, :], ACT.Square).then_inc(s_sq, 1)
                nc.scalar.copy(V[:, (1 + XT + 1 + n) if n < CT else 1 + n - CT, :], bank(n)[:, 640:768]).then_inc(s_v, 1)
                act.wait_ge(s_ss, n + 1)
                nc.scalar.activation(st[:, n % 2, 1, h], st[:, n % 2, 0, h], ACT.Sqrt).then_inc(s_rt, 1)
                if n:
                    keep(n - 1)
            keep(NT - 1)

        @block.vector
        def _(dve):
            step = Serial(dve, s_dve)
            v = nc.vector
            dve.wait_ge(s_con, 16)
            for n in range(NT):
                h, b = heads(n), n % 2
                N = NQK if n >= CT else SKV
                out = bank(n)[:, 0:NQK * HD].rearrange("p (h d) -> p h d", d=HD)
                dve.wait_ge(s_sq, n + 1)
                step(v.tensor_reduce(st[:, b, 2, h], sq[:, h, :], AX, ALU.add))
                v.tensor_scalar(st[:, b, 0, h], st[:, b, 2, h], 1.0 / HD, EPS, ALU.mult, ALU.add).then_inc(s_ss, 1)
                dve.wait_ge(s_rt, n + 1)
                step(v.reciprocal(st[:, b, 3, h], st[:, b, 1, h]))
                v.tensor_tensor(t[:, b, h, :], out[:, h, :], st[:, b, 3, h].unsqueeze(2).broadcast_to([P, N, HD]),
                                ALU.mult).then_inc(s_rd, 1)
                dve.wait_ge(s_rd, n + 1)
                v.tensor_tensor(t[:, b, h, :], t[:, b, h, :], gain[:, h, :], ALU.mult).then_inc(s_g, 1)
                dve.wait_ge(s_g, n + 1)
                if n >= 2:
                    dve.wait_ge(s_tr, n - 1)
                tt = t[:, b].rearrange("p h (d e) -> p h d e", e=2)
                if n < CT:
                    v.tensor_copy(dst[:, b, NQ:, 0:32], tt[:, NQ:, :, 0])
                    v.tensor_copy(dst[:, b, NQ:, 32:64], tt[:, NQ:, :, 1]).then_inc(s_rope, 1)
                    continue
                cs = cos[:, n - CT, :].unsqueeze(1).broadcast_to([P, NQK, 32])
                sn = sin[:, n - CT, :].unsqueeze(1).broadcast_to([P, NQK, 32])
                v.tensor_tensor(m[:, 0], tt[:, :, :, 0], cs, ALU.mult)
                step(v.tensor_tensor(m[:, 2], tt[:, :, :, 0], sn, ALU.mult))
                dve.wait_ge(s_pp, n - CT + 1)
                q_dst = dst[:, b, 0:NQ, :].rearrange("p (g v) d -> p v g d", v=2)
                for lo, x, y, op in ((0, 0, 1, ALU.subtract), (32, 2, 3, ALU.add)):
                    v.tensor_tensor(q_dst[:, :, :, lo:lo + 32], m[:, x, 0:NQ].rearrange("p (v g) d -> p v g d", v=2),
                                    m[:, y, 0:NQ].rearrange("p (v g) d -> p v g d", v=2), op)
                    last = v.tensor_tensor(dst[:, b, NQ:, lo:lo + 32], m[:, x, NQ:], m[:, y, NQ:], op)
                last.then_inc(s_rope, 1)
            dve.wait_ge(s_zero, 1)


def swa_attend(core, qT, kT, V):
    nc, io, ps = core.nc, core.io, core.ps
    out_b = core.branch[1]
    flat = ps[:].rearrange("p b n -> p (b n)")
    s_s, s_mx, s_nm, s_e, s_es, s_den, s_dve, s_p, s_tr, s_pt, s_pv, s_o = (core.sem("swa_" + n) for n in (
        "scores", "masked_max", "minus_max", "exps", "sink_exp", "den", "dve_steps", "probs", "probs_turned", "turned_kept",
        "values_summed", "output_kept"))
    with ExitStack() as ctx:
        def sb(name, shape):
            return ctx.enter_context(nc.sbuf_tensor(name, shape, F32))
        S = sb("swa_S", [P, 2, KEYS])
        pr = sb("swa_P", [P, 3, KEYS])
        PT = sb("swa_PT", [P, 2, 5, 4, P])
        sc = sb("swa_cols", [P, 2, 8])
        block = ctx.enter_context(nc.Block())
        mask = core.a("smask").rearrange("p (m s) -> p m s", m=3)
        sink = core.r("sink")
        JOBS = [(n, kv, g) for n in range(XT) for kv in range(SKV) for g in range(4)]

        @block.tensor
        def _(pe):
            def turned(m):
                n, kv, g = JOBS[m]
                pe.wait_ge(s_p, m + 1)
                if m >= 2:
                    pe.wait_ge(s_pt, m - 1)
                big, small = (4, 5) if m % 2 == 0 else (6, 5)
                lo = 256 * (m % 2)
                for i in range(5):
                    if i == 4 and m:
                        pe.wait_ge(s_pt, m)
                    o = ps[:, big, i * P:(i + 1) * P] if i < 4 else ps[:, small, lo:lo + P]
                    tr = nc.tensor.transpose(o, pr[:, m % 3, i * P:(i + 1) * P], core.k("ident"))
                tr.then_inc(s_tr, 1)

            def values(m):
                n, kv, _ = JOBS[m]
                pe.wait_ge(s_pt, m + 1)
                if kv == 0 and n:
                    pe.wait_ge(s_o, n)
                for i in range(5):
                    tile = n + i if i < 3 else XT + 2 + i - 3
                    mm = nc.tensor.matmul(ps[64 * kv:64 * kv + 64, 7, :], V[:, tile, 64 * kv:64 * kv + 64],
                                          PT[:, kv, i].rearrange("p g q -> p (g q)"), start=(i == 0), stop=(i == 4))
                mm.then_inc(s_pv, 1)

            for m, (n, kv, g) in enumerate(JOBS):
                if m >= 2:
                    pe.wait_ge(s_mx, m - 1)
                o = 1024 * (m % 2)
                q = qT[64 * kv:64 * kv + 64, g, n * P:(n + 1) * P]
                nc.tensor.matmul(flat[:, o + P:o + 4 * P], q, kT[64 * kv:64 * kv + 64, n * P:(n + 3) * P],
                                 start=True, stop=True)
                nc.tensor.matmul(flat[:, o + 4 * P:o + 6 * P], q, kT[64 * kv:64 * kv + 64, PADK:KEYCOLS],
                                 start=True, stop=True).then_inc(s_s, 1)
                if m >= 2:
                    turned(m - 2)
                    if m % 4 == 2 and m > 4:
                        values(m - 3)
            turned(len(JOBS) - 2)
            turned(len(JOBS) - 1)
            values(len(JOBS) - 1)

        @block.vector
        def _(dve):
            v = nc.vector
            step = Serial(dve, s_dve)

            def evacuate(n):
                dve.wait_ge(s_pv, 2 * n + 2)
                v.tensor_copy(out_b[:, :, n * P:(n + 1) * P], ps[:, 7, :].rearrange("p (g q) -> p g q", g=4)).then_inc(s_o, 1)

            def norm(m):
                b = m % 2
                dve.wait_ge(s_es, m + 1)
                step(v.tensor_tensor(sc[:, b, 4:5], sc[:, b, 2:3], sc[:, b, 3:4], ALU.add))
                step(v.reciprocal(sc[:, b, 5:6], sc[:, b, 4:5]))
                v.tensor_scalar(pr[:, m % 3], pr[:, m % 3], sc[:, b, 5:6], None, ALU.mult).then_inc(s_p, 1)

            for m, (n, kv, g) in enumerate(JOBS):
                b, o = m % 2, 1024 * (m % 2)
                kind = 0 if n == 0 else 2 if n == XT - 1 else 1
                slot = 2 * g + kv
                dve.wait_ge(s_s, m + 1)
                v.tensor_tensor_reduce(S[:, b], flat[:, o + P:o + 6 * P], mask[:, kind], HD ** -0.5,
                                       sink[:, slot:slot + 1], ALU.add, ALU.max, sc[:, b, 0:1]).then_inc(s_mx, 1)
                dve.wait_ge(s_mx, m + 1)
                v.tensor_scalar(sc[:, b, 1:2], sc[:, b, 0:1], -1.0, None, ALU.mult).then_inc(s_nm, 1)
                if m:
                    norm(m - 1)
                if m % 8 == 3 and m > 8:
                    evacuate((m - 11) // 8)
            norm(len(JOBS) - 1)
            evacuate(XT - 1)

        @block.scalar
        def _(act):
            def kept(m):
                n, kv, g = JOBS[m]
                act.wait_ge(s_tr, m + 1)
                if n and g == 0:
                    act.wait_ge(s_pv, 2 * (n - 1) + kv + 1)
                big, lo = (4, 0) if m % 2 == 0 else (6, 256)
                nc.scalar.copy(PT[:, kv, 0:4, g, :], ps[:, big, :].rearrange("p (i q) -> p i q", i=4))
                nc.scalar.copy(PT[:, kv, 4, g, :], ps[:, 5, lo:lo + P]).then_inc(s_pt, 1)

            for m, (n, kv, g) in enumerate(JOBS):
                b, slot = m % 2, 2 * g + kv
                act.wait_ge(s_nm, m + 1)
                if m >= 3:
                    act.wait_ge(s_tr, m - 2)
                nc.scalar.activation(pr[:, m % 3], S[:, b], ACT.Exp, bias=sc[:, b, 1:2], accum_out=sc[:, b, 2:3]).then_inc(s_e, 1)
                nc.scalar.activation(sc[:, b, 3:4], sink[:, slot:slot + 1], ACT.Exp, bias=sc[:, b, 1:2]).then_inc(s_es, 1)
                if m >= 2:
                    kept(m - 2)
            kept(len(JOBS) - 2)
            kept(len(JOBS) - 1)


def swa(core):
    core.branch[1] = core.keep("branch_swa", [P, C5, SEQ])
    with ExitStack() as ctx:
        def sb(name, shape):
            return ctx.enter_context(core.nc.sbuf_tensor(name, shape, F32))
        core.swa_con = sb("swa_tables_sb", [P, PSWA_N])
        qT, kT, V = sb("qT", [P, 4, SEQ]), sb("kT", [P, KEYCOLS]), sb("V", [P, XT + 2 + CT, P])
        core.phase(swa_project, qT, kT, V)
        core.phase(swa_attend, qT, kT, V)


class Gdn:

    def __init__(self, core, ctx):
        def sb(name, shape):
            return ctx.enter_context(core.nc.sbuf_tensor(name, shape, F32))
        self.ktok, self.vtok = sb("gdn_ktok", [P, NT, GH, P]), sb("gdn_vtok", [P, NT, GH, P])
        self.kT, self.qT = sb("gdn_kT", [P, GH, TOK]), sb("gdn_qT", [P, GH, SEQ])
        self.g, self.gb, self.beta, self.bg, self.el = (sb("gdn_" + n, [P, NT, 2 * GH]) for n in ("g", "gb", "beta", "bg", "el"))


def gdn_project(core, G):
    nc, io, ps, hT = core.nc, core.io, core.ps, core.hT
    flat = ps[:].rearrange("p b n -> p (b n)")
    GW = 256
    CH = 3 * C5
    s_w = [core.sem(f"gdn_w{i}") for i in range(2)]
    names = ("padded", "projected", "raw_kept", "conv", "silu", "by_tokens", "squares", "means", "roots", "dve_steps",
             "tok_kept", "turned_back", "turned_kept")
    s_pad, s_mm, s_raw, s_cv, s_si, s_tt, s_sq, s_ss, s_rt, s_dve, s_tk, s_tb, s_tbk = (core.sem("gdnp_" + n) for n in names)
    with ExitStack() as ctx:
        def sb(name, shape):
            return ctx.enter_context(nc.sbuf_tensor(name, shape, F32))
        w = sb("gdn_w_in", [P, 2, KD, GW])
        raw = sb("gdn_raw", [P, 2, PADDED])
        cv = sb("gdn_conv", [P, PADDED])
        si = sb("gdn_silu", [P, PADDED])
        sq = sb("gdn_squares", [P, NT, P])
        qtok = sb("gdn_qtok", [P, NT, P])
        st = sb("gdn_stats", [P, 4, NT])
        block = ctx.enter_context(nc.Block())
        conv_w = core.c("gconv").rearrange("p (c j) -> p c j", j=4)
        TOKB = 1536 * 1 + 256
        TURN = 3072
        tok_ps = flat[:, TOKB:TOKB + TOK].rearrange("p (t c) -> p t c", c=P)

        def turns(c):
            return 2 * min(c, C5) + 3 * max(0, c - C5)

        def si_tile(t):
            o = t * P if t < CT else CTX + 3 + (t - CT) * P
            return si[:, o:o + P]

        @block.sync
        def _(sp):
            for n in range(CH * P // GW):
                if n >= 2:
                    sp.wait_ge(s_mm, 2 * (n - 1))
                load_w_in(core, sp, w[:, n % 2], Q0 + n * GW, GW, s_w[n % 2])

        @block.gpsimd
        def _(pool):
            for b in range(2):
                nc.gpsimd.memset(raw[:, b, 0:2], 0.0)
                nc.gpsimd.memset(raw[:, b, 2 + CTX:5 + CTX], 0.0)
                nc.gpsimd.memset(raw[:, b, PADDED - 1:PADDED], 0.0).then_inc(s_pad, 1)

        @block.tensor
        def _(pe):
            def by_tokens(c):
                pe.wait_ge(s_si, c + 1)
                if c:
                    pe.wait_ge(s_tk, c)
                for t in range(NT):
                    tr = nc.tensor.transpose(tok_ps[:, t, :], si_tile(t), core.k("ident"))
                tr.then_inc(s_tt, 1)

            def turn_back(c):
                pe.wait_ge(s_tk, c + 1)
                tiles = list(range(CT if c < C5 else 0, NT))
                for i in range(0, len(tiles), 4):
                    group = tiles[i:i + 4]
                    n = turns(c) + i // 4
                    if n >= 2:
                        pe.wait_ge(s_tbk, n - 1)
                    for j, t in enumerate(group):
                        src = qtok[:, t, :] if c < C5 else G.ktok[:, t, c - C5, :]
                        tr = nc.tensor.transpose(flat[:, TURN + 512 * (n % 2) + j * P:TURN + 512 * (n % 2) + (j + 1) * P],
                                                 src, core.k("ident"))
                    tr.then_inc(s_tb, 1)

            for c in range(CH):
                pe.wait_ge(s_w[(c // 2) % 2], 16 * (c // 4 + 1))
                if c:
                    pe.wait_ge(s_raw, c)
                for t0, n, at in PIECES:
                    for k in range(KD):
                        mm = nc.tensor.matmul(flat[:, at:at + n], w[:, (c // 2) % 2, k, (c % 2) * P:(c % 2 + 1) * P],
                                              hT[:, k, t0:t0 + n], start=(k == 0), stop=(k == KD - 1))
                mm.then_inc(s_mm, 1)
                if c:
                    by_tokens(c - 1)
                if 2 <= c <= 2 * C5 + 1:
                    turn_back(c - 2)
            by_tokens(CH - 1)

        @block.scalar
        def _(act):
            def turned_kept(c):
                tiles = list(range(CT if c < C5 else 0, NT))
                for i in range(0, len(tiles), 4):
                    n, count = turns(c) + i // 4, len(tiles[i:i + 4])
                    act.wait_ge(s_tb, n + 1)
                    dst = (G.qT[:, c, (tiles[i] - CT) * P:] if c < C5 else G.kT[:, c - C5, tiles[i] * P:])[:, 0:count * P]
                    nc.scalar.copy(dst, flat[:, TURN + 512 * (n % 2):TURN + 512 * (n % 2) + count * P]).then_inc(s_tbk, 1)

            for c in range(CH + 1):
                if c < CH:
                    act.wait_ge(s_mm, c + 1)
                    if c >= 2:
                        act.wait_ge(s_cv, c - 1)
                    nc.scalar.copy(raw[:, c % 2, 2:2 + CTX], flat[:, 256:512])
                    nc.scalar.copy(raw[:, c % 2, PAD_AT[1]:PAD_AT[1] + SEQ], flat[:, 512:1536]).then_inc(s_raw, 1)
                    if 2 <= c <= 2 * C5 + 1:
                        turned_kept(c - 2)
                    act.wait_ge(s_cv, c + 1)
                    if c:
                        act.wait_ge(s_tt, c)
                    nc.scalar.activation(si[:, 0:CONV], cv[:, 0:CONV], ACT.Silu).then_inc(s_si, 1)
                if 1 <= c:
                    b = c - 1
                    act.wait_ge(s_tt, b + 1)
                    if b < 2 * C5:
                        if b:
                            act.wait_ge(s_ss, b)
                        nc.scalar.activation(sq[:], tok_ps, ACT.Square).then_inc(s_sq, 1)
                        act.wait_ge(s_ss, b + 1)
                        nc.scalar.activation(st[:, 2, :], st[:, 1, :], ACT.Sqrt).then_inc(s_rt, 1)
                    else:
                        nc.scalar.copy(G.vtok[:, :, b - 2 * C5, :], tok_ps).then_inc(s_tk, 1)

        @block.vector
        def _(dve):
            v = nc.vector
            step = Serial(dve, s_dve)
            dve.wait_ge(s_pad, 2)
            for c in range(CH + 1):
                if c < CH:
                    dve.wait_ge(s_raw, c + 1)
                    if c:
                        dve.wait_ge(s_si, c)
                    r = raw[:, c % 2]
                    step(v.tensor_scalar(cv[:, 0:CONV], r[:, 0:CONV], conv_w[:, c, 0:1], None, ALU.mult))
                    for j in range(1, 4):
                        op = v.scalar_tensor_tensor(cv[:, 0:CONV], r[:, j:j + CONV], conv_w[:, c, j:j + 1],
                                                    cv[:, 0:CONV], ALU.mult, ALU.add)
                        step(op) if j < 3 else op.then_inc(s_cv, 1)
                if 1 <= c <= 2 * C5:
                    b = c - 1
                    dve.wait_ge(s_sq, b + 1)
                    step(v.tensor_reduce(st[:, 0, :], sq[:], AX, ALU.add))
                    v.tensor_scalar(st[:, 1, :], st[:, 0, :], EPS, None, ALU.add).then_inc(s_ss, 1)
                    dve.wait_ge(s_rt, b + 1)
                    step(v.reciprocal(st[:, 3, :], st[:, 2, :]))
                    if b < C5:
                        step(v.tensor_scalar(st[:, 3, :], st[:, 3, :], P ** -0.5, None, ALU.mult))
                    if b == C5:
                        dve.wait_ge(s_tb, turns(C5))
                    if 1 <= b < C5:
                        dve.wait_ge(s_tb, turns(b))
                    dst = qtok[:] if b < C5 else G.ktok[:, :, b - C5, :]
                    v.tensor_tensor(dst, tok_ps, st[:, 3, :].unsqueeze(2).broadcast_to([P, NT, P]), ALU.mult).then_inc(s_tk, 1)


def gdn_gates(core, G):
    nc, io, ps, hT = core.nc, core.io, core.ps, core.hT
    s_abc, s_abk = core.sem("gdng_by_channel"), core.sem("gdng_kept")
    s_w, s_ab, s_dve, s_x, s_z, s_be, s_g, s_sum, s_gb, s_e = (core.sem("gdng_" + n) for n in (
        "w", "projected", "dve_steps", "shifted", "exp", "beta", "decay", "summed", "sums_kept", "exps"))
    with ExitStack() as ctx:
        def sb(name, shape):
            return ctx.enter_context(nc.sbuf_tensor(name, shape, F32))
        w, abc = sb("gdn_w_ab", [P, KD, 16]), sb("gdn_ab_by_channel", [16, TOK])
        x, z, t1, t2, acc, ea = (sb("gdn_sp_" + n, [P, NT, 8]) for n in ("x", "z", "s", "q", "acc", "ea"))
        block = ctx.enter_context(nc.Block())
        by_channel = ps[0:16, 3:6, :].rearrange("p b n -> p (b n)")
        ab = ps[:, 0, 0:NT * 16].rearrange("p (t c) -> p t c", c=16)
        sums = ps[:, 1, 0:NT * 8].rearrange("p (t c) -> p t c", c=8)
        total = ps[:, 2, 0:NT * 8].rearrange("p (t c) -> p t c", c=8)

        @block.sync
        def _(sp):
            load_w_in(core, sp, w[:], AB0, 16, s_w)

        @block.tensor
        def _(pe):
            pe.wait_ge(s_w, 16)
            for t0, n, at in PIECES:
                for k in range(KD):
                    mm = nc.tensor.matmul(by_channel[:, at:at + n], w[:, k, :], hT[:, k, t0:t0 + n],
                                          start=(k == 0), stop=(k == KD - 1))
            mm.then_inc(s_abc, 1)
            pe.wait_ge(s_abk, 1)
            for t in range(NT):
                tr = nc.tensor.transpose(ab[:, t, :], abc[:, t * P:(t + 1) * P], core.k("ident")[0:16, 0:16])
            tr.then_inc(s_ab, 1)
            pe.wait_ge(s_g, 1)
            for d in range(2):
                nc.tensor.matmul(sums[:, :, 4 * d:4 * d + 4], core.k("tri128")[:, d * P:(d + 1) * P],
                                 G.g[:, :, 4 * d:4 * d + 4], start=True, stop=True)
            nc.tensor.matmul(total, core.k("blk"), G.g[:], start=True, stop=True).then_inc(s_sum, 1)

        @block.scalar
        def _(act):
            act.wait_ge(s_abc, 1)
            nc.scalar.copy(abc[:], by_channel[:, 256:1536]).then_inc(s_abk, 1)
            act.wait_ge(s_ab, 1)
            nc.scalar.activation(G.beta[:], ab[:, :, 8:16], ACT.Sigmoid).then_inc(s_be, 1)
            act.wait_ge(s_x, 1)
            nc.scalar.activation(z[:], x[:], ACT.Abs).then_inc(s_z, 1)
            act.wait_ge(s_z, 1)
            nc.scalar.activation(z[:], z[:], ACT.Exp, scale=-1.0).then_inc(s_z, 1)
            nc.scalar.activation(ea[:, 0, :], core.r("alog"), ACT.Exp).then_inc(s_z, 1)
            act.wait_ge(s_gb, 2)
            nc.scalar.activation(t1[:], G.gb[:], ACT.Exp).then_inc(s_e, 1)
            nc.scalar.activation(G.el[:], t2[:], ACT.Exp).then_inc(s_e, 1)

        @block.vector
        def _(dve):
            v = nc.vector
            step = Serial(dve, s_dve)
            wide = lambda a: a.unsqueeze(1).broadcast_to([P, NT, 8])
            dve.wait_ge(s_be, 1)
            v.tensor_tensor(x[:], ab[:, :, 0:8], wide(core.r("dtb")), ALU.add).then_inc(s_x, 1)
            dve.wait_ge(s_z, 3)
            softplus_tail(nc, step, z[:], t1[:], t2[:], acc[:])
            step(v.scalar_tensor_tensor(acc[:], x[:], 0.0, acc[:], ALU.max, ALU.add))
            v.scalar_tensor_tensor(G.g[:], acc[:], -1.0, wide(ea[:, 0, :]), ALU.mult, ALU.mult).then_inc(s_g, 1)
            dve.wait_ge(s_sum, 1)
            v.tensor_copy(G.gb[:], sums).then_inc(s_gb, 1)
            dve.wait_ge(s_gb, 1)
            v.tensor_tensor(t2[:], total, G.gb[:], ALU.subtract).then_inc(s_gb, 1)
            dve.wait_ge(s_e, 2)
            dve.wait_ge(s_be, 1)
            step(v.scalar_tensor_tensor(G.bg[:], G.beta[:], -1.0, t1[:], ALU.mult, ALU.mult))


def gdn_scan(core, G):
    nc, io, ps, hT = core.nc, core.io, core.ps, core.hT
    oT = core.branch[0]
    LEVELS = 6
    names = dict(rows_full=1, grams=1, diffs=1, exp_D=1, exp_DT="latent", exp_rows=1, beta_mask=1, A=1, qkd="latent", A_turned=1,
                 PT=LEVELS - 1, Pk=LEVELS - 1, X=LEVELS, powers=LEVELS, scaled=1, qe="latent", ks=2, rest=2,
                 v_product=2, v_new=2, o="2 latent", state=2, state_kept="1 + 2", o_kept="2 latent", strict_beta=1)
    S = [{n: core.sem(f"gdns_{n}{d}") for n in names} for d in range(2)]
    s_dve = core.sem("gdns_dve_steps")
    GROUPS = 3 * KD
    JOBS, STAGES = 2 * GROUPS, 14
    PLACES = STAGES * NT
    s_gw, s_gst = [core.sem(f"gate_w{i}") for i in range(2)], [core.sem(f"gate_stored{i}") for i in range(2)]
    s_gmm, s_gcp = core.sem("gate_multiplied"), core.sem("gate_copied")
    with ExitStack() as ctx:
        gw0 = ctx.enter_context(nc.sbuf_tensor("gate_w_sb", [P, KD, P], F32))
        gw = (gw0[:], core.late[:, 1, :].rearrange("p (k n) -> p k n", k=KD))
        gl = core.late[:, 0, :].rearrange("p (b t) -> p b t", b=2)

        def sb(name, shape):
            return [ctx.enter_context(nc.sbuf_tensor(f"gdns_{name}{d}", shape, F32)) for d in range(2)]
        diff, D, DT, bm = (sb(n, [P, GH, GC]) for n in ("diff", "D", "DT", "bm"))
        QKD = sb("QKDT", [P, GH, GC])
        Pw = sb("P", [P, GH, 2, GC])
        XP = sb("XP", [P, GH, 2, GC])
        ke, vb, vn, St, qe = (sb(n, [P, GH, P]) for n in ("ke", "vb", "v_new", "S", "qe"))
        rows_full = sb("rows_full", [P, 2, GH, GC])
        E = sb("E", [P, 2, GH, GC])
        block = ctx.enter_context(nc.Block())
        ident, ones = core.k("ident"), core.k("ones")
        md, mdt, strict = (core.k(n).rearrange("p (d j) -> p d j", d=2) for n in ("md", "mdt", "strict"))
        HALF = [slice(0, GC), slice(GC, P)]

        def tile_of(s, d):
            return s if d == 0 else (CT - 1 - s if s < CT else NT + CT - 1 - s)

        def chunk(d, i):
            return i if d == 0 else 1 - i

        def wide(a):
            return a.unsqueeze(1).broadcast_to([P, GH, GC])

        def cols(a, t, d, n):
            return a[:, t, 4 * d:4 * d + 4].unsqueeze(2).broadcast_to([P, GH, n])

        def bank(d, b):
            return ps[:, 4 * d + b, :]

        def heads(a):
            return a.rearrange("p (h j) -> p h j", h=GH)

        def flat(a):
            return a.rearrange("p h e -> p (h e)")

        def pair(d):
            return bank(d, 2).rearrange("p (h x j) -> p h x j", h=GH, x=2)

        def right(hd):
            return slice(4 * GC + GC * hd, 5 * GC + GC * hd)

        BOTH = range(2)

        def first_of(place):
            return place * JOBS * KD // PLACES

        def last_place(job):
            return next(p for p in range(PLACES) if first_of(p + 1) >= KD * (job + 1))

        def jobs_between(a, b):
            return [j for j in range(JOBS) if a <= last_place(j) < b]

        @block.sync
        def _(sp):
            def load(g, slot):
                sp.dma_start(gw[slot], io["w_gates"][g].rearrange("p (k n) -> p k n", k=KD)).then_inc(s_gw[slot], 16)

            def store(i, j):
                sp.wait_ge(s_gcp, 12 * i + j + 1)
                sp.dma_start(core.gate_dram[2 * i + j // 6, j % 2, :, (j // 2) % 3, :], gl[:, j % 2, :])\
                    .then_inc(s_gst[j % 2], 16)
            load(0, 0)
            load(1, 1)
            for i in range(GROUPS // 6):
                for j in range(12):
                    store(i, j)
                    if j % 2 and 6 * i + j // 2 + 2 < GROUPS:
                        load(6 * i + j // 2 + 2, (j // 2) % 2)
            for b in BOTH:
                sp.wait_ge(s_gst[b], 16 * GROUPS)

        @block.tensor
        def _(pe):
            mmul = nc.tensor.matmul

            def fill(s, stage):
                place = STAGES * s + stage
                for n in range(first_of(place), first_of(place + 1)):
                    job, k = divmod(n, KD)
                    g, half = divmod(job, 2)
                    if k == 0 and half == 0:
                        pe.wait_ge(s_gw[g % 2], 16 * (g // 2 + 1))
                    if k == 0 and job >= 2:
                        pe.wait_ge(s_gcp, job - 1)
                    mm = mmul(ps[:, 3 + 4 * half, :], gw[g % 2][:, k, :], hT[:, k, CTX + 512 * half:CTX + 512 * half + 512],
                              start=(k == 0), stop=(k == KD - 1))
                    if k == KD - 1:
                        mm.then_inc(s_gmm, 1)

            def grams(s, d):
                q, t = S[d], tile_of(s, d)
                if s:
                    pe.wait_ge(q["rest"], 2 * s)
                    pe.wait_ge(q["state_kept"], 1 + 2 * s)
                if s > CT:
                    pe.wait_ge(q["o_kept"], 2 * (s - CT))
                pe.wait_ge(q["rows_full"], s + 1)
                mmul(bank(d, 1), ones, rows_full[d][:].rearrange("p c h j -> p (c h j)"), start=True, stop=True)
                for c in BOTH:
                    t0 = t * P + GC * c
                    for hd in range(GH):
                        k = G.kT[:, hd, t0:t0 + GC]
                        mm = mmul(bank(d, 0)[HALF[c], 256 + GC * hd:256 + GC * hd + GC], k, k, start=True, stop=True)
                        if s >= CT:
                            mm = mmul(bank(d, 2)[HALF[c], GC * hd:GC * hd + GC], k, G.qT[:, hd, t0 - CTX:t0 - CTX + GC],
                                      start=True, stop=True)
                mm.then_inc(q["grams"], 1)

            def turn_A(s, d):
                q = S[d]
                pe.wait_ge(q["A"], s + 1)
                if s >= CT:
                    pe.wait_ge(q["qkd"], s - CT + 1)
                for c in BOTH:
                    for hd in range(GH):
                        mm = mmul(pair(d)[HALF[c], hd, 1, :], Pw[d][HALF[c], hd, c, :],
                                  ident[HALF[c], HALF[c]], start=True, stop=True)
                mm.then_inc(q["A_turned"], 1)

            def power(s, d, lev):
                q = S[d]
                if lev:
                    pe.wait_ge(q["Pk"], (LEVELS - 1) * s + lev)
                if lev < LEVELS - 1:
                    pe.wait_ge(q["PT"], (LEVELS - 1) * s + lev + 1)
                if lev:
                    pe.wait_ge(q["X"], LEVELS * s + lev)
                if lev < LEVELS - 1:
                    for c in BOTH:
                        for hd in range(GH):
                            mm = mmul(bank(d, 0)[HALF[c], GC * hd:GC * hd + GC], XP[d][HALF[c], hd, 1, :],
                                      Pw[d][HALF[c], hd, c, :], start=True, stop=True)
                part = slice(0 if lev else 1, 2 if lev < LEVELS - 2 else 1)
                for hd in range(GH):
                    mm = mmul(pair(d)[:, hd, part, :], Pw[d][:, hd].rearrange("p c j -> p (c j)"), XP[d][:, hd, part, :],
                              start=True, stop=True)
                mm.then_inc(q["powers"], 1)

            def scan_ks(s, d, i):
                q, c = S[d], chunk(d, i)
                pe.wait_ge(q["state_kept"], 1 + 2 * s + i)
                if i == 0:
                    pe.wait_ge(q["Pk"], (LEVELS - 1) * (s + 1))
                t0 = tile_of(s, d) * P + GC * c
                for hd in range(GH):
                    mm = mmul(bank(d, 0)[HALF[c], P * hd:P * hd + P], G.kT[:, hd, t0:t0 + GC], St[d][:, hd, :],
                              start=True, stop=True)
                mm.then_inc(q["ks"], 1)

            def scan_v(s, d, i):
                q, c = S[d], chunk(d, i)
                pe.wait_ge(q["rest"], 2 * s + i + 1)
                if i == 0:
                    pe.wait_ge(q["X"], LEVELS * (s + 1))
                    pe.wait_ge(q["exp_rows"], s + 1)
                for hd in range(GH):
                    mm = mmul(bank(d, 1)[HALF[c], P * hd:P * hd + P], XP[d][HALF[c], hd, 0, :], vb[d][HALF[c], hd, :],
                              start=True, stop=True)
                mm.then_inc(q["v_product"], 1)

            def scan_out(s, d, i):
                q, c = S[d], chunk(d, i)
                pe.wait_ge(q["v_new"], 2 * s + i + 1)
                if i == 0:
                    pe.wait_ge(q["scaled"], s + 1)
                for hd in range(GH):
                    mm = mmul(bank(d, 1)[:, P * hd:P * hd + P], ke[d][HALF[c], hd, :], vn[d][HALF[c], hd, :],
                              start=True, stop=True)
                mm.then_inc(q["state"], 1)
                if s >= CT:
                    if i == 0:
                        pe.wait_ge(q["qe"], s - CT + 1)
                    else:
                        pe.wait_ge(q["o_kept"], 2 * (s - CT) + 1)
                    for hd in range(GH):
                        o = bank(d, 2)[:, right(hd)]
                        mmul(o, St[d][:, hd, :], qe[d][:, hd, HALF[c]], start=True, stop=False)
                        mm = mmul(o, vn[d][HALF[c], hd, :], QKD[d][HALF[c], hd, :], start=False, stop=True)
                    mm.then_inc(q["o"], 1)

            for s in range(NT):
                for d in BOTH:
                    grams(s, d)
                fill(s, 0)
                for d in BOTH:
                    turn_A(s, d)
                fill(s, 1)
                for lev in range(LEVELS):
                    for d in BOTH:
                        power(s, d, lev)
                    fill(s, 2 + lev)
                for i in BOTH:
                    for d in BOTH:
                        scan_ks(s, d, i)
                    fill(s, 8 + 3 * i)
                    for d in BOTH:
                        scan_v(s, d, i)
                    fill(s, 9 + 3 * i)
                    for d in BOTH:
                        scan_out(s, d, i)
                    fill(s, 10 + 3 * i)

        @block.vector
        def _(dve):
            v = nc.vector
            step = Serial(dve, s_dve)

            def make_diffs(s, d):
                q, t = S[d], tile_of(s, d)
                dve.wait_ge(q["grams"], s + 1)
                for c in BOTH:
                    op = v.tensor_tensor(diff[d][HALF[c]], heads(bank(d, 1)[HALF[c], 256 * c:256 * c + 256]),
                                         cols(G.gb, t, d, GC)[HALF[c]], ALU.subtract)
                step(op)
                if s:
                    dve.wait_ge(q["beta_mask"], s)
                v.tensor_tensor(D[d][:], diff[d][:], wide(md[:, d, :]), ALU.max)
                v.tensor_tensor(DT[d][:], diff[d][:], wide(mdt[:, d, :]), ALU.min).then_inc(q["diffs"], 1)

            def make_A(s, d):
                q = S[d]
                dve.wait_ge(q["beta_mask"], s + 1)
                if s:
                    dve.wait_ge(q["powers"], LEVELS * s)
                for c in BOTH:
                    op = v.tensor_tensor(Pw[d][HALF[c], :, c, :], heads(bank(d, 0)[HALF[c], 256:512]), bm[d][HALF[c]], ALU.mult)
                op.then_inc(q["A"], 1)
                if s >= CT:
                    dve.wait_ge(q["exp_DT"], s - CT + 1)
                    v.tensor_tensor(QKD[d][:], heads(bank(d, 2)[:, 0:256]), DT[d][:], ALU.mult).then_inc(q["qkd"], 1)

            def first_X(s, d):
                q = S[d]
                dve.wait_ge(q["PT"], (LEVELS - 1) * s + 1)
                if s:
                    dve.wait_ge(q["v_product"], 2 * s)
                v.scalar_tensor_tensor(XP[d][:, :, 0, :], XP[d][:, :, 1, :], -1.0, wide(core.k("ident64")),
                                       ALU.mult, ALU.add).then_inc(q["X"], 1)

            def next_X(s, d, lev):
                q = S[d]
                dve.wait_ge(q["powers"], LEVELS * s + lev + 1)
                dve.wait_ge(q["X"], LEVELS * s + lev)
                if lev < LEVELS - 2:
                    dve.wait_ge(q["PT"], (LEVELS - 1) * s + lev + 2)
                v.tensor_tensor(XP[d][:, :, 0, :], XP[d][:, :, 0, :],
                                pair(d)[:, :, 0, :], ALU.add).then_inc(q["X"], 1)

            def rest(s, d, i):
                q, c, t = S[d], chunk(d, i), tile_of(s, d)
                h = HALF[c]
                dve.wait_ge(q["ks"], 2 * s + i + 1)
                dve.wait_ge(q["scaled"], s + 1)
                for hd in range(GH):
                    op = v.scalar_tensor_tensor(vb[d][h, hd, :], bank(d, 0)[h, P * hd:P * hd + P],
                                                G.bg[h, t, 4 * d + hd:4 * d + hd + 1], vb[d][h, hd, :], ALU.mult, ALU.add)
                op.then_inc(q["rest"], 1)

            def new_state(s, d, i):
                q, c, t = S[d], chunk(d, i), tile_of(s, d)
                last = GC - 1 if d == 0 else 0
                if s >= CT:
                    dve.wait_ge(q["o"], 2 * (s - CT) + i + 1)
                dve.wait_ge(q["state"], 2 * s + i + 1)
                dve.wait_ge(q["state_kept"], 1 + 2 * s + i)
                for hd in range(GH):
                    op = v.scalar_tensor_tensor(St[d][:, hd, :], St[d][:, hd, :], E[d][:, c, hd, last:last + 1],
                                                bank(d, 1)[:, P * hd:P * hd + P], ALU.mult, ALU.add)
                op.then_inc(q["state_kept"], 1)
                if s >= CT:
                    other = NT + CT - 1 - s
                    if other < s:
                        dve.wait_ge(S[1 - d]["o_kept"], 2 * (other - CT) + 2)
                    x = (t - CT) * P + GC * c
                    v.tensor_tensor(oT[:, :, x:x + GC], oT[:, :, x:x + GC], heads(bank(d, 2)[:, 256:512]),
                                    ALU.add).then_inc(q["o_kept"], 1)

            for d in BOTH:
                step(v.memset(Pw[d][:], 0.0))
            step(v.memset(oT[:], 0.0))
            for d in BOTH:
                v.memset(St[d][:], 0.0).then_inc(S[d]["state_kept"], 1)
            for s in range(NT):
                for d in BOTH:
                    make_diffs(s, d)
                for d in BOTH:
                    make_A(s, d)
                for d in BOTH:
                    first_X(s, d)
                for lev in range(1, LEVELS):
                    for d in BOTH:
                        next_X(s, d, lev)
                for i in BOTH:
                    for d in BOTH:
                        rest(s, d, i)
                    for d in BOTH:
                        new_state(s, d, i)

        @block.scalar
        def _(act):
            def exps(s, d):
                q = S[d]
                act.wait_ge(q["diffs"], s + 1)
                nc.scalar.activation(D[d][:], D[d][:], ACT.Exp, scale=-1.0).then_inc(q["exp_D"], 1)
                if s >= CT:
                    nc.scalar.activation(DT[d][:], DT[d][:], ACT.Exp).then_inc(q["exp_DT"], 1)
                if s:
                    act.wait_ge(q["state_kept"], 1 + 2 * s)
                if s > CT:
                    act.wait_ge(q["qe"], s - CT)
                nc.scalar.activation(E[d][:].rearrange("p c h j -> p (c h j)"), bank(d, 1), ACT.Exp).then_inc(q["exp_rows"], 1)

            def keep_PT(s, d, lev):
                q = S[d]
                if lev == 0:
                    act.wait_ge(q["A_turned"], s + 1)
                else:
                    act.wait_ge(q["powers"], LEVELS * s + lev)
                    if lev == 1:
                        act.wait_ge(q["X"], LEVELS * s + 1)
                nc.scalar.copy(XP[d][:, :, 1, :], pair(d)[:, :, 1, :]).then_inc(q["PT"], 1)

            def keep_P(s, d, lev):
                q = S[d]
                act.wait_ge(q["powers"], LEVELS * s + lev)
                for c in BOTH:
                    cp = nc.scalar.copy(Pw[d][HALF[c], :, c, :], heads(bank(d, 0)[HALF[c], 0:256]))
                cp.then_inc(q["Pk"], 1)

            def keep_v(s, d, i):
                q, h = S[d], HALF[chunk(d, i)]
                act.wait_ge(q["v_product"], 2 * s + i + 1)
                nc.scalar.copy(flat(vn[d][h]), bank(d, 1)[h, :]).then_inc(q["v_new"], 1)

            def copy_gates(s, a, b):
                for j in jobs_between(STAGES * s + a, STAGES * s + b):
                    act.wait_ge(s_gmm, j + 1)
                    if j >= 2:
                        act.wait_ge(s_gst[j % 2], 16 * (j // 2))
                    nc.scalar.copy(gl[:, j % 2, :], ps[:, 3 + 4 * (j % 2), :]).then_inc(s_gcp, 1)

            for s in range(NT):
                for d in BOTH:
                    exps(s, d)
                for d in BOTH:
                    keep_PT(s, d, 0)
                copy_gates(s, 0, 1)
                for lev in range(1, LEVELS):
                    for d in BOTH:
                        keep_P(s, d, lev)
                        if lev < LEVELS - 1:
                            keep_PT(s, d, lev)
                    copy_gates(s, lev, lev + 1)
                for d in BOTH:
                    keep_v(s, d, 0)
                copy_gates(s, LEVELS, 9)
                for d in BOTH:
                    keep_v(s, d, 1)
                copy_gates(s, 9, STAGES)

        @block.gpsimd
        def _(pool):
            g = nc.gpsimd
            tri_full = core.k("tri128").rearrange("p (d c j) -> p d c j", d=2, c=2)
            for s in range(NT):
                for d in BOTH:
                    q, t = S[d], tile_of(s, d)
                    if s:
                        pool.wait_ge(q["grams"], s)
                    for c in BOTH:
                        op = g.tensor_tensor(rows_full[d][:, c], wide(tri_full[:, d, c]), cols(G.g, t, d, GC), ALU.mult)
                    op.then_inc(q["rows_full"], 1)
                    if s:
                        pool.wait_ge(q["A"], s)
                    g.tensor_tensor(bm[d][:], wide(strict[:, d, :]), cols(G.beta, t, d, GC), ALU.mult)                        .then_inc(q["strict_beta"], 1)
                for d in BOTH:
                    q = S[d]
                    pool.wait_ge(q["exp_D"], s + 1)
                    pool.wait_ge(q["strict_beta"], s + 1)
                    g.tensor_tensor(bm[d][:], bm[d][:], D[d][:], ALU.mult).then_inc(q["beta_mask"], 1)
                for d in BOTH:
                    q, t = S[d], tile_of(s, d)
                    if s:
                        pool.wait_ge(q["v_product"], 2 * s)
                        pool.wait_ge(q["state"], 2 * s)
                    g.tensor_tensor(vb[d][:], G.vtok[:, t], cols(G.beta, t, d, P), ALU.mult)
                    g.tensor_tensor(ke[d][:], G.ktok[:, t], cols(G.el, t, d, P), ALU.mult).then_inc(q["scaled"], 1)
                if s < CT:
                    continue
                for d in BOTH:
                    q, t = S[d], tile_of(s, d)
                    pool.wait_ge(q["exp_rows"], s + 1)
                    if s > CT:
                        pool.wait_ge(q["o"], 2 * (s - CT))
                    x = (t - CT) * P
                    g.tensor_tensor(qe[d][:].rearrange("p h (c j) -> p h c j", c=2),
                                    G.qT[:, :, x:x + P].rearrange("p h (c j) -> p h c j", c=2),
                                    E[d][:].rearrange("p c h j -> p h c j"), ALU.mult).then_inc(q["qe"], 1)


def gdn_finish(core):
    nc, io, ps, hT = core.nc, core.io, core.ps, core.hT
    oT = core.branch[0]
    flat = ps[:].rearrange("p b n -> p (b n)")
    s_w, s_sq, s_ss, s_mean, s_rt, s_dve, s_dg, s_rows, s_mm, s_z, s_n, s_y = (core.sem("gdnf_" + n) for n in (
        "w", "squares", "sums", "means", "roots", "dve_steps", "diagonals", "rows", "projected", "silu", "normed", "done"))
    with ExitStack() as ctx:
        def sb(name, shape):
            return ctx.enter_context(nc.sbuf_tensor(name, shape, F32))
        w = sb("gdnf_w_z", [P, KD, W5])
        sq = sb("gdnf_sq", [P, GH, SEQ])
        zs = sb("gdnf_z", [P, GH, SEQ])
        st = sb("gdnf_stats", [P, 3, XT, GH])
        diag = sb("gdnf_diag", [P, 2, GH, P])
        block = ctx.enter_context(nc.Block())
        sums = ps[:, 7, 0:XT * GH].rearrange("p (t h) -> p t h", h=GH)

        @block.sync
        def _(sp):
            load_w_in(core, sp, w[:], Z0, W5, s_w)

        @block.tensor
        def _(pe):
            pe.wait_ge(s_sq, 1)
            for t in range(XT):
                for h in range(GH):
                    mm = nc.tensor.matmul(sums[:, t, h:h + 1], sq[:, h, t * P:(t + 1) * P], core.k("ones")[:, 0:1],
                                          start=True, stop=True)
            mm.then_inc(s_ss, 1)
            pe.wait_ge(s_w, 16)
            for n in range(2 * C5):
                c, half = divmod(n, 2)
                if n >= 3:
                    pe.wait_ge(s_z, n - 2)
                for k in range(KD):
                    mm = nc.tensor.matmul(ps[:, n % 3, :], w[:, k, c * P:(c + 1) * P],
                                          hT[:, k, CTX + 512 * half:CTX + 512 * half + 512], start=(k == 0), stop=(k == KD - 1))
                mm.then_inc(s_mm, 1)
                pe.wait_ge(s_dg, n + 1)
                if n >= 2:
                    pe.wait_ge(s_n, n - 1)
                nc.tensor.matmul(ps[:, 4 + n % 2, :], core.k("ones"), diag[:, n % 2].rearrange("p h t -> p (h t)"),
                                 start=True, stop=True).then_inc(s_rows, 1)

        @block.scalar
        def _(act):
            nc.scalar.activation(sq[:], oT[:], ACT.Square).then_inc(s_sq, 1)
            act.wait_ge(s_mean, 1)
            nc.scalar.activation(st[:, 1], st[:, 0], ACT.Sqrt).then_inc(s_rt, 1)
            for n in range(2 * C5):
                c, half = divmod(n, 2)
                act.wait_ge(s_mm, n + 1)
                nc.scalar.activation(zs[:, c, 512 * half:512 * half + 512], ps[:, n % 3, :], ACT.Silu).then_inc(s_z, 1)

        @block.vector
        def _(dve):
            v = nc.vector
            step = Serial(dve, s_dve)
            dve.wait_ge(s_ss, 1)
            v.tensor_scalar(st[:, 0], sums, 1.0 / P, EPS, ALU.mult, ALU.add).then_inc(s_mean, 1)
            dve.wait_ge(s_rt, 1)
            step(v.reciprocal(st[:, 2], st[:, 1]))
            for t in range(XT):
                if t >= 2:
                    dve.wait_ge(s_rows, t - 1)
                v.tensor_tensor(diag[:, t % 2], core.k("ident").unsqueeze(1).broadcast_to([P, GH, P]),
                                st[:, 2, t, :].unsqueeze(2).broadcast_to([P, GH, P]), ALU.mult).then_inc(s_dg, 1)
                dve.wait_ge(s_rows, t + 1)
                o = oT[:, :, t * P:(t + 1) * P]
                v.scalar_tensor_tensor(o, o, core.c("onorm"), ps[:, 4 + t % 2, :].rearrange("p (h t) -> p h t", h=GH),
                                       ALU.mult, ALU.mult).then_inc(s_n, 1)
            dve.wait_ge(s_n, XT)
            dve.wait_ge(s_z, 2 * C5)
            v.tensor_tensor(oT[:], oT[:], zs[:], ALU.mult).then_inc(s_y, 1)
            dve.wait_ge(s_y, 1)


def gdn(core):
    with ExitStack() as ctx:
        G = Gdn(core, ctx)
        core.phase(gdn_project, G)
        core.phase(gdn_gates, G)
        core.phase(gdn_scan, G)
    core.phase(gdn_finish)


def merge(core, mixT, w_out, w_router):
    nc, io, ps = core.nc, core.io, core.ps
    s_next = core.sem("mix_next_weights")
    s_w, s_gl = [core.sem(f"mix_w{i}") for i in range(2)], [core.sem(f"mix_logits{i}") for i in range(2)]
    s_mm, s_sg, s_dve, s_m, s_sum = (core.sem("mix_" + n) for n in ("multiplied", "sigmoids", "dve_steps", "banks_read", "summed"))
    with ExitStack() as ctx:
        def sb(name, shape):
            return ctx.enter_context(nc.sbuf_tensor(name, shape, F32))
        wb = sb("mix_w_branch", [P, 2, 3, C5, P])
        sg = sb("mix_sigmoids", [P, 2, 3, 512])
        block = ctx.enter_context(nc.Block())

        @block.sync
        def _(sp):
            def body(i, first):
                for b in range(2):
                    if not first:
                        sp.wait_ge(s_mm, 4 * (i - 1) + 2 * b + 2)
                    sp.dma_start(wb[:, b].rearrange("p i k n -> p (i k n)"), io["w_mix"][2 * i + b]).then_inc(s_w[b], 16)
                    for half in range(2):
                        if not (first and b == 0):
                            sp.wait_ge(s_sum, 4 * i + 2 * b + half - 1)
                        sp.dma_start(sg[:, half].rearrange("p g t -> p (g t)"),
                                     core.gate_dram[2 * i + b, half].rearrange("p g t -> p (g t)")).then_inc(s_gl[half], 16)
            body(0, True)
            sp.dma_start(w_out[:], io["w_out"].rearrange("(k p) n -> p k n", p=P)).then_inc(s_next, 16)
            sp.dma_start(w_router[:], io["w_router"].rearrange("(k p) n -> p k n", p=P)).then_inc(s_next, 16)
            with sp.Fori(1, KD // 2) as i:
                body(i, False)
            sp.wait_ge(s_next, 32)

        @block.tensor
        def _(pe):
            def body(i, first):
                for b in range(2):
                    pe.wait_ge(s_w[b], 16 * i + 16)
                    for half in range(2):
                        if not (first and b == 0):
                            pe.wait_ge(s_m, 4 * i + 2 * b + half - 1)
                        for g in range(3):
                            for k in range(C5):
                                mm = nc.tensor.matmul(ps[:, 3 * half + g, :], wb[:, b, g, k, :],
                                                      core.branch[g][:, k, 512 * half:512 * half + 512],
                                                      start=(k == 0), stop=(k == C5 - 1))
                        mm.then_inc(s_mm, 1)
            body(0, True)
            with pe.Fori(1, KD // 2) as i:
                body(i, False)

        @block.scalar
        def _(act):
            with act.Fori(0, KD // 2) as i:
                for j in range(4):
                    act.wait_ge(s_gl[j % 2], 32 * i + 16 * (j // 2) + 16)
                    nc.scalar.activation(sg[:, j % 2], sg[:, j % 2], ACT.Sigmoid).then_inc(s_sg, 1)

        @block.vector
        def _(dve):
            v = nc.vector
            with dve.Fori(0, KD // 2) as i:
                step = Serial(dve, s_dve, 4 * i)
                for b in range(2):
                    for half in range(2):
                        dve.wait_ge(s_sg, 4 * i + 2 * b + half + 1)
                        dve.wait_ge(s_mm, 4 * i + 2 * b + half + 1)
                        v.tensor_tensor(sg[:, half], sg[:, half], ps[:, 3 * half:3 * half + 3, :], ALU.mult).then_inc(s_m, 1)
                        dve.wait_ge(s_m, 4 * i + 2 * b + half + 1)
                        step(v.tensor_tensor(sg[:, half, 0, :], sg[:, half, 0, :], sg[:, half, 1, :], ALU.add))
                        v.tensor_tensor(mixT[:, bass.ds(2 * i + b, 1), 512 * half:512 * half + 512].rearrange("p a t -> p (a t)"),
                                        sg[:, half, 0, :], sg[:, half, 2, :], ALU.add).then_inc(s_sum, 1)


def mod_rows(core, rows):
    nc, ps = core.nc, core.ps
    s_sc, s_mm, s_cp = (core.sem("rows_" + n) for n in ("scaled", "spread", "kept"))
    with ExitStack() as ctx:
        block = ctx.enter_context(nc.Block())
        late = core.late_mods
        JOBS = [(r, q) for r in (0, 1, 2, 3) for q in range(2)]
        dest = (rows[:, 0, :], rows[:, 2, :], rows[:, 1, :], core.moe_gain)

        @block.vector
        def _(dve):
            nc.vector.scalar_tensor_tensor(late[64:65, :], late[64:65, :], 1.0, core.late[64:65, 0, :],
                                           ALU.add, ALU.mult).then_inc(s_sc, 1)

        @block.tensor
        def _(pe):
            for n, (r, q) in enumerate(JOBS):
                if r == 2 and q == 0:
                    pe.wait_ge(s_sc, 1)
                nc.tensor.matmul(ps[:, n, :], core.k("ones")[32 * r:32 * r + 1, :], late[32 * r:32 * r + 1, 512 * q:512 * q + 512],
                                 start=True, stop=True).then_inc(s_mm, 1)

        @block.scalar
        def _(act):
            for n, (r, q) in enumerate(JOBS):
                act.wait_ge(s_mm, n + 1)
                nc.scalar.copy(dest[r][:, 512 * q:512 * q + 512], ps[:, n, :]).then_inc(s_cp, 1)
            act.wait_ge(s_cp, len(JOBS))


def project_out(core, mixT, w, wr, rows, affT, h2_dram):
    nc, io, ps = core.nc, core.io, core.ps
    s_x, s_o, s_h = [core.sem(f"out_x_in{i}") for i in range(2)], \
        [core.sem(f"out_stored{i}") for i in range(2)], [core.sem(f"h2_stored{i}") for i in range(2)]
    names = ("projected", "x1", "squares", "means", "roots", "dve_steps", "h2", "turned", "turned_kept", "logits", "max",
             "exps", "probs", "probs_turned", "aff_kept", "bank_read")
    s_mm, s_x1, s_sq, s_ss, s_rt, s_dve, s_h2, s_tr, s_tk, s_lg, s_mx, s_ex, s_pr, s_pt, s_ak, s_br = (core.sem("out_" + n) for n in names)
    with ExitStack() as ctx:
        def sb(name, shape):
            return ctx.enter_context(nc.sbuf_tensor(name, shape, F32))
        x, x1, h2 = core.branch[0][:, 0:2, :], core.branch[0][:, 2:4, :], core.branch[1][:, 0:2, :]
        junk = core.branch[2][:, 0, :]
        h2T = sb("out_h2T", [P, 2, KD, P])
        st, pr = sb("out_stats", [P, 8]), sb("out_probs_sb", [P, 2, NE])
        block = ctx.enter_context(nc.Block())
        xv = io["tokens"].rearrange("(t p) d -> t p d", p=P)
        ov = io["out"].rearrange("(t p) d -> t p d", p=P)
        hv = h2_dram.rearrange("(t p) d -> t p d", p=P)

        @block.sync
        def _(sp):
            for t in range(XT + 1):
                if t < XT:
                    if t >= 2:
                        sp.wait_ge(s_x1, t - 1)
                    sp.dma_start(x[:, t % 2, :], xv[CT + t]).then_inc(s_x[t % 2], 16)
                if t:
                    sp.wait_ge(s_x1, t)
                    sp.dma_start(ov[t - 1], x1[:, (t - 1) % 2, :]).then_inc(s_o[(t - 1) % 2], 16)
                    sp.wait_ge(s_h2, t)
                    sp.dma_start(hv[t - 1], h2[:, (t - 1) % 2, :]).then_inc(s_h[(t - 1) % 2], 16)
            for b in range(2):
                sp.wait_ge(s_o[b], 16 * XT // 2)
                sp.wait_ge(s_h[b], 16 * XT // 2)

        @block.tensor
        def _(pe):
            def route(t):
                pe.wait_ge(s_h2, t + 1)
                if t:
                    pe.wait_ge(s_tk, t)
                for k in range(KD):
                    tr = nc.tensor.transpose(ps[:, 4 + k // 4, (k % 4) * P:(k % 4 + 1) * P],
                                             h2[:, t % 2, k * P:(k + 1) * P], core.k("ident"))
                tr.then_inc(s_tr, 1)
                if t:
                    turn_probs(t - 1)
                pe.wait_ge(s_tk, t + 1)
                if t:
                    pe.wait_ge(s_ex, t)
                for k in range(KD):
                    mm = nc.tensor.matmul(ps[:, 6, 0:NE], h2T[:, t % 2, k, :], wr[:, k, :], start=(k == 0), stop=(k == KD - 1))
                mm.then_inc(s_lg, 1)

            def turn_probs(t):
                pe.wait_ge(s_pr, t + 1)
                if t:
                    pe.wait_ge(s_ak, t)
                nc.tensor.transpose(ps[0:NE, 7, 0:P], pr[:, t % 2, :], core.k("ident")).then_inc(s_pt, 1)

            for t in range(XT):
                if t >= 2:
                    pe.wait_ge(s_x1, t - 1)
                for n in range(2):
                    for k in range(KD):
                        mm = nc.tensor.matmul(ps[:, 2 * (t % 2) + n, :], mixT[:, k, t * P:(t + 1) * P],
                                              w[:, k, 512 * n:512 * n + 512], start=(k == 0), stop=(k == KD - 1))
                mm.then_inc(s_mm, 1)
                if t:
                    route(t - 1)
            route(XT - 1)
            turn_probs(XT - 1)

        @block.scalar
        def _(act):
            def keep_turned(t):
                act.wait_ge(s_tr, t + 1)
                if t >= 2:
                    act.wait_ge(s_lg, t - 1)
                nc.scalar.copy(h2T[:, t % 2].rearrange("p k t -> p (k t)"),
                               ps[:, 4:6, :].rearrange("p b n -> p (b n)")).then_inc(s_tk, 1)

            def route(t):
                act.wait_ge(s_mx, t + 1)
                if t >= 2:
                    act.wait_ge(s_pt, t - 1)
                nc.scalar.activation(pr[:, t % 2, :], ps[:, 6, 0:NE], ACT.Exp, bias=st[:, 5:6], accum_out=st[:, 6:7]).then_inc(s_ex, 1)

            for t in range(XT):
                if t:
                    keep_turned(t - 1)
                act.wait_ge(s_x1, t + 1)
                if t:
                    act.wait_ge(s_ss, t)
                nc.scalar.activation(junk, x1[:, t % 2, :], ACT.Square, accum_out=st[:, 0:1]).then_inc(s_sq, 1)
                act.wait_ge(s_ss, t + 1)
                nc.scalar.activation(st[:, 2:3], st[:, 1:2], ACT.Sqrt).then_inc(s_rt, 1)
                if t:
                    route(t - 1)
            keep_turned(XT - 1)
            route(XT - 1)

        @block.vector
        def _(dve):
            v = nc.vector
            step = Serial(dve, s_dve)

            def softmax(t):
                dve.wait_ge(s_lg, t + 1)
                v.tensor_reduce(st[:, 5:6], ps[:, 6, 0:NE], AX, ALU.max, negate=True).then_inc(s_mx, 1)
                dve.wait_ge(s_ex, t + 1)
                step(v.reciprocal(st[:, 7:8], st[:, 6:7]))
                v.tensor_scalar(pr[:, t % 2, :], pr[:, t % 2, :], st[:, 7:8], None, ALU.mult).then_inc(s_pr, 1)
                dve.wait_ge(s_pt, t + 1)
                v.tensor_copy(affT[:, t * P:(t + 1) * P], ps[0:NE, 7, 0:P]).then_inc(s_ak, 1)

            for t in range(XT):
                b = t % 2
                dve.wait_ge(s_mm, t + 1)
                dve.wait_ge(s_x[b], 16 * (t // 2 + 1))
                if t >= 2:
                    dve.wait_ge(s_o[b], 16 * (t // 2))
                    dve.wait_ge(s_sq, t - 1)
                step(v.tensor_tensor(x1[:, b, :], ps[:, 2 * b:2 * b + 2, :].rearrange("p b n -> p (b n)"), rows[:, 0, :], ALU.mult))
                v.tensor_tensor(x1[:, b, :], x1[:, b, :], x[:, b, :], ALU.add).then_inc(s_x1, 1)
                dve.wait_ge(s_sq, t + 1)
                v.tensor_scalar(st[:, 1:2], st[:, 0:1], 1.0 / D, EPS, ALU.mult, ALU.add).then_inc(s_ss, 1)
                dve.wait_ge(s_rt, t + 1)
                step(v.reciprocal(st[:, 3:4], st[:, 2:3]))
                if t >= 2:
                    dve.wait_ge(s_h[b], 16 * (t // 2))
                    dve.wait_ge(s_tr, t - 1)
                step(v.scalar_tensor_tensor(h2[:, b, :], x1[:, b, :], st[:, 3:4], rows[:, 1, :], ALU.mult, ALU.mult))
                v.tensor_tensor(h2[:, b, :], h2[:, b, :], rows[:, 2, :], ALU.add).then_inc(s_h2, 1)
                if t:
                    softmax(t - 1)
            softmax(XT - 1)
            dve.wait_ge(s_ak, XT)


def experts(core, h2_dram):
    nc, io, ps = core.nc, core.io, core.ps
    PIECES_E, RING, SPLIT, FN = 12, 3, 3, EH // 512
    s_w = [core.sem(f"moe_w{i}") for i in range(RING)]
    s_hi, s_lo, s_piece = core.sem("moe_w_high"), core.sem("moe_w_low"), core.sem("moe_piece_used")
    s_xs, s_xt, s_xh, s_xl = (core.sem("moe_x_" + n) for n in ("gathered", "turned", "high", "low"))
    s_topk, s_sel, s_tr, s_end = (core.sem("topk_" + n) for n in ("steps", "chosen", "turned", "kept"))
    s_si, s_hid, s_ht, s_hh, s_hl, s_gc, s_y, s_add = (core.sem("moe_" + n) for n in (
        "silu", "hidden", "hidden_turned", "hidden_high", "hidden_low", "gate_copied", "y", "added"))
    with ExitStack() as ctx:
        def sb(name, shape, dt=F32):
            return ctx.enter_context(nc.sbuf_tensor(name, shape, dt))
        w = sb("moe_w", [P, RING, 4096])
        wh, wl = sb("moe_w_high_sb", [P, SPLIT, 4096], F32R), sb("moe_w_low_sb", [P, SPLIT, 4096], F32R)
        xs, xh, xl = sb("moe_x", [P, D]), sb("moe_xT_high", [P, KD, P], F32R), sb("moe_xT_low", [P, KD, P], F32R)
        si, hid = sb("moe_silu_sb", [P, 2, 512]), sb("moe_hidden_sb", [P, 2, 512])
        hh, hl = sb("moe_hiddenT_high", [P, FN, 4, P], F32R), sb("moe_hiddenT_low", [P, FN, 4, P], F32R)
        y, gcur = sb("moe_y_sb", [P, D]), sb("moe_gate", [P, 1])
        best, at, at_f = sb("topk_best", [NE, CAP]), sb("topk_at", [NE, CAP], U32), sb("topk_at_f", [NE, CAP])
        idx, gate = sb("expert_tokens", [P, NE], U32), sb("expert_gates", [P, NE])
        block = ctx.enter_context(nc.Block())
        pieces = io["w_experts"]
        turned = ps[:, 4:6, :].rearrange("p b n -> p (b n)")

        def every_expert(eng, body):
            body(0, True)
            with eng.Fori(1, NE) as e:
                body(e, False)

        @block.sync
        def _(sp):
            def body(e, first):
                for j in range(PIECES_E):
                    if not (first and j < RING):
                        sp.wait_ge(s_lo, PIECES_E * e + j - RING + 1)
                    sp.dma_start(w[:, j % RING, :], pieces[e, j]).then_inc(s_w[j % RING], 16)
            every_expert(sp, body)

        @block.gpsimd
        def _(pool):
            g = nc.gpsimd

            def gather(e):
                g.indirect_dma_start(xs[:], None, h2_dram,
                                     bass.IndirectOffsetOnAxis(ap=idx[:, e:e + 1], axis=0)).then_inc(s_xs, 16)

            for j in range(SPLIT):
                pool.wait_ge(s_hi, j + 1)
                g.tensor_tensor(wl[:, j, :], w[:, j % RING, :], wh[:, j, :].bitcast(F32), ALU.subtract).then_inc(s_lo, 1)
            pool.wait_ge(s_end, 1)
            gather(0)
            for e in range(NE):
                if e + 1 < NE:
                    pool.wait_ge(s_xt, e + 1)
                    gather(e + 1)
                pool.wait_ge(s_y, e + 1)
                if e:
                    pool.wait_ge(s_add, 16 * e)
                g.indirect_dma_start(io["out"], bass.IndirectOffsetOnAxis(ap=idx[:, e:e + 1], axis=0), y[:], None,
                                     compute_op=ALU.add).then_inc(s_add, 16)
            pool.wait_ge(s_add, 16 * NE)

        @block.tensor
        def _(pe):
            def product(out, lhs, rhs, ks, first, last):
                for n, k in enumerate(ks):
                    for m, (a, b) in enumerate(((0, 0), (0, 1), (1, 0))):
                        mm = nc.tensor.matmul(out, lhs(a, k), rhs(b, k), start=(first and n == 0 and m == 0),
                                              stop=(last and n == len(ks) - 1 and m == 2))
                return mm

            def turn_x(e):
                pe.wait_ge(s_xs, 16 * e + 16)
                for k in range(KD):
                    tr = nc.tensor.transpose(turned[:, k * P:(k + 1) * P], xs[:, k * P:(k + 1) * P], core.k("ident"))
                tr.then_inc(s_xt, 1)

            def body(e, first, last=False):
                def part(j, b, k, n):
                    return (wh, wl)[b][:, j % SPLIT, :].rearrange("p (k n) -> p k n", n=n)[:, k]

                def turn(n):
                    pe.wait_ge(s_hid, FN * e + n + 1)
                    if n >= 2:
                        pe.wait_ge(s_hl, FN * e + n - 1)
                    for f in range(4):
                        tr = nc.tensor.transpose(ps[:, 4 + n % 2, f * P:(f + 1) * P],
                                                 hid[:, n % 2, f * P:(f + 1) * P], core.k("ident"))
                    tr.then_inc(s_ht, 1)

                pe.wait_ge(s_xl, e + 1)
                for j in range(2 * FN):
                    n, u = divmod(j, 2)
                    if u == 0 and not (first and n < 2):
                        pe.wait_ge(s_hid, FN * e + n - 1)
                    pe.wait_ge(s_lo, PIECES_E * e + j + 1)
                    product(ps[:, 2 * (n % 2) + u, :], lambda a, k: (xh, xl)[a][:, k, :], lambda b, k: part(j, b, k, 512),
                            range(KD), True, True).then_inc(s_piece, 1)
                    if u and n:
                        turn(n - 1)
                for n in range(FN):
                    j = 2 * FN + n
                    pe.wait_ge(s_lo, PIECES_E * e + j + 1)
                    pe.wait_ge(s_hl, FN * e + n + 1)
                    if n == 0 and not first:
                        pe.wait_ge(s_y, e)
                    for half in range(2):
                        mm = product(ps[:, 6 + half, :], lambda a, f: (hh, hl)[a][:, n, f, :],
                                     lambda b, f: part(j, b, f, D)[:, 512 * half:512 * half + 512], range(4), n == 0, n == FN - 1)
                    mm.then_inc(s_piece, 1)
                    if n == 0:
                        turn(FN - 1)
                    if n == 1 and not last:
                        pe.wait_ge(s_hl, FN * e + FN)
                        turn_x(e + 1)

            pe.wait_ge(s_sel, 1)
            nc.tensor.transpose(ps[:, 0, 0:NE], at_f[:], core.k("ident")[0:NE, 0:NE])
            nc.tensor.transpose(ps[:, 0, 64:64 + NE], best[:], core.k("ident")[0:NE, 0:NE]).then_inc(s_tr, 1)
            turn_x(0)
            body(0, True)
            with pe.Fori(1, NE - 1) as e:
                body(e, False)
            body(NE - 1, False, True)

        @block.scalar
        def _(act):
            def x_high(e):
                act.wait_ge(s_xt, e + 1)
                nc.scalar.copy(xh[:].rearrange("p k t -> p (k t)"), turned).then_inc(s_xh, 1)

            def body(e, first, last=False):
                def keep(n):
                    act.wait_ge(s_ht, FN * e + n + 1)
                    nc.scalar.copy(hh[:, n].rearrange("p f t -> p (f t)"), ps[:, 4 + n % 2, :]).then_inc(s_hh, 1)

                for j in range(PIECES_E):
                    act.wait_ge(s_w[j % RING], 16 * (PIECES_E // RING * e + j // RING + 1))
                    if not (first and j < SPLIT):
                        act.wait_ge(s_piece, PIECES_E * e + j - SPLIT + 1)
                    nc.scalar.copy(wh[:, j % SPLIT, :], w[:, j % RING, :]).then_inc(s_hi, 1)
                    if first and j == 2:
                        x_high(0)
                    if j in (3, 5, 7, 9):
                        n = (j - 3) // 2
                        act.wait_ge(s_piece, PIECES_E * e + 2 * n + 2)
                        if not (first and n < 2):
                            act.wait_ge(s_hid, FN * e + n - 1)
                        nc.scalar.activation(si[:, n % 2, :], ps[:, 2 * (n % 2), :], ACT.Silu).then_inc(s_si, 1)
                    if j in (5, 7, 9):
                        keep((j - 5) // 2)
                    if j == 10:
                        keep(FN - 1)
                if not last:
                    x_high(e + 1)

            body(0, True)
            with act.Fori(1, NE - 1) as e:
                body(e, False)
            body(NE - 1, False, True)

        @block.vector
        def _(dve):
            v = nc.vector

            def x_low(e):
                dve.wait_ge(s_xh, e + 1)
                v.tensor_tensor(xl[:].rearrange("p k t -> p (k t)"), turned,
                                xh[:].rearrange("p k t -> p (k t)").bitcast(F32), ALU.subtract).then_inc(s_xl, 1)

            def result(e, first=False):
                v.tensor_copy(gcur[:], gate[:, e:e + 1] if isinstance(e, int) else gate[:, bass.ds(e, 1)]).then_inc(s_gc, 1)
                dve.wait_ge(s_gc, e + 1)
                dve.wait_ge(s_piece, PIECES_E * e + PIECES_E)
                if not first:
                    dve.wait_ge(s_add, 16 * e)
                v.scalar_tensor_tensor(y[:], ps[:, 6:8, :].rearrange("p b n -> p (b n)"), gcur[:],
                                       core.moe_gain[:], ALU.mult, ALU.mult).then_inc(s_y, 1)

            def body(e, first, second=False, last=False):
                def keep(n):
                    dve.wait_ge(s_hh, FN * e + n + 1)
                    v.tensor_tensor(hl[:, n].rearrange("p f t -> p (f t)"), ps[:, 4 + n % 2, :],
                                    hh[:, n].rearrange("p f t -> p (f t)").bitcast(F32), ALU.subtract).then_inc(s_hl, 1)

                if first:
                    dve.wait_ge(s_lo, SPLIT)
                for j in range(SPLIT if first else 0, PIECES_E):
                    dve.wait_ge(s_hi, PIECES_E * e + j + 1)
                    v.tensor_tensor(wl[:, j % SPLIT, :], w[:, j % RING, :], wh[:, j % SPLIT, :].bitcast(F32),
                                    ALU.subtract).then_inc(s_lo, 1)
                    if j == 1 and not first:
                        result(e - 1, second)
                    if j in (3, 5, 7, 9):
                        n = (j - 3) // 2
                        dve.wait_ge(s_si, FN * e + n + 1)
                        if not (first and n < 2):
                            dve.wait_ge(s_ht, FN * e + n - 1)
                        v.tensor_tensor(hid[:, n % 2, :], si[:, n % 2, :], ps[:, 2 * (n % 2) + 1, :], ALU.mult).then_inc(s_hid, 1)
                    if j in (5, 7, 9):
                        keep((j - 5) // 2)
                    if j == 10:
                        keep(FN - 1)
                if not last:
                    x_low(e + 1)

            def top_k():
                step = Serial(dve, s_topk)
                affT = core.affT
                for i in range(CAP // 8):
                    b8, a8 = best[:, 8 * i:8 * i + 8], at[:, 8 * i:8 * i + 8]
                    step(v.max(b8, affT))
                    step(v.max_index(a8, b8, affT))
                    step(v.match_replace(affT, b8, affT, -1.0))
                v.tensor_copy(at_f[:], at[:]).then_inc(s_sel, 1)
                dve.wait_ge(s_tr, 1)
                v.tensor_copy(idx[:], ps[:, 0, 0:NE])
                v.tensor_copy(gate[:], ps[:, 0, 64:64 + NE]).then_inc(s_end, 1)
                dve.wait_ge(s_end, 1)

            top_k()
            x_low(0)
            body(0, True)
            body(1, False, second=True)
            with dve.Fori(2, NE - 1) as e:
                body(e, False)
            body(NE - 1, False, last=True)
            result(NE - 1)


def tail(core, h2_dram):
    with ExitStack() as ctx:
        def sb(name, shape, dt=F32):
            return ctx.enter_context(core.nc.sbuf_tensor(name, shape, dt))
        mixT = sb("mixT", [P, KD, SEQ])
        w_out, w_router = sb("out_w_sb", [P, KD, D]), sb("router_w", [P, KD, NE])
        core.phase(merge, mixT, w_out, w_router)
        rows = sb("mod_rows_sb", [P, 3, D])
        core.phase(mod_rows, rows)
        core.phase(project_out, mixT, w_out, w_router, rows, core.affT, h2_dram)


def program(nc, io):
    h2_dram = nc.dram_tensor("h2_rows", [SEQ, D], F32, kind="Internal").ap()
    with ExitStack() as whole:
        core = Core(nc, io, whole)
        core.late = core.keep("gain_and_affinities", [P, 2, D])
        core.moe_gain, core.affT = core.late[:, 0, :], core.late[0:NE, 1, :]
        core.gate_dram = nc.dram_tensor("gate_logits", [KD, 2, P, 3, 512], F32, kind="Internal").ap()
        core.phase(adaln)
        with ExitStack() as mixers:
            core.ctx = mixers
            core.hT = core.keep("hT", [P, KD, TOK])
            core.phase(norm1)
            core.branch = [core.keep("branch_gdn", [P, C5, SEQ]), None, None]
            gdn(core)
            core.late_mods = core.keep("late_mods", [P, D])
            core.branch[2] = core.keep("branch_lru", [P, C5, SEQ])
            core.phase(lru)
            swa(core)
            tail(core, h2_dram)
        core.phase(experts, h2_dram)


def host_arrays(i):
    import numpy as np
    f = np.float32

    def by_chunk(v):
        v = np.asarray(v)
        v = v.reshape(-1, v.shape[-1] // P, P)
        return v.transpose(2, 0, 1).reshape(P, -1)

    g = {k: np.asarray(v) for k, v in i.items()}
    cc = np.stack([by_chunk(g["c"][0]), by_chunk(g["c_ctx"])], axis=2).reshape(P, -1)
    gconv = by_chunk(g["gdn_conv_w"][0]).reshape(P, 4, 12).transpose(0, 2, 1).reshape(P, -1)
    lconv = by_chunk(g["lru_conv_w"][0]).reshape(P, 4, 4).transpose(0, 2, 1).reshape(P, -1)
    col = dict(cc=cc, b_ada=by_chunk(g["b_ada"][0][:2 * D]), n1=by_chunk(g["norm1_g"][0]),
               gconv=gconv, lconv=lconv, lconvb=by_chunk(g["lru_conv_b"][0]), lgb=by_chunk(g["lru_gate_b"][0].reshape(4, W5)),
               lam=by_chunk(g["lru_lambda"][0]), onorm=g["gdn_onorm_g"][0].reshape(P, 1))
    col = np.concatenate([col[n].reshape(P, w) for n, w in PCOL.items()], axis=1)

    slots = [h + 4 * kv for h in range(4) for kv in range(2)]
    qkg = np.concatenate([np.tile(g["swa_qnorm_g"][0], SH), np.tile(g["swa_knorm_g"][0], SKV)])
    row = dict(alog=g["gdn_a_log"][0].reshape(-1), dtb=g["gdn_dt_bias"][0].reshape(-1), qkg=qkg,
               sink=g["swa_sink"][0][slots])
    row = np.concatenate([row[n] for n in PROW])
    row = np.ascontiguousarray(np.broadcast_to(row[None], (P, PROW_N)))

    a = np.arange(P)
    same = (a[:, None] // GC) == (a[None] // GC)
    lo = a[:, None] % GC
    j = np.arange(GC)[None]
    tri128 = np.concatenate([same & (a[:, None] <= a[None]), same & (a[:, None] >= a[None])], 1)
    md = np.concatenate([np.where(lo >= j, 0, BIG), np.where(lo <= j, 0, BIG)], 1)
    mdt = np.concatenate([np.where(lo <= j, 0, -BIG), np.where(lo >= j, 0, -BIG)], 1)
    strict = np.concatenate([lo > j, lo < j], 1)
    s = np.arange(3 * P)[None]
    band = np.abs(s - P - a[:, None]) <= P
    sm = []
    for kind in range(3):
        ok = band & ~((kind == 0) & (s < P)) & ~((kind == 2) & (s >= 2 * P))
        sm.append(np.concatenate([np.where(ok, 0, -BIG), np.zeros((P, CTX))], 1))
    t = np.arange(SEQ)
    inv = 10000.0 ** (-np.arange(0, 32, 2) / 32)
    ang = np.concatenate([(t // 64)[:, None] * inv, (t % 64)[:, None] * inv], 1)
    by_tile = lambda v: v.reshape(XT, P, 32).transpose(1, 0, 2).reshape(P, -1)
    con = dict(ident=np.eye(P), ones=np.ones((P, P)), ident64=lo == j, blk=same, tri128=tri128, md=md, mdt=mdt,
               strict=strict, smask=np.concatenate(sm, 1), cos=by_tile(np.cos(ang)), sin=by_tile(np.sin(ang)))
    swa_con = np.concatenate([np.asarray(con[n], f) for n in PSWA], axis=1)
    con = np.concatenate([np.asarray(con[n], f) for n in PCON], axis=1)

    gw = g["lru_gate_w"][0]
    lgw = np.zeros((P, 2, 2, C5, P), f)
    for b in range(8):
        o = 64 * (b % 2)
        lgw[o:o + 64, :, :, b // 2, o:o + 64] = gw[:, :, b].transpose(2, 0, 1, 3)
    w_in = g["w_in"][0]
    w_gates = w_in[:, G0:].reshape(KD, P, 3, KD, P).transpose(3, 2, 1, 0, 4).reshape(3 * KD, P, -1)
    wb = g["w_branch"][0].copy()
    wb[1] = wb[1].reshape(2, 4, HD, D).transpose(1, 0, 2, 3).reshape(W5, D)
    w_mix = wb.reshape(3, C5, P, KD, P).transpose(3, 2, 0, 1, 4).reshape(KD, P, -1)
    wg, wu, wd = g["w_exp_gate"][0], g["w_exp_up"][0], g["w_exp_down"][0]
    pieces = np.empty((NE, 12, P, 4096), f)
    for q in range(4):
        for u, a in enumerate((wg, wu)):
            pieces[:, 2 * q + u] = a[:, :, 512 * q:512 * q + 512].reshape(NE, KD, P, 512).transpose(0, 2, 1, 3).reshape(NE, P, -1)
        pieces[:, 8 + q] = wd[:, 512 * q:512 * q + 512].reshape(NE, 4, P, D).transpose(0, 2, 1, 3).reshape(NE, P, -1)
    return {
        "tokens": np.concatenate([g["ctx"][0], g["x"][0]], axis=0), "col": col, "row": row, "con": con, "swa_con": swa_con,
        "b_late": g["b_ada"][0][2 * D:].reshape(4, D), "n2_row": g["norm2_g"][0].reshape(1, D), "w_ada": g["w_ada"][0], "w_in": w_in, "lgw": lgw.reshape(P, -1), "w_gates": w_gates, "w_mix": w_mix,
        "w_out": g["w_out"][0], "w_router": g["w_router"][0], "w_experts": pieces,
    }


def kernel(**inputs):
    import numpy as np
    import concourse.bacc as bacc
    from concourse.bass_utils import run_bass_kernel_spmd as run

    nc = bacc.Bacc("TRN2", target_bir_lowering=False, num_devices=1)
    arrays = {n: np.ascontiguousarray(a) for n, a in host_arrays(inputs).items()}
    io = {n: nc.dram_tensor(n, a.shape, F32, kind="ExternalInput").ap() for n, a in arrays.items()}
    io["out"] = nc.dram_tensor("out", [SEQ, D], F32, kind="ExternalOutput").ap()
    program(nc, io)
    r = run(nc, [arrays], core_ids=[0])
    return np.asarray(r.results[0]["out"]).reshape(1, SEQ, D)
```
